# Optimizing a Trainium2 kernel written in Bass

```python
import jax, jax.numpy as jnp
from jax import lax
import numpy as np

D_MODEL = 1024
BATCH = 1
SEQ = 256
DEPTH = 2

CHUNK = 64
Q_BLOCK = 128
EPS = 1e-6
POOL_WIDTH = D_MODEL // 4
POOL_WINDOWS = (2, 4, 8, 16)
POOL_GROUPS = len(POOL_WINDOWS)
POOL_GROUP_DIM = POOL_WIDTH // POOL_GROUPS
FOX_HEAD_DIM = 64
FOX_WIDTH = D_MODEL - POOL_WIDTH
FOX_HEADS = FOX_WIDTH // FOX_HEAD_DIM
SB_WIDTH = D_MODEL // 2
SB_HEAD_DIM = 64
SB_HEADS = SB_WIDTH // SB_HEAD_DIM
MLSTM_WIDTH = D_MODEL - SB_WIDTH
MLSTM_HEADS = 4
MLSTM_HEAD_DIM = MLSTM_WIDTH // MLSTM_HEADS
CONV_WIDTH = 4
D_FF = 7 * D_MODEL // 2
N_EXPERTS = 8
TOP_K = 2
EXPERT_ROWS = 128
EVEN_IN = POOL_WIDTH + 3 * FOX_WIDTH + FOX_HEADS
ODD_IN = 3 * SB_WIDTH + 4 * MLSTM_WIDTH + 2 * MLSTM_HEADS

kernel_name = 'hybrid_pool_fox_stickbreak_mlstm_moe_trunk'

F32 = jnp.float32

def rms_norm(x, g):
    xf = x.astype(F32)
    y = xf * lax.rsqrt(jnp.mean(xf * xf, axis=-1, keepdims=True) + EPS)
    return (y * g.astype(F32)).astype(x.dtype)

def split_cols(t, widths):
    idx = [int(i) for i in np.cumsum(widths)[:-1]]
    return jnp.split(t, idx, axis=-1)

def split_heads(t, n_heads):
    b, s, w = t.shape
    return t.reshape(b, s, n_heads, w // n_heads).transpose(0, 2, 1, 3)

def merge_heads(t):
    b, h, s, d = t.shape
    return t.transpose(0, 2, 1, 3).reshape(b, s, h * d)

def trailing_mean(x, window):
    s = x.shape[1]
    cs = jnp.cumsum(x.astype(F32), axis=1)
    lagged = jnp.pad(cs, ((0, 0), (window, 0), (0, 0)))[:, :s]
    count = jnp.minimum(jnp.arange(1, s + 1), window).astype(F32)
    return (cs - lagged) / count[None, :, None]

def pool_mixer(a, pool_w, pool_scale):
    b, s, _ = a.shape
    groups = []
    for g, window in enumerate(POOL_WINDOWS):
        ag = a[..., g * POOL_GROUP_DIM:(g + 1) * POOL_GROUP_DIM]
        groups.append(trailing_mean(ag, window) - ag.astype(F32))
    pooled = jnp.stack(groups, axis=2).astype(a.dtype)
    mixed = jnp.einsum('bsgc,gcd->bsgd', pooled, pool_w).reshape(b, s, POOL_WIDTH)
    return mixed * pool_scale

def forgetting_attention(q, k, v, f_pre, b_forget):
    q, k, v = split_heads(q, FOX_HEADS), split_heads(k, FOX_HEADS), split_heads(v, FOX_HEADS)
    log_f = jax.nn.log_sigmoid(f_pre.astype(F32) + b_forget.astype(F32))
    cum = jnp.cumsum(log_f, axis=1).transpose(0, 2, 1)
    s = q.shape[2]
    scale = FOX_HEAD_DIM ** -0.5
    outs = []
    for q0 in range(0, s, Q_BLOCK):
        q1 = q0 + Q_BLOCK
        logits = jnp.einsum('bhqd,bhkd->bhqk', q[:, :, q0:q1], k[:, :, :q1]).astype(F32) * scale
        logits = logits + cum[:, :, q0:q1, None] - cum[:, :, None, :q1]
        causal = jnp.arange(q1)[None, :] <= jnp.arange(q0, q1)[:, None]
        probs = jax.nn.softmax(jnp.where(causal, logits, -jnp.inf), axis=-1)
        outs.append(jnp.einsum('bhqk,bhkd->bhqd', probs.astype(v.dtype), v[:, :, :q1]))
    return merge_heads(jnp.concatenate(outs, axis=2))

def stick_breaking_attention(q, k, v):
    q, k, v = split_heads(q, SB_HEADS), split_heads(k, SB_HEADS), split_heads(v, SB_HEADS)
    s = q.shape[2]
    scale = SB_HEAD_DIM ** -0.5
    outs = []
    for q0 in range(0, s, Q_BLOCK):
        q1 = q0 + Q_BLOCK
        z = jnp.einsum('bhqd,bhkd->bhqk', q[:, :, q0:q1], k[:, :, :q1]).astype(F32) * scale
        valid = jnp.arange(q1)[None, :] < jnp.arange(q0, q1)[:, None]
        log_keep = jnp.where(valid, jax.nn.log_sigmoid(-z), 0.0)
        later = lax.cumsum(log_keep, axis=3, reverse=True) - log_keep
        w = jnp.where(valid, jnp.exp(jax.nn.log_sigmoid(z) + later), 0.0)
        outs.append(jnp.einsum('bhqk,bhkd->bhqd', w.astype(v.dtype), v[:, :, :q1]))
    return merge_heads(jnp.concatenate(outs, axis=2))

def causal_depthwise_conv(x, w):
    c = x.shape[-1]
    return lax.conv_general_dilated(
        x, w.astype(x.dtype)[:, None, :], window_strides=(1,),
        padding=[(CONV_WIDTH - 1, 0)], dimension_numbers=('NWC', 'WIO', 'NWC'),
        feature_group_count=c)

def mlstm(q, k, v, i_pre, f_pre, head_norm_g):
    b, s, _ = q.shape
    nc = s // CHUNK

    def chunks(t):
        return t.astype(F32).reshape(b, nc, CHUNK, MLSTM_HEADS, -1).transpose(0, 3, 1, 2, 4)

    def gate_chunks(t):
        return t.astype(F32).reshape(b, nc, CHUNK, MLSTM_HEADS).transpose(0, 3, 1, 2)

    q = chunks(q)
    k = chunks(k) * MLSTM_HEAD_DIM ** -0.5
    v = chunks(v)
    log_i = gate_chunks(i_pre)
    log_f = jax.nn.log_sigmoid(gate_chunks(f_pre))
    bcum = jnp.cumsum(log_f, axis=-1)
    g = bcum[..., -1]

    a = g[..., None] - bcum + log_i
    m_loc = jnp.max(a, axis=-1)
    w_loc = jnp.exp(a - m_loc[..., None])
    c_loc = jnp.einsum('bhnl,bhnld,bhnle->bhnde', w_loc, v, k)
    n_loc = jnp.einsum('bhnl,bhnle->bhne', w_loc, k)

    def step(carry, inp):
        c_st, n_st, m_st = carry
        g_c, m_l, c_l, n_l = inp
        m_new = jnp.maximum(g_c + m_st, m_l)
        decay = jnp.exp(g_c + m_st - m_new)
        fresh = jnp.exp(m_l - m_new)
        c_new = decay[..., None, None] * c_st + fresh[..., None, None] * c_l
        n_new = decay[..., None] * n_st + fresh[..., None] * n_l
        return (c_new, n_new, m_new), (c_st, n_st, m_st)

    init = (jnp.zeros((b, MLSTM_HEADS, MLSTM_HEAD_DIM, MLSTM_HEAD_DIM), F32),
            jnp.zeros((b, MLSTM_HEADS, MLSTM_HEAD_DIM), F32),
            jnp.zeros((b, MLSTM_HEADS), F32))
    xs = (jnp.moveaxis(g, 2, 0), jnp.moveaxis(m_loc, 2, 0),
          jnp.moveaxis(c_loc, 2, 0), jnp.moveaxis(n_loc, 2, 0))
    _, (c_prev, n_prev, m_prev) = lax.scan(step, init, xs)
    c_prev = jnp.moveaxis(c_prev, 0, 2)
    n_prev = jnp.moveaxis(n_prev, 0, 2)
    m_prev = jnp.moveaxis(m_prev, 0, 2)

    inter = bcum + m_prev[..., None]
    log_d = bcum[..., :, None] - bcum[..., None, :] + log_i[..., None, :]
    tri = jnp.tril(jnp.ones((CHUNK, CHUNK), dtype=bool))
    log_d = jnp.where(tri, log_d, -jnp.inf)
    m_out = jnp.maximum(inter, jnp.max(log_d, axis=-1))
    d_mat = jnp.exp(log_d - m_out[..., None])
    inter_w = jnp.exp(inter - m_out)
    qk = jnp.einsum('bhnld,bhnsd->bhnls', q, k) * d_mat
    num = jnp.einsum('bhnls,bhnsd->bhnld', qk, v) \
        + inter_w[..., None] * jnp.einsum('bhnde,bhnle->bhnld', c_prev, q)
    den = jnp.sum(qk, axis=-1) + inter_w * jnp.einsum('bhne,bhnle->bhnl', n_prev, q)
    h = num / jnp.maximum(jnp.abs(den), jnp.exp(-m_out))[..., None]
    h = h.transpose(0, 2, 3, 1, 4).reshape(b, s, MLSTM_HEADS, MLSTM_HEAD_DIM)
    h = h * lax.rsqrt(jnp.mean(h * h, axis=-1, keepdims=True) + EPS) * head_norm_g.astype(F32)
    return h.reshape(b, s, MLSTM_WIDTH)

def even_mixer(h, w_in, b_forget, pool_w, pool_scale, w_out):
    proj = h @ w_in
    a_in, fq, fk, fv, f_pre = split_cols(
        proj, (POOL_WIDTH, FOX_WIDTH, FOX_WIDTH, FOX_WIDTH, FOX_HEADS))
    a_out = pool_mixer(a_in, pool_w, pool_scale)
    b_out = forgetting_attention(fq, fk, fv, f_pre, b_forget)
    return jnp.concatenate([a_out.astype(h.dtype), b_out.astype(h.dtype)], axis=-1) @ w_out

def odd_mixer(h, w_in, b_igate, b_fgate, conv_w, head_norm_g, w_out):
    proj = h @ w_in
    sq, sk, sv, ml_qk, ml_v, ml_o, ml_i, ml_f = split_cols(
        proj, (SB_WIDTH, SB_WIDTH, SB_WIDTH, 2 * MLSTM_WIDTH, MLSTM_WIDTH, MLSTM_WIDTH,
               MLSTM_HEADS, MLSTM_HEADS))
    c_out = stick_breaking_attention(sq, sk, sv)
    ml_qk = jax.nn.silu(causal_depthwise_conv(ml_qk, conv_w))
    ml_q, ml_k = ml_qk[..., :MLSTM_WIDTH], ml_qk[..., MLSTM_WIDTH:]
    d_out = mlstm(ml_q, ml_k, ml_v, ml_i + b_igate, ml_f + b_fgate, head_norm_g)
    d_out = d_out * jax.nn.sigmoid(ml_o.astype(F32))
    return jnp.concatenate([c_out.astype(h.dtype), d_out.astype(h.dtype)], axis=-1) @ w_out

def swiglu(h, w_gate, w_up, w_down):
    return (jax.nn.silu(h @ w_gate) * (h @ w_up)) @ w_down

def moe_swiglu(h, w_router, w_gate, w_up, w_down):
    b, s, d = h.shape
    n_tok = b * s
    xt = h.reshape(n_tok, d)
    logits = xt.astype(F32) @ w_router.astype(F32)
    top_logit, top_idx = lax.top_k(logits, TOP_K)
    gates = jax.nn.softmax(top_logit, axis=-1).reshape(-1)
    flat_e = top_idx.reshape(-1)
    flat_tok = jnp.arange(n_tok * TOP_K, dtype=jnp.int32) // TOP_K
    onehot = jax.nn.one_hot(flat_e, N_EXPERTS, dtype=jnp.int32)
    rank = jnp.sum((jnp.cumsum(onehot, axis=0) - onehot) * onehot, axis=-1)
    counts = jnp.sum(onehot, axis=0)
    padded = (counts + EXPERT_ROWS - 1) // EXPERT_ROWS * EXPERT_ROWS
    group_end = jnp.cumsum(padded)
    pos = group_end[flat_e] - padded[flat_e] + rank
    n_rows = -(-n_tok * TOP_K // EXPERT_ROWS) * EXPERT_ROWS + N_EXPERTS * EXPERT_ROWS
    n_blocks = n_rows // EXPERT_ROWS
    row_tok = jnp.zeros((n_rows,), jnp.int32).at[pos].set(flat_tok)
    block_expert = jnp.minimum(
        jnp.searchsorted(group_end, jnp.arange(n_blocks) * EXPERT_ROWS, side='right'),
        N_EXPERTS - 1)

    def expert_block(args):
        tok, e = args
        xb = xt[tok]
        return (jax.nn.silu(xb @ w_gate[e]) * (xb @ w_up[e])) @ w_down[e]

    y_rows = lax.map(expert_block, (row_tok.reshape(n_blocks, EXPERT_ROWS), block_expert))
    y_rows = y_rows.reshape(n_rows, d)
    contrib = y_rows[pos].astype(F32) * gates[:, None]
    y = jax.ops.segment_sum(contrib, flat_tok, num_segments=n_tok)
    return y.reshape(b, s, d).astype(h.dtype)

def setup_inputs(seed: int = 0) -> dict:
    key = jax.random.key(seed)
    ks = jax.random.split(key, 24)
    n_even = (DEPTH + 1) // 2
    n_odd = DEPTH // 2

    def dense(k, shape, fan_in):
        return jax.random.normal(k, shape, F32) * fan_in ** -0.5

    def gain(k, shape):
        return 1.0 + 0.1 * jax.random.normal(k, shape, F32)

    return {
        'x': jax.random.normal(ks[0], (BATCH, SEQ, D_MODEL), F32),
        'norm_mix_g': gain(ks[1], (DEPTH, D_MODEL)),
        'norm_ffn_g': gain(ks[2], (DEPTH, D_MODEL)),
        'norm_final_g': gain(ks[3], (D_MODEL,)),
        'ev_w_in': dense(ks[4], (n_even, D_MODEL, EVEN_IN), D_MODEL),
        'ev_b_forget': jax.random.uniform(ks[5], (n_even, FOX_HEADS), F32, 1.0, 6.0),
        'ev_pool_w': dense(ks[6], (n_even, POOL_GROUPS, POOL_GROUP_DIM, POOL_GROUP_DIM), POOL_GROUP_DIM),
        'ev_pool_scale': gain(ks[7], (n_even, POOL_WIDTH)),
        'ev_w_out': dense(ks[8], (n_even, D_MODEL, D_MODEL), D_MODEL),
        'ffn_w_gate': dense(ks[9], (n_even, D_MODEL, D_FF), D_MODEL),
        'ffn_w_up': dense(ks[10], (n_even, D_MODEL, D_FF), D_MODEL),
        'ffn_w_down': dense(ks[11], (n_even, D_FF, D_MODEL), D_FF),
        'od_w_in': dense(ks[12], (n_odd, D_MODEL, ODD_IN), D_MODEL),
        'od_b_igate': 0.1 * jax.random.normal(ks[13], (n_odd, MLSTM_HEADS), F32),
        'od_b_fgate': jax.random.uniform(ks[14], (n_odd, MLSTM_HEADS), F32, 3.0, 6.0),
        'od_conv_w': dense(ks[15], (n_odd, CONV_WIDTH, 2 * MLSTM_WIDTH), CONV_WIDTH),
        'od_head_norm_g': gain(ks[16], (n_odd, MLSTM_HEADS, MLSTM_HEAD_DIM)),
        'od_w_out': dense(ks[17], (n_odd, D_MODEL, D_MODEL), D_MODEL),
        'moe_w_router': dense(ks[18], (n_odd, D_MODEL, N_EXPERTS), D_MODEL),
        'moe_w_gate': dense(ks[19], (n_odd, N_EXPERTS, D_MODEL, D_FF), D_MODEL),
        'moe_w_up': dense(ks[20], (n_odd, N_EXPERTS, D_MODEL, D_FF), D_MODEL),
        'moe_w_down': dense(ks[21], (n_odd, N_EXPERTS, D_FF, D_MODEL), D_FF),
    }

def reference(x, norm_mix_g, norm_ffn_g, norm_final_g, ev_w_in, ev_b_forget, ev_pool_w,
              ev_pool_scale, ev_w_out, ffn_w_gate, ffn_w_up, ffn_w_down, od_w_in, od_b_igate,
              od_b_fgate, od_conv_w, od_head_norm_g, od_w_out, moe_w_router, moe_w_gate,
              moe_w_up, moe_w_down):
    for layer in range(DEPTH):
        h = rms_norm(x, norm_mix_g[layer])
        if layer % 2 == 0:
            e = layer // 2
            x = x + even_mixer(h, ev_w_in[e], ev_b_forget[e], ev_pool_w[e], ev_pool_scale[e],
                               ev_w_out[e])
            h = rms_norm(x, norm_ffn_g[layer])
            x = x + swiglu(h, ffn_w_gate[e], ffn_w_up[e], ffn_w_down[e])
        else:
            o = layer // 2
            x = x + odd_mixer(h, od_w_in[o], od_b_igate[o], od_b_fgate[o], od_conv_w[o],
                              od_head_norm_g[o], od_w_out[o])
            h = rms_norm(x, norm_ffn_g[layer])
            x = x + moe_swiglu(h, moe_w_router[o], moe_w_gate[o], moe_w_up[o], moe_w_down[o])
    return rms_norm(x, norm_final_g)


_drawn_inputs = setup_inputs


def setup_inputs(seed=0):
    import zlib

    import numpy as np

    out = dict(_drawn_inputs(seed))
    spreads = {}
    factors = {'od_b_igate': 200.0}
    for name, (base, spread) in spreads.items():
        noise = np.random.default_rng([zlib.crc32(name.encode()), seed]).standard_normal(out[name].shape)
        drawn = base * np.exp(spread * noise) if base else spread * noise
        out[name] = __import__('jax').numpy.asarray(drawn.astype(out[name].dtype))
    for name, factor in factors.items():
        out[name] = (out[name] * factor).astype(out[name].dtype)
    return out
```

```python
from contextlib import ExitStack

import numpy as np
import concourse.bass as bass
from concourse import mybir

F32 = mybir.dt.float32
I32 = mybir.dt.int32
ALU = mybir.AluOpType
ACT = mybir.ActivationFunctionType
AX = mybir.AxisListType.X

P = 128
SEQ = 256
T = SEQ // P
DM = 1024
DK = DM // P
EPS = 1e-6
POOL_WINDOWS = (2, 4, 8, 16)
POOL_W = DM // 4
HD = 64
FOX_H = (DM - POOL_W) // HD
SB_H = 8
ML_H = 4
TAPS = 4
D_FF = 7 * DM // 2
FC = 512
NCH = D_FF // FC
NE = 8
NOVER = (2 * SEQ) // (P + 1)
NITEM = NE + NOVER
RING = 7
SLOT = 8 * FC
EVEN_SLOTS = 5
ODD_SLOTS = 7
FFN_SLOTS = 3 * NCH
SLOT_WO0 = EVEN_SLOTS
SLOT_FFN = SLOT_WO0 + 2
SLOT_ODD = SLOT_FFN + FFN_SLOTS
SLOT_WO1 = SLOT_ODD + ODD_SLOTS
SLOT_MOE = SLOT_WO1 + 2
MASKED = -1e30
FIRST = 0

C_ID = 0
C_UINC = 128
C_ONES = 256
C_USTR = 384
C_LSTR = 512
C_CM = 640
C_IOTA = 896
C_TIE = 1024
C_EID = C_TIE + 64
C_SLOTNO = C_EID + 8
C_BAND = C_SLOTNO + 16
C_ALL = C_BAND + len(POOL_WINDOWS) * 3 * P

V_NORM = 0
V_CONV = 32
V_POOL = 64
V_HEAD = 66
V_ALL = 70


def constants():
    c = np.zeros((P, C_ALL), np.float32)
    i, o = np.meshgrid(np.arange(P), np.arange(P), indexing="ij")
    c[:, C_ID:C_ID + P] = i == o
    c[:, C_UINC:C_UINC + P] = i <= o
    c[:, C_ONES:C_ONES + P] = 1
    c[:, C_USTR:C_USTR + P] = i < o
    c[:, C_LSTR:C_LSTR + P] = i > o
    c[:, C_CM + P:C_CM + 2 * P] = np.where(o <= i, 0.0, MASKED)
    c[:, C_IOTA:C_IOTA + P] = o
    e, f = np.meshgrid(np.arange(NE), np.arange(NE), indexing="ij")
    c[:, C_TIE:C_TIE + NE * NE] = (f < e).reshape(-1)
    c[:, C_EID:C_EID + NE] = np.arange(NE)
    c[:, C_SLOTNO:C_SLOTNO + NOVER] = np.arange(NOVER)
    ti, to = np.meshgrid(np.arange(SEQ), np.arange(SEQ), indexing="ij")
    for g, w in enumerate(POOL_WINDOWS):
        band = np.where((ti <= to) & (ti > to - w), 1.0 / np.minimum(to + 1, w), 0.0) - (ti == to)
        for b, blk in enumerate((band[:P, :P], band[:P, P:], band[P:, P:])):
            at = C_BAND + (3 * g + b) * P
            c[:, at:at + P] = blk
    return c


class Banks:

    def __init__(self):
        self.count = [0] * 8
        self.uses = {}

    def fill(self, name, bank):
        self.count[bank] += 1
        self.uses[name] = (bank, self.count[bank])


EVEN_JOBS = [
    (0, "N", 0, "a", None), (0, "T", 256, "q", 0),
    (1, "T", 0, "q", 2), (1, "T", 256, "q", 4),
    (2, "T", 0, "k", 0), (2, "T", 256, "k", 2),
    (3, "T", 0, "k", 4), (3, "N", 256, "v0", None),
    (4, "N", 0, "v1", 0), (4, "N", 0, "v1", 1)]
ODD_JOBS = [
    (0, "T", 0, "sq", 0), (0, "T", 256, "sq", 2),
    (1, "T", 0, "sk", 0), (1, "T", 256, "sk", 2),
    (2, "N", 0, "sv", 0), (2, "N", 0, "sv", 1),
    (3, "T", 0, "mq", 0), (3, "T", 256, "mq", 2),
    (4, "T", 0, "mk", 0), (4, "T", 256, "mk", 2),
    (5, "N", 0, "mv", 0), (5, "N", 0, "mv", 1),
    (6, "N", 0, "mo", 0), (6, "N", 0, "mo", 1)]

FFN_ORDER = []
for _c in range(NCH):
    FFN_ORDER += [("g", _c), ("u", _c)] + ([("d", _c - 1)] if _c else [])
FFN_ORDER.append(("d", NCH - 1))
FFN_AT = {key: n for n, key in enumerate(FFN_ORDER)}


def plan_banks():
    banks = Banks()

    def norm(j):
        for i in range(4):
            banks.fill(("norm", j, i), i)

    banks.fill("vectors", 7)
    norm(0)
    banks.fill("fgate", 4)
    for n in range(len(EVEN_JOBS)):
        banks.fill(("even", n), (5, 6, 7, 4)[n % 4])
    banks.fill("fcum", 2)
    for g in range(2):
        banks.fill(("pool", g), 3)
        banks.fill(("poolmix", g), 3)
    for h in range(FOX_H + 2):
        if h < FOX_H:
            banks.fill(("fox_s", h), h % 2)
        if 1 <= h <= FOX_H:
            banks.fill(("fox_pt", h - 1), 2 + (h - 1) % 2)
        if h >= 2 and h % 2 == 1:
            banks.fill(("fox_o", (h - 2) // 2), 4 + (h - 2) // 2 % 2)
    for n in range(4):
        banks.fill(("wout", 0, n), n)
    norm(1)
    for c in range(NCH):
        for j in range(4):
            banks.fill(("gu", c, j), j)
    for n in range(4):
        banks.fill(("fdown", n), 4 + n)
    norm(2)
    banks.fill("mgate", 4)
    for n in range(len(ODD_JOBS)):
        banks.fill(("odd", n), (5, 6, 7, 4)[n % 4])
    banks.fill("mcum", 2)
    for h in range(ML_H):
        banks.fill(("mrow", h), 6 + h % 2)
    banks.fill("mr", 3)
    for h in range(SB_H + 2):
        if h < SB_H:
            banks.fill(("sb_z", h), h % 2)
        if 1 <= h <= SB_H:
            banks.fill(("sb_lat", h - 1), 2 + (h - 1) % 2)
        if h >= 2 and h % 2 == 1:
            banks.fill(("sb_o", (h - 2) // 2), 4 + (h - 2) // 2 % 2)
    for h in range(ML_H + 1):
        if h < ML_H:
            banks.fill(("ml_s", h), h % 2)
        if h:
            banks.fill(("ml_n", h - 1), 2 + (h - 1) % 2)
    for h in range(ML_H):
        banks.fill(("ml_t", h), 4 + h % 2)
    for n in range(4):
        banks.fill(("wout", 1, n), n)
    norm(3)
    banks.fill("router", 4)
    banks.fill("rank", 5)
    before = list(banks.count)
    for half in range(2):
        banks.fill(("gather", half), 2 * half)
    banks.fill("sgt", 7)
    for c in range(NCH + 1):
        if c < NCH:
            banks.fill(("mg", c), c % 2)
            banks.fill(("mu", c), 2 + c % 2)
        if c:
            banks.fill(("mt", c - 1), 6)
    for n in range(2):
        banks.fill(("my", n), 4 + n)
    for n in range(4):
        banks.fill(("mc", n), 6 + n % 2)
    per_item = [a - b for a, b in zip(banks.count, before)]
    return banks.uses, per_item


def build_trunk(nc, x_d, w, cst_d, out_d):
    uses, bank_fills_per_item = plan_banks()

    with ExitStack() as ctx:
        def sb(name, shape, dt=F32):
            return ctx.enter_context(nc.sbuf_tensor(name, shape, dt))

        def sem(name):
            return ctx.enter_context(nc.semaphore(name))

        bank = [ctx.enter_context(nc.psum_tensor(f"bank{b}", [P, 512], F32)) for b in range(8)]
        s_filled = [sem(f"filled{b}") for b in range(8)]
        s_drained = [sem(f"drained{b}") for b in range(8)]
        ring_full = [sem(f"ring_full{r}") for r in range(RING)]
        wo_half_used = sem("wo_half_used")
        ffn_down_used = sem("ffn_down_used")
        expert_down_used = sem("expert_down_used")

        def ps(use):
            return bank[uses[use][0]][:, :]

        def filled(use, item=0):
            b, n = uses[use]
            return s_filled[b], n + item * bank_fills_per_item[b]

        def drained(use, item=0):
            b, n = uses[use]
            return s_drained[b], n + item * bank_fills_per_item[b]

        def fill_sem(use):
            return s_filled[uses[use][0]]

        def drain_sem(use):
            return s_drained[uses[use][0]]

        def open_bank(pe, use, item=0):
            b, n = uses[use]
            if n > 1:
                pe.wait_ge(s_drained[b], n - 1 + item * bank_fills_per_item[b])

        ring = sb("ring", [P, RING, SLOT])
        x = sb("x", [P, T, DM])
        hn = sb("hn", [P, T, DM])
        ht = sb("ht", [P, DK, SEQ])
        mix_t = sb("mix_t", [P, DK, SEQ])
        cst = sb("cst", [P, C_BAND])
        g_final = sb("g_final", [P, DM])
        vec_rows = sb("vec_rows", [V_ALL, P])
        vec = sb("vec", [P, V_ALL])
        w_fgate = sb("w_fgate", [P, DK, FOX_H])
        w_mgate = sb("w_mgate", [P, DK, 2 * ML_H])
        w_router = sb("w_router", [P, DK, NE])
        b_fgate = sb("b_fgate", [P, FOX_H])
        b_mgate = sb("b_mgate", [P, 2 * ML_H])
        ssq = sb("ssq", [P, 5, T])
        inv_ms = sb("inv_ms", [P, 5, T])
        rstd = sb("rstd", [P, 5, T])
        route_i = sb("route_i", [1, 16], I32)
        s_cols = sb("s_cols", [P, 1024])
        arena = sb("arena", [P, 12400])

        taken = [0, 0]

        def view(region, at, *shape):
            size = int(np.prod(shape))
            v = region[:, at:at + size]
            if len(shape) == 2:
                return v.rearrange("p (a b) -> p a b", a=shape[0])
            if len(shape) == 3:
                return v.rearrange("p (a b c) -> p a b c", a=shape[0], b=shape[1])
            return v

        def layout(region, *parts):
            at, out = 0, []
            for shape in parts:
                out.append(view(region, at, *shape))
                at += int(np.prod(shape))
            taken[0] = max(taken[0], at)
            return out

        bands, pool_a, fq, fk, fv, fp, fpt, pooled, pool_w = layout(
            arena, (len(POOL_WINDOWS) * 3, P), (T, POOL_W), (6, SEQ), (6, SEQ), (T, FOX_H * HD), (3, 384), (4, 384),
            (2, SEQ), (2, P))
        f_silu, f_act = layout(arena, (2, SEQ), (2 * 4, SEQ))
        sq, sk, sv, mk_in, mqk, mv, sb_l, sb_sp, sb_w, ml_r, ml_f = layout(
            arena, (4, SEQ), (4, SEQ), (T, 512), (4, SEQ), (8, SEQ), (T * ML_H, 129), (2, 384), (3, 384), (4, 384),
            (ML_H, SEQ), (2, SEQ))
        assert taken[0] <= 12400
        mq_in = mix_t[:, 4:8, :]
        ml_e = sb_sp
        ml_w = sb_w
        ml_h = hn[:, :, 0:512]
        ml_o = hn[:, :, 512:1024]
        xg_t, sel, sel_g, sgt, m_silu, m_act, m_act_t, y_e = layout(
            arena, (DK, P), (T, P), (T, P), (T, P), (2, FC), (2, FC), (2 * 4, P), (2, 512))

        (fu, fe, flf, fnlf, fcum, fmax, fsum, finv, mu, me, ml_lf, m_rn_f, m_an, m_em, m_den, m_rden, m_ssq, m_inv,
         m_rstd) = layout(
            s_cols, (T, FOX_H), (T, FOX_H), (T, FOX_H), (T, FOX_H), (T, FOX_H), (FOX_H, T), (FOX_H, T), (FOX_H, T),
            (T, 2 * ML_H), (T, ML_H), (T, ML_H), (T, ML_H), (T, ML_H), (T, ML_H), (ML_H, T), (ML_H, T), (ML_H, T),
            (ML_H, T), (ML_H, T))
        (r_log, r_cmp, r_eq, r_rank, r_sel, r_max, r_e, r_sum, r_gate, r_pos, r_cnt, r_over, r_oc, r_tmp, pos_i,
         gate_i, r_eidf) = layout(
            s_cols, (T, NE), (T * NE, NE), (T * NE, NE), (T, NE), (T, NE), (T, 1), (T, NE), (T, 1), (T, NE),
            (T, NE), (T, NE), (NE,), (NE,), (4, NE), (NITEM, T), (NITEM, T), (16,))
        assert taken[0] <= 12400

        ident = cst[:, C_ID:C_ID + P]
        u_inc = cst[:, C_UINC:C_UINC + P]
        u_inc_ones = cst[:, C_UINC:C_UINC + 2 * P]
        ones = cst[:, C_ONES:C_ONES + P]
        u_str = cst[:, C_USTR:C_USTR + P]
        l_str = cst[:, C_LSTR:C_LSTR + P]

        x_loaded = sem("x_loaded")
        cst_loaded = sem("cst_loaded")
        vec_loaded = sem("vec_loaded")
        gate_w_loaded = sem("gate_w_loaded")
        pool_w_zero = sem("pool_w_zero")
        pool_w_loaded = sem("pool_w_loaded")
        late_loaded = sem("late_loaded")
        x_updated = sem("x_updated")
        ssq_ready = sem("ssq_ready")
        inv_ready = sem("inv_ready")
        rstd_ready = sem("rstd_ready")
        hn_ready = sem("hn_ready")
        dve_step = sem("dve_step")
        act_step = sem("act_step")
        fu_ready = sem("fu_ready")
        fln_ready = sem("fln_ready")
        flf_ready = sem("flf_ready")
        fmax_ready = sem("fmax_ready")
        fexp_ready = sem("fexp_ready")
        fprob_ready = sem("fprob_ready")
        fsilu_ready = sem("fsilu_ready")
        mu_ready = sem("mu_ready")
        mln_ready = sem("mln_ready")
        mlf_ready = sem("mlf_ready")
        mv_ones = sem("mv_ones")
        conv_ready = sem("conv_ready")
        conv_silu = sem("conv_silu")
        mr_ready = sem("mr_ready")
        mem_ready = sem("mem_ready")
        sbl_ready = sem("sbl_ready")
        sbsp_ready = sem("sbsp_ready")
        sbsp_masked = sem("sbsp_masked")
        sbw_exp = sem("sbw_exp")
        sbw_masked = sem("sbw_masked")
        me_in = sem("me_in")
        me_ready = sem("me_ready")
        mw_masked = sem("mw_masked")
        mh_sq = sem("mh_sq")
        mh_inv = sem("mh_inv")
        mh_rstd = sem("mh_rstd")
        md_ready = sem("md_ready")
        r_in = sem("r_in")
        r_exp = sem("r_exp")
        rsel_ready = sem("rsel_ready")
        route_ready = sem("route_ready")
        sel_ready = sem("sel_ready")
        experts_done = sem("experts_done")
        out_ready = sem("out_ready")
        out_done = sem("out_done")

        def slot8(n):
            return ring[:, n % RING, :].rearrange("p (k f) -> p k f", k=DK)

        def slot4(n):
            return ring[:, n % RING, :].rearrange("p (k f) -> p k f", k=4)

        def slot_landed(eng, n, item=0):
            eng.wait_ge(ring_full[n % RING], 16 * (n // RING + 1) + item * (16 * FFN_SLOTS // RING))

        def x_done(j):
            return 4 * j

        def released(n, item=0):
            if n < SLOT_WO0:
                return filled(("even", max(i for i, job in enumerate(EVEN_JOBS) if job[0] == n)))
            if SLOT_ODD <= n < SLOT_WO1:
                return filled(("odd", max(i for i, job in enumerate(ODD_JOBS) if job[0] == n - SLOT_ODD)))
            for layer, base in enumerate((SLOT_WO0, SLOT_WO1)):
                if n == base:
                    return wo_half_used, layer + 1
                if n == base + 1:
                    return filled(("wout", layer, 3))
            experts = n >= SLOT_MOE
            kind, c = FFN_ORDER[n - (SLOT_MOE if experts else SLOT_FFN)]
            if kind == "d":
                if c == NCH - 1:
                    return filled(("my", 1), item) if experts else filled(("fdown", 3))
                if experts:
                    return expert_down_used, (NCH - 1) * item + c + 1
                return ffn_down_used, c + 1
            if experts:
                return filled(("m" + kind, c), item)
            return filled(("gu", c, 3))

        class Steps:

            def __init__(self, eng, s):
                self.eng, self.s, self.n, self.item, self.per_item = eng, s, 0, 0, 0

            def mark(self, ins):
                self.n += 1
                ins.then_inc(self.s, 1)
                return self.n

            def wait(self, n):
                self.eng.wait_ge(self.s, n + self.item * self.per_item)

            def done(self, ins):
                self.wait(self.mark(ins))

        def job_target(job):
            _, _, _, what, idx = job

            def whole(b):
                return b[:, :]

            def pairs(b):
                return b[:, :].rearrange("p (c n) -> p c n", c=2)

            def heads(b):
                return b[:, :].rearrange("p (h d) -> p h d", h=ML_H)

            if what == "a":
                return pool_a, 1.0, pairs
            if what == "v0":
                return fv[:, :, 0:SEQ], 1.0, pairs
            if what == "v1":
                return fv[:, idx, SEQ:], 1.0, whole
            if what == "sv":
                return sv[:, idx, :], 1.0, whole
            if what == "mv":
                return mv[:, idx * ML_H:(idx + 1) * ML_H, 0:P], 1.0, heads
            dst = {"q": fq, "k": fk, "sq": sq, "sk": sk, "mq": mq_in, "mk": mk_in}[what]
            return dst[:, idx:idx + 2, :], (HD ** -0.5 if what in ("q", "sq") else 1.0), pairs

        ACT_ODD_JOBS = [n for n, job in enumerate(ODD_JOBS) if n % 2 or job[3] == "mo"]

        block = ctx.enter_context(nc.Block())

        @block.sync
        def _(sp):
            def into_ring(n, dst_of, src, item=FIRST):
                if n - RING >= SLOT_MOE or (n >= RING and item is FIRST):
                    sp.wait_ge(*released(n - RING, item))
                elif n >= RING:
                    sp.wait_ge(*released(n - RING + FFN_SLOTS, item - 1))
                sp.dma_start(dst_of(n), src).then_inc(ring_full[n % RING], 16)

            def ffn_slots(base, wg, wu, wd, item=FIRST):
                for j, (kind, c) in enumerate(FFN_ORDER):
                    if kind == "d":
                        src = wd[c * FC:(c + 1) * FC, :].rearrange("(k p) n -> p k n", p=P)
                        into_ring(base + j, slot4, src, item)
                    else:
                        src = (wg if kind == "g" else wu)[:, c * FC:(c + 1) * FC].rearrange("(k p) f -> p k f", p=P)
                        into_ring(base + j, slot8, src, item)

            def rows(wo, half):
                return wo[half * 512:(half + 1) * 512, :].rearrange("(k p) n -> p k n", p=P)

            w_in = w["ev_w_in"][0].rearrange("(k p) c -> p k c", p=P)
            for s in range(EVEN_SLOTS):
                into_ring(s, slot8, w_in[:, :, s * FC:(s + 1) * FC])
            for half in range(2):
                into_ring(SLOT_WO0 + half, slot4, rows(w["ev_w_out"][0], half))
            ffn_slots(SLOT_FFN, w["ffn_w_gate"][0], w["ffn_w_up"][0], w["ffn_w_down"][0])
            w_in = w["od_w_in"][0].rearrange("(k p) c -> p k c", p=P)
            for s in range(ODD_SLOTS):
                into_ring(SLOT_ODD + s, slot8, w_in[:, :, s * FC:(s + 1) * FC])
            for half in range(2):
                into_ring(SLOT_WO1 + half, slot4, rows(w["od_w_out"][0], half))

            def expert_slots(item, expert):
                def of(name):
                    return w[name][0][bass.ds(expert, 1)].rearrange("o r c -> (o r) c")
                ffn_slots(SLOT_MOE, of("moe_w_gate"), of("moe_w_up"), of("moe_w_down"), item)

            expert_slots(FIRST, 0)
            with sp.Fori(1, NE) as item:
                expert_slots(item, item)
            sp.wait_ge(route_ready, 1)
            n_items = sp.value_load(route_i[0:1, 0:1], min_val=NE, max_val=NITEM)
            for over in range(NOVER):
                expert = sp.value_load(route_i[0:1, 1 + over:2 + over], min_val=0, max_val=NE - 1)
                with sp.If(n_items > NE + over):
                    expert_slots(NE + over, expert)
            for t in range(T):
                sp.wait_ge(out_ready, t + 1)
                sp.dma_start(out_d[0, t * P:(t + 1) * P, :], hn[:, t, :]).then_inc(out_done, 16)
            sp.wait_ge(out_done, 16 * T)

        @block.tensor
        def _(pe):
            mm = nc.tensor.matmul

            def transposes_of_norm(j):
                for i in range(4):
                    open_bank(pe, ("norm", j, i))
                    for c in range(2):
                        for t in range(T):
                            if i == 0 and c == 0:
                                pe.wait_ge(hn_ready, T * j + t + 1)
                            last = nc.tensor.transpose(
                                ps(("norm", j, i))[:, (c * T + t) * P:(c * T + t + 1) * P],
                                hn[:, t, (2 * i + c) * P:(2 * i + c + 1) * P], ident)
                    last.then_inc(fill_sem(("norm", j, i)), 1)

            def ht_ready(j):
                for i in range(4):
                    pe.wait_ge(*drained(("norm", j, i)))

            def project(stage, jobs, base, slots):
                for n, (s, kind, col, what, idx) in enumerate(jobs):
                    if n == 0 or jobs[n - 1][0] != s:
                        slot_landed(pe, base + s)
                    wt = slot8(base + s)
                    use = (stage, n)
                    open_bank(pe, use)
                    if kind == "T":
                        for c in range(2):
                            for k in range(DK):
                                last = mm(ps(use)[:, c * SEQ:(c + 1) * SEQ],
                                          wt[:, k, col + c * P:col + (c + 1) * P], ht[:, k, :],
                                          start=k == 0, stop=k == DK - 1)
                    else:
                        width = 512 if idx is not None else 256
                        for g, t in enumerate(range(T) if idx is None else [idx]):
                            for k in range(DK):
                                last = mm(ps(use)[:, g * width:(g + 1) * width],
                                          ht[:, k, t * P:(t + 1) * P], wt[:, k, col:col + width],
                                          start=k == 0, stop=k == DK - 1)
                    last.then_inc(fill_sem(use), 1)

            def small_projection(use, wt, width):
                open_bank(pe, use)
                for t in range(T):
                    for k in range(DK):
                        last = mm(ps(use)[:, t * width:(t + 1) * width], ht[:, k, t * P:(t + 1) * P], wt[:, k, :],
                                  start=k == 0, stop=k == DK - 1)
                last.then_inc(fill_sem(use), 1)

            def prefix_sums(use, src, width):
                open_bank(pe, use)
                mm(ps(use)[:, 0:width], u_inc, src[:, 0, :], start=True, stop=True)
                mm(ps(use)[:, width:2 * width], ones, src[:, 0, :], start=True, stop=False)
                mm(ps(use)[:, width:2 * width], u_inc, src[:, 1, :], start=False,
                   stop=True).then_inc(fill_sem(use), 1)

            def output_projection(layer, base):
                for half in range(2):
                    slot_landed(pe, base + half)
                    for n in range(4):
                        t, nh = n // 2, n % 2
                        use = ("wout", layer, n)
                        if half == 0:
                            open_bank(pe, use)
                        for k in range(4):
                            last = mm(ps(use), mix_t[:, half * 4 + k, t * P:(t + 1) * P],
                                      slot4(base + half)[:, k, nh * 512:(nh + 1) * 512],
                                      start=half == 0 and k == 0, stop=half == 1 and k == 3)
                        if half == 1:
                            last.then_inc(fill_sem(use), 1)
                        elif n == 3:
                            last.then_inc(wo_half_used, 1)

            pe.wait_ge(cst_loaded, 16)
            pe.wait_ge(vec_loaded, 16 * 7)
            nc.tensor.transpose(ps("vectors")[:, 0:V_ALL], vec_rows[:, :], ident[0:V_ALL, 0:V_ALL]).then_inc(
                fill_sem("vectors"), 1)

            transposes_of_norm(0)
            ht_ready(0)
            pe.wait_ge(gate_w_loaded, 16 * 5)
            small_projection("fgate", w_fgate, FOX_H)
            project("even", EVEN_JOBS, 0, EVEN_SLOTS)
            for n in range(len(EVEN_JOBS) - 4, len(EVEN_JOBS)):
                pe.wait_ge(*drained(("even", n)))
            pe.wait_ge(flf_ready, 1)
            prefix_sums("fcum", flf, FOX_H)
            pe.wait_ge(*drained(("even", 0)))
            pe.wait_ge(pool_w_loaded, 16 * 5)
            for g2 in range(2):
                use = ("pool", g2)
                open_bank(pe, use)
                for g in range(2):
                    grp = 2 * g2 + g
                    o = ps(use)[g * HD:(g + 1) * HD, :]
                    cols = slice(grp * HD, (grp + 1) * HD)
                    mm(o[:, 0:P], pool_a[:, 0, cols], bands[:, 3 * grp, :], start=True, stop=True)
                    mm(o[:, P:2 * P], pool_a[:, 0, cols], bands[:, 3 * grp + 1, :], start=True, stop=False)
                    last = mm(o[:, P:2 * P], pool_a[:, 1, cols], bands[:, 3 * grp + 2, :], start=False, stop=True)
                last.then_inc(fill_sem(use), 1)
                pe.wait_ge(*drained(use))
                use = ("poolmix", g2)
                mm(ps(use)[:, 0:SEQ], pool_w[:, g2, :], pooled[:, g2, :], start=True, stop=True).then_inc(
                    fill_sem(use), 1)

            def values(use, h, v, p0, q01, q1):
                o = ps(use)[(h % 2) * HD:(h % 2 + 1) * HD, 0:SEQ]
                mm(o, v[:, 0, h * HD:(h + 1) * HD], q01, start=True, stop=False)
                return mm(o[:, P:SEQ], v[:, 1, h * HD:(h + 1) * HD], q1, start=False, stop=True)

            for h in range(FOX_H + 2):
                if h < FOX_H:
                    use = ("fox_s", h)
                    rows_h = slice((h % 2) * HD, (h % 2 + 1) * HD)
                    open_bank(pe, use)
                    lf0 = fnlf[:, 0, h:h + 1].to_broadcast([P, P])
                    lf1 = fnlf[:, 1, h:h + 1].to_broadcast([P, P])
                    mm(ps(use)[:, 0:P], fq[rows_h, h // 2, 0:P], fk[rows_h, h // 2, 0:P], start=True, stop=False)
                    mm(ps(use)[:, 0:P], lf0, u_inc, start=False, stop=True)
                    mm(ps(use)[:, P:384], fq[rows_h, h // 2, P:SEQ], fk[rows_h, h // 2, :], start=True, stop=False)
                    mm(ps(use)[:, P:384], lf0, u_inc_ones, start=False, stop=False)
                    mm(ps(use)[:, 2 * P:384], lf1, u_inc, start=False, stop=True).then_inc(fill_sem(use), 1)
                if 1 <= h <= FOX_H:
                    use = ("fox_pt", h - 1)
                    open_bank(pe, use)
                    pe.wait_ge(fprob_ready, h)
                    for b in range(3):
                        last = nc.tensor.transpose(ps(use)[:, b * P:(b + 1) * P],
                                                   fp[:, (h - 1) % 3, b * P:(b + 1) * P], ident)
                    last.then_inc(fill_sem(use), 1)
                if h >= 2:
                    g = h - 2
                    use = ("fox_o", g // 2)
                    if g % 2 == 0:
                        open_bank(pe, use)
                    pe.wait_ge(*drained(("fox_pt", g)))
                    last = values(use, g, fv, 0, fpt[:, g % 4, 0:SEQ], fpt[:, g % 4, SEQ:384])
                    if g % 2 == 1:
                        last.then_inc(fill_sem(use), 1)
            pe.wait_ge(*drained(("poolmix", 1)))
            for g in range(FOX_H // 2 - 2, FOX_H // 2):
                pe.wait_ge(*drained(("fox_o", g)))
            output_projection(0, SLOT_WO0)

            transposes_of_norm(1)
            ht_ready(1)

            def ffn_down(c):
                n = SLOT_FFN + FFN_AT[("d", c)]
                slot_landed(pe, n)
                for j in range(4):
                    pe.wait_ge(*drained(("gu", c, j)))
                    for q in range(4):
                        t, nh = q // 2, q % 2
                        if c == 0 and j == 0:
                            open_bank(pe, ("fdown", q))
                        last = mm(ps(("fdown", q)), f_act[:, (c % 2) * 4 + j, t * P:(t + 1) * P],
                                  slot4(n)[:, j, nh * 512:(nh + 1) * 512],
                                  start=c == 0 and j == 0, stop=c == NCH - 1 and j == 3)
                        if c == NCH - 1 and j == 3:
                            last.then_inc(fill_sem(("fdown", q)), 1)
                if c < NCH - 1:
                    last.then_inc(ffn_down_used, 1)

            for c in range(NCH):
                ng, nu = SLOT_FFN + FFN_AT[("g", c)], SLOT_FFN + FFN_AT[("u", c)]
                slot_landed(pe, ng)
                slot_landed(pe, nu)
                for j in range(4):
                    use = ("gu", c, j)
                    open_bank(pe, use)
                    for g, n in enumerate((ng, nu)):
                        for k in range(DK):
                            last = mm(ps(use)[:, g * SEQ:(g + 1) * SEQ], slot8(n)[:, k, j * P:(j + 1) * P],
                                      ht[:, k, :], start=k == 0, stop=k == DK - 1)
                    last.then_inc(fill_sem(use), 1)
                if c:
                    ffn_down(c - 1)
            ffn_down(NCH - 1)

            transposes_of_norm(2)
            ht_ready(2)
            small_projection("mgate", w_mgate, 2 * ML_H)
            project("odd", ODD_JOBS, SLOT_ODD, ODD_SLOTS)
            pe.wait_ge(mlf_ready, 1)
            prefix_sums("mcum", ml_lf, ML_H)
            for h in range(ML_H):
                use = ("mrow", h)
                open_bank(pe, use)
                lf = [ml_lf[:, t, h:h + 1].to_broadcast([P, P]) for t in range(T)]
                li = [mu[:, t, h:h + 1].to_broadcast([P, P]) for t in range(T)]
                mm(ps(use)[:, 0:SEQ], lf[0], u_inc_ones, start=True, stop=False)
                mm(ps(use)[:, P:SEQ], lf[1], u_inc, start=False, stop=True)
                for t in range(T):
                    last = mm(ps(use)[:, SEQ + t * P:SEQ + (t + 1) * P], li[t], ident, start=True, stop=True)
                last.then_inc(fill_sem(use), 1)

            def rows_to_columns():
                open_bank(pe, "mr")
                pe.wait_ge(mr_ready, ML_H)
                for t in range(T):
                    for h in range(ML_H):
                        last = mm(ps("mr")[:, t * ML_H + h:t * ML_H + h + 1], ml_r[0:1, h, t * P:(t + 1) * P],
                                  ones[0:1, 0:1], start=True, stop=True)
                last.then_inc(fill_sem("mr"), 1)

            for n in range(6):
                pe.wait_ge(*drained(("odd", n)))
            for h in range(SB_H + 2):
                if h < SB_H:
                    use = ("sb_z", h)
                    rows_h = slice((h % 2) * HD, (h % 2 + 1) * HD)
                    open_bank(pe, use)
                    mm(ps(use)[:, 0:SEQ], sk[rows_h, h // 2, 0:P], sq[rows_h, h // 2, :], start=True, stop=True)
                    mm(ps(use)[:, SEQ:384], sk[rows_h, h // 2, P:SEQ], sq[rows_h, h // 2, P:SEQ], start=True,
                       stop=True).then_inc(fill_sem(use), 1)
                if 1 <= h <= SB_H:
                    use = ("sb_lat", h - 1)
                    sp_h = sb_sp[:, (h - 1) % 3, :]
                    open_bank(pe, use)
                    pe.wait_ge(sbsp_masked, h)
                    mm(ps(use)[:, 0:SEQ], l_str, sp_h[:, 0:SEQ], start=True, stop=False)
                    mm(ps(use)[:, P:SEQ], ones, sp_h[:, SEQ:384], start=False, stop=True)
                    mm(ps(use)[:, SEQ:384], l_str, sp_h[:, SEQ:384], start=True, stop=True).then_inc(
                        fill_sem(use), 1)
                if h >= 2:
                    g = h - 2
                    use = ("sb_o", g // 2)
                    if g % 2 == 0:
                        open_bank(pe, use)
                    pe.wait_ge(sbw_masked, g + 1)
                    last = values(use, g, sv, 0, sb_w[:, g % 4, 0:SEQ], sb_w[:, g % 4, SEQ:384])
                    if g % 2 == 1:
                        last.then_inc(fill_sem(use), 1)
                if h == 1:
                    rows_to_columns()

            pe.wait_ge(conv_silu, 2)
            for n in range(10, 12):
                pe.wait_ge(*drained(("odd", n)))
            pe.wait_ge(mv_ones, 1)
            for h in range(ML_H + 1):
                if h < ML_H:
                    use = ("ml_s", h)
                    open_bank(pe, use)
                    mm(ps(use)[:, 0:SEQ], mqk[:, 4 + h, 0:P], mqk[:, h, :], start=True, stop=True)
                    mm(ps(use)[:, SEQ:384], mqk[:, 4 + h, P:SEQ], mqk[:, h, P:SEQ], start=True, stop=True).then_inc(
                        fill_sem(use), 1)
                if h:
                    g = h - 1
                    use = ("ml_n", g)
                    open_bank(pe, use)
                    pe.wait_ge(mw_masked, g + 1)
                    o = ps(use)[:, 0:2 * 129].rearrange("p (t d) -> p t d", t=T)
                    wt = ml_w[:, g % 4, :]
                    mm(o[:, 0, :], wt[:, 0:P], mv[:, g, :], start=True, stop=True)
                    mm(o[:, 1, :], wt[:, P:SEQ], mv[:, g, :], start=True, stop=False)
                    mm(o[:, 1, :], wt[:, SEQ:384], mv[:, ML_H + g, :], start=False, stop=True).then_inc(
                        fill_sem(use), 1)
            for h in range(ML_H):
                use = ("ml_t", h)
                open_bank(pe, use)
                for t in range(T):
                    pe.wait_ge(md_ready, t + 1)
                    last = nc.tensor.transpose(ps(use)[:, t * P:(t + 1) * P], ml_h[:, t, h * P:(h + 1) * P], ident)
                last.then_inc(fill_sem(use), 1)
            for g in range(SB_H // 2 - 2, SB_H // 2):
                pe.wait_ge(*drained(("sb_o", g)))
            for h in range(ML_H - 2, ML_H):
                pe.wait_ge(*drained(("ml_t", h)))
            output_projection(1, SLOT_WO1)

            transposes_of_norm(3)
            ht_ready(3)
            pe.wait_ge(late_loaded, 32)
            small_projection("router", w_router, NE)
            pe.wait_ge(rsel_ready, 1)
            open_bank(pe, "rank")
            rk = ps("rank")
            mm(rk[:, 0:NE], u_inc, r_sel[:, 0, :], start=True, stop=True)
            mm(rk[:, NE:2 * NE], ones, r_sel[:, 0, :], start=True, stop=False)
            mm(rk[:, NE:2 * NE], u_inc, r_sel[:, 1, :], start=False, stop=True)
            mm(rk[:, 2 * NE:3 * NE], ones, r_sel[:, 0, :], start=True, stop=False)
            mm(rk[:, 2 * NE:3 * NE], ones, r_sel[:, 1, :], start=False, stop=True).then_inc(fill_sem("rank"), 1)

            def expert_down(c, item):
                n = SLOT_MOE + FFN_AT[("d", c)]
                use = ("mt", c)
                open_bank(pe, use, item)
                pe.wait_ge(*drained(("mu", c), item))
                for j in range(4):
                    last = nc.tensor.transpose(ps(use)[:, j * P:(j + 1) * P], m_act[:, c % 2, j * P:(j + 1) * P],
                                               ident)
                last.then_inc(fill_sem(use), 1)
                slot_landed(pe, n, item)
                pe.wait_ge(*drained(use, item))
                for nh in range(2):
                    if c == 0:
                        open_bank(pe, ("my", nh), item)
                    for j in range(4):
                        last = mm(ps(("my", nh)), m_act_t[:, (c % 2) * 4 + j, :],
                                  slot4(n)[:, j, nh * 512:(nh + 1) * 512],
                                  start=c == 0 and j == 0, stop=c == NCH - 1 and j == 3)
                    if c == NCH - 1:
                        last.then_inc(fill_sem(("my", nh)), 1)
                if c < NCH - 1:
                    last.then_inc(expert_down_used, 1)

            def expert_item(item):
                pe.wait_ge(sel_ready, item + 1)
                for half in range(2):
                    use = ("gather", half)
                    open_bank(pe, use, item)
                    for k in range(4):
                        for t in range(T):
                            last = mm(ps(use)[:, k * P:(k + 1) * P],
                                      hn[:, t, (half * 4 + k) * P:(half * 4 + k + 1) * P], sel[:, t, :],
                                      start=t == 0, stop=t == T - 1)
                    last.then_inc(fill_sem(use), 1)
                open_bank(pe, "sgt", item)
                for t in range(T):
                    last = nc.tensor.transpose(ps("sgt")[:, t * P:(t + 1) * P], sel_g[:, t, :], ident)
                last.then_inc(fill_sem("sgt"), 1)
                for half in range(2):
                    pe.wait_ge(*drained(("gather", half), item))
                for c in range(NCH):
                    for key, use in ((("g", c), ("mg", c)), (("u", c), ("mu", c))):
                        n = SLOT_MOE + FFN_AT[key]
                        slot_landed(pe, n, item)
                        open_bank(pe, use, item)
                        for k in range(DK):
                            last = mm(ps(use), xg_t[:, k, :], slot8(n)[:, k, :], start=k == 0, stop=k == DK - 1)
                        last.then_inc(fill_sem(use), 1)
                    if c:
                        expert_down(c - 1, item)
                expert_down(NCH - 1, item)
                for n in range(4):
                    t, nh = n // 2, n % 2
                    use = ("mc", n)
                    open_bank(pe, use, item)
                    pe.wait_ge(*drained(("my", nh), item))
                    mm(ps(use), sgt[:, t, :], y_e[:, nh, :], start=True, stop=True).then_inc(fill_sem(use), 1)

            with pe.Fori(0, NE) as item:
                expert_item(item)
            pe.wait_ge(route_ready, 1)
            n_items = pe.value_load(route_i[0:1, 0:1], min_val=NE, max_val=NITEM)
            with pe.Fori(NE, NITEM) as item:
                with pe.If(n_items > item):
                    expert_item(item)

        @block.scalar
        def _(act):
            fn = nc.scalar.activation
            steps = Steps(act, act_step)

            for t in range(T):
                act.dma_start(x[:, t, :], x_d[0, t * P:(t + 1) * P, :]).then_inc(x_loaded, 16)
            act.dma_start(cst[:, :], cst_d[:, 0:C_BAND]).then_inc(cst_loaded, 16)

            def as_rows(v):
                return v.rearrange("(k p) -> k p", p=P)

            for row, src in ((0, as_rows(w["norm_mix_g"][0])), (8, as_rows(w["norm_ffn_g"][0])),
                             (16, as_rows(w["norm_mix_g"][1])), (24, as_rows(w["norm_ffn_g"][1])),
                             (V_CONV, w["od_conv_w"][0].rearrange("t (k p) -> (t k) p", p=P)),
                             (V_POOL, as_rows(w["ev_pool_scale"][0])), (V_HEAD, w["od_head_norm_g"][0])):
                act.dma_start(vec_rows[row:row + src.shape[0], :], src).then_inc(vec_loaded, 16)
            gate_cols = slice(EVEN_SLOTS * FC, EVEN_SLOTS * FC + FOX_H)
            act.dma_start(w_fgate[:, :, :], w["ev_w_in"][0].rearrange("(k p) c -> p k c", p=P)[:, :, gate_cols]
                          ).then_inc(gate_w_loaded, 16)
            gate_cols = slice(ODD_SLOTS * FC, ODD_SLOTS * FC + 2 * ML_H)
            act.dma_start(w_mgate[:, :, :], w["od_w_in"][0].rearrange("(k p) c -> p k c", p=P)[:, :, gate_cols]
                          ).then_inc(gate_w_loaded, 16)
            act.dma_start(b_fgate[:, :], w["ev_b_forget"][0].partition_broadcast(P)).then_inc(gate_w_loaded, 16)
            act.dma_start(b_mgate[:, 0:ML_H], w["od_b_igate"][0].partition_broadcast(P)).then_inc(gate_w_loaded, 16)
            act.dma_start(b_mgate[:, ML_H:], w["od_b_fgate"][0].partition_broadcast(P)).then_inc(gate_w_loaded, 16)
            act.dma_start(bands, cst_d[:, C_BAND:C_ALL].rearrange("p (b c) -> p b c", c=P)
                          ).then_inc(pool_w_loaded, 16)
            act.wait_ge(pool_w_zero, 1)
            for g in range(4):
                half = slice((g % 2) * HD, (g % 2 + 1) * HD)
                act.dma_start(pool_w[half, g // 2, half], w["ev_pool_w"][0, g]).then_inc(pool_w_loaded, 16)
            act.dma_start(g_final[:, :], w["norm_final_g"].partition_broadcast(P)).then_inc(late_loaded, 16)
            act.dma_start(w_router[:, :, :], w["moe_w_router"][0].rearrange("(k p) e -> p k e", p=P)
                          ).then_inc(late_loaded, 16)

            def squares(j):
                for t in range(T):
                    fn(hn[:, t, :], x[:, t, :], ACT.Square, accum_out=ssq[:, j, t:t + 1]).then_inc(ssq_ready, 1)
                act.wait_ge(inv_ready, j + 1)
                fn(rstd[:, j, :], inv_ms[:, j, :], ACT.Sqrt).then_inc(rstd_ready, 1)

            def norm_banks(j):
                for i in (1, 3):
                    act.wait_ge(*filled(("norm", j, i)))
                    for c in range(2):
                        k = 2 * i + c
                        last = fn(ht[:, k, :], ps(("norm", j, i))[:, c * SEQ:(c + 1) * SEQ], ACT.Copy,
                                  scale=vec[:, V_NORM + 8 * j + k:V_NORM + 8 * j + k + 1])
                    last.then_inc(drain_sem(("norm", j, i)), 1)

            def log_of_1_plus_exp(v, ready, n, out_sem):
                act.wait_ge(ready, n)
                steps.done(fn(v, v, ACT.Exp))
                fn(v, v, ACT.Ln, bias=1.0).then_inc(out_sem, 1)

            act.wait_ge(x_loaded, 32)
            squares(0)
            act.wait_ge(*drained("vectors"))
            norm_banks(0)
            log_of_1_plus_exp(fe, fu_ready, 1, fln_ready)
            for n in range(1, len(EVEN_JOBS), 2):
                act.wait_ge(*filled(("even", n)))
                dst, scale, shape = job_target(EVEN_JOBS[n])
                fn(dst, shape(ps(("even", n))), ACT.Copy, scale=scale).then_inc(drain_sem(("even", n)), 1)
            for h in range(FOX_H + 2):
                if h < FOX_H:
                    act.wait_ge(fmax_ready, 2 * h + 2)
                    fn(fp[:, h % 3, 0:P], fp[:, h % 3, 0:P], ACT.Exp, bias=fmax[:, h, 0:1],
                       accum_out=fsum[:, h, 0:1])
                    fn(fp[:, h % 3, P:384], fp[:, h % 3, P:384], ACT.Exp, bias=fmax[:, h, 1:2],
                       accum_out=fsum[:, h, 1:2]).then_inc(fexp_ready, 1)
                if 1 <= h <= FOX_H:
                    use = ("fox_pt", h - 1)
                    act.wait_ge(*filled(use))
                    fn(fpt[:, (h - 1) % 4, :], ps(use)[:, 0:384], ACT.Copy).then_inc(drain_sem(use), 1)
                if h >= 2 and h % 2 == 1:
                    use = ("fox_o", (h - 2) // 2)
                    act.wait_ge(*filled(use))
                    fn(mix_t[:, 2 + (h - 2) // 2, :], ps(use)[:, 0:SEQ], ACT.Copy).then_inc(drain_sem(use), 1)

            for n in range(4):
                act.wait_ge(*drained(("wout", 0, n)))
            squares(1)
            norm_banks(1)
            chunks = [(c, j) for c in range(NCH) for j in range(4)]
            for n, (c, j) in enumerate(chunks):
                act.wait_ge(*filled(("gu", c, j)))
                if n >= 2:
                    act.wait_ge(*drained(("gu",) + chunks[n - 2]))
                fn(f_silu[:, n % 2, :], ps(("gu", c, j))[:, 0:SEQ], ACT.Silu).then_inc(fsilu_ready, 1)

            for n in range(4):
                act.wait_ge(*drained(("fdown", n)))
            squares(2)
            norm_banks(2)
            log_of_1_plus_exp(me, mu_ready, 1, mln_ready)
            for n in ACT_ODD_JOBS:
                act.wait_ge(*filled(("odd", n)))
                if ODD_JOBS[n][3] == "mo":
                    fn(ml_o[:, ODD_JOBS[n][4], :], ps(("odd", n)), ACT.Sigmoid).then_inc(
                        drain_sem(("odd", n)), 1)
                else:
                    dst, scale, shape = job_target(ODD_JOBS[n])
                    fn(dst, shape(ps(("odd", n))), ACT.Copy, scale=scale).then_inc(drain_sem(("odd", n)), 1)
            for h in range(SB_H + 2):
                if h < SB_H:
                    use = ("sb_z", h)
                    lb = sb_l[:, h % 2, :]
                    act.wait_ge(*filled(use))
                    if h >= 2:
                        act.wait_ge(*drained(("sb_z", h - 2)))
                    steps.done(fn(lb, ps(use)[:, 0:384], ACT.Abs))
                    steps.done(fn(lb, lb, ACT.Exp, scale=-1.0))
                    fn(lb, lb, ACT.Ln, bias=1.0).then_inc(sbl_ready, 1)
                if 1 <= h <= SB_H:
                    act.wait_ge(*drained(("sb_lat", h - 1)))
                    fn(sb_w[:, (h - 1) % 4, :], sb_w[:, (h - 1) % 4, :], ACT.Exp).then_inc(sbw_exp, 1)
                if h >= 2 and h % 2 == 1:
                    use = ("sb_o", (h - 2) // 2)
                    act.wait_ge(*filled(use))
                    fn(mix_t[:, (h - 2) // 2, :], ps(use)[:, 0:SEQ], ACT.Copy).then_inc(drain_sem(use), 1)
            act.wait_ge(*drained("mr"))
            fn(m_em, m_em, ACT.Exp).then_inc(mem_ready, 1)
            act.wait_ge(conv_ready, 8)
            for half in range(2):
                v = mqk[:, 4 * half:4 * half + 4, :]
                fn(v, v, ACT.Silu).then_inc(conv_silu, 1)
            for h in range(ML_H + 1):
                if h < ML_H:
                    act.wait_ge(me_in, h + 1)
                    fn(ml_e[:, h % 3, :], ml_e[:, h % 3, :], ACT.Exp).then_inc(me_ready, 1)
                if h:
                    g = h - 1
                    act.wait_ge(*drained(("ml_n", g)))
                    for t in range(T):
                        fn(sb_l[:, t, 0:P], ml_h[:, t, g * P:(g + 1) * P], ACT.Square,
                           accum_out=m_ssq[:, g, t:t + 1]).then_inc(mh_sq, 1)
                        act.wait_ge(mh_sq, 2 * g + t + 1)
            act.wait_ge(mh_inv, 1)
            fn(m_rstd, m_inv, ACT.Sqrt).then_inc(mh_rstd, 1)
            for h in range(ML_H):
                use = ("ml_t", h)
                act.wait_ge(*filled(use))
                fn(mix_t[:, 4 + h, :], ps(use)[:, 0:SEQ], ACT.Copy,
                   scale=vec[:, V_HEAD + h:V_HEAD + h + 1]).then_inc(drain_sem(use), 1)

            for n in range(4):
                act.wait_ge(*drained(("wout", 1, n)))
            squares(3)
            norm_banks(3)
            act.wait_ge(r_in, 1)
            fn(r_e, r_e, ACT.Exp).then_inc(r_exp, 1)

            def expert_item(item):
                use = ("gather", 1)
                act.wait_ge(*filled(use, item))
                for k in range(4, 8):
                    last = fn(xg_t[:, k, :], ps(use)[:, (k - 4) * P:(k - 3) * P], ACT.Copy,
                              scale=vec[:, V_NORM + 24 + k:V_NORM + 25 + k])
                last.then_inc(drain_sem(use), 1)
                act.wait_ge(*filled("sgt", item))
                fn(sgt, ps("sgt")[:, 0:SEQ].rearrange("p (t c) -> p t c", t=T), ACT.Copy).then_inc(
                    drain_sem("sgt"), 1)
                for c in range(NCH + 1):
                    if c < NCH:
                        act.wait_ge(*filled(("mg", c), item))
                        b, n = uses[("mu", c)]
                        act.wait_ge(s_drained[b], n - 1 + item * bank_fills_per_item[b])
                        fn(m_silu[:, c % 2, :], ps(("mg", c)), ACT.Silu).then_inc(drain_sem(("mg", c)), 1)
                    if c:
                        use = ("mt", c - 1)
                        act.wait_ge(*filled(use, item))
                        at = ((c - 1) % 2) * 4
                        fn(m_act_t[:, at:at + 4, :], ps(use).rearrange("p (j c) -> p j c", j=4),
                           ACT.Copy).then_inc(drain_sem(use), 1)
                act.wait_ge(*filled(("my", 0), item))
                fn(y_e[:, 0, :], ps(("my", 0)), ACT.Copy).then_inc(drain_sem(("my", 0)), 1)

            with act.Fori(0, NE) as item:
                expert_item(item)
            act.wait_ge(route_ready, 1)
            n_items = act.value_load(route_i[0:1, 0:1], min_val=NE, max_val=NITEM)
            with act.Fori(NE, NITEM) as item:
                with act.If(n_items > item):
                    expert_item(item)
            act.wait_ge(experts_done, 1)
            squares(4)

        @block.gpsimd
        def _(pool):
            nc.gpsimd.memset(pool_w, 0.0).then_inc(pool_w_zero, 1)

            def mask_diagonals(v, mask, s):
                blocks = v.rearrange("p (b c) -> p b c", b=3)[:, 0:3:2, :]
                nc.gpsimd.tensor_tensor(blocks, blocks, mask[:, None, :].to_broadcast([P, 2, P]),
                                        ALU.mult).then_inc(s, 1)

            pool.wait_ge(*filled(("odd", 0)))
            nc.gpsimd.memset(mv[:, :, 128:129], 1.0).then_inc(mv_ones, 1)
            for h in range(SB_H + 1):
                if h < SB_H:
                    pool.wait_ge(sbsp_ready, h + 1)
                    mask_diagonals(sb_sp[:, h % 3, :], u_str, sbsp_masked)
                if h:
                    pool.wait_ge(sbw_exp, h)
                    mask_diagonals(sb_w[:, (h - 1) % 4, :], u_str, sbw_masked)
            for h in range(ML_H):
                pool.wait_ge(*drained(("ml_s", h)))
                mask_diagonals(ml_w[:, h % 4, :], u_inc, mw_masked)

        @block.vector
        def _(dve):
            V = nc.vector
            steps = Steps(dve, dve_step)

            def norm_scale(j):
                dve.wait_ge(ssq_ready, T * (j + 1))
                steps.done(V.tensor_scalar(inv_ms[:, j, :], ssq[:, j, :], 1.0 / DM, EPS, ALU.mult, ALU.add))
                V.reciprocal(inv_ms[:, j, :], inv_ms[:, j, :]).then_inc(inv_ready, 1)
                dve.wait_ge(rstd_ready, j + 1)
                if j == 4:
                    return
                for t in range(T):
                    V.tensor_scalar(hn[:, t, :], x[:, t, :], rstd[:, j, t:t + 1], None, ALU.mult).then_inc(
                        hn_ready, 1)

            def norm_banks(j):
                for i in (0, 2):
                    dve.wait_ge(*filled(("norm", j, i)))
                    for c in range(2):
                        k = 2 * i + c
                        last = V.tensor_scalar(ht[:, k, :], ps(("norm", j, i))[:, c * SEQ:(c + 1) * SEQ],
                                               vec[:, V_NORM + 8 * j + k:V_NORM + 8 * j + k + 1], None, ALU.mult)
                    last.then_inc(drain_sem(("norm", j, i)), 1)

            def drain_jobs(stage, jobs, numbers):
                for n in numbers:
                    dve.wait_ge(*filled((stage, n)))
                    dst, scale, shape = job_target(jobs[n])
                    V.tensor_scalar(dst, shape(ps((stage, n))), scale, None, ALU.mult).then_inc(
                        drain_sem((stage, n)), 1)

            def add_to_x(names):
                for n, use in enumerate(names):
                    t, nh = n // 2, n % 2
                    quarter = x[:, t, nh * 512:(nh + 1) * 512]
                    dve.wait_ge(*filled(use))
                    V.tensor_tensor(quarter, quarter, ps(use), ALU.add).then_inc(drain_sem(use), 1)

            def row_bias(b, n):
                return b[:, None, :].to_broadcast([P, T, n])

            dve.wait_ge(x_loaded, 32)
            dve.wait_ge(*filled("vectors"))
            V.tensor_copy(vec[:, :], ps("vectors")[:, 0:V_ALL]).then_inc(drain_sem("vectors"), 1)
            norm_scale(0)
            dve.wait_ge(*drained("vectors"))
            norm_banks(0)
            dve.wait_ge(gate_w_loaded, 16 * 5)
            dve.wait_ge(*filled("fgate"))
            V.tensor_tensor(fu, ps("fgate")[:, 0:T * FOX_H].rearrange("p (t h) -> p t h", t=T),
                            row_bias(b_fgate, FOX_H), ALU.add).then_inc(drain_sem("fgate"), 1)
            dve.wait_ge(*drained("fgate"))
            V.scalar_tensor_tensor(fe, fu, -1.0, fu, ALU.mult, ALU.min).then_inc(fu_ready, 1)
            dve.wait_ge(fln_ready, 1)
            steps.done(V.scalar_tensor_tensor(flf, fu, 0.0, fe, ALU.min, ALU.subtract))
            V.tensor_scalar(fnlf, flf, -1.0, None, ALU.mult).then_inc(flf_ready, 1)
            drain_jobs("even", EVEN_JOBS, range(0, len(EVEN_JOBS), 2))
            dve.wait_ge(*filled("fcum"))
            V.tensor_copy(fcum, ps("fcum")[:, 0:T * FOX_H].rearrange("p (t h) -> p t h", t=T)).then_inc(
                drain_sem("fcum"), 1)
            dve.wait_ge(*drained("fcum"))
            for g2 in range(2):
                dve.wait_ge(*filled(("pool", g2)))
                V.tensor_copy(pooled[:, g2, :], ps(("pool", g2))[:, 0:SEQ]).then_inc(drain_sem(("pool", g2)), 1)
                dve.wait_ge(*filled(("poolmix", g2)))
                V.tensor_scalar(mix_t[:, g2, :], ps(("poolmix", g2))[:, 0:SEQ], vec[:, V_POOL + g2:V_POOL + g2 + 1],
                                None, ALU.mult).then_inc(drain_sem(("poolmix", g2)), 1)
            for h in range(FOX_H + 1):
                if h < FOX_H:
                    use = ("fox_s", h)
                    buf = fp[:, h % 3, :]
                    dve.wait_ge(*filled(use))
                    V.scalar_tensor_tensor(buf[:, 0:P], ps(use)[:, 0:P], fcum[:, 0, h:h + 1],
                                           cst[:, C_CM + P:C_CM + 2 * P], ALU.add, ALU.add)
                    V.scalar_tensor_tensor(buf[:, P:384], ps(use)[:, P:384], fcum[:, 1, h:h + 1],
                                           cst[:, C_CM:C_CM + 2 * P], ALU.add, ALU.add).then_inc(drain_sem(use), 1)
                    dve.wait_ge(*drained(use))
                    V.tensor_reduce(fmax[:, h, 0:1], buf[:, 0:P], AX, ALU.max, negate=True).then_inc(fmax_ready, 1)
                    V.tensor_reduce(fmax[:, h, 1:2], buf[:, P:384], AX, ALU.max, negate=True).then_inc(
                        fmax_ready, 1)
                if h:
                    g = h - 1
                    buf = fp[:, g % 3, :]
                    dve.wait_ge(fexp_ready, h)
                    steps.done(V.reciprocal(finv[:, g, :], fsum[:, g, :]))
                    V.tensor_scalar(buf[:, 0:P], buf[:, 0:P], finv[:, g, 0:1], None, ALU.mult)
                    V.tensor_scalar(buf[:, P:384], buf[:, P:384], finv[:, g, 1:2], None, ALU.mult).then_inc(
                        fprob_ready, 1)
            add_to_x([("wout", 0, n) for n in range(4)])

            norm_scale(1)
            norm_banks(1)
            for n, (c, j) in enumerate([(c, j) for c in range(NCH) for j in range(4)]):
                use = ("gu", c, j)
                dve.wait_ge(fsilu_ready, n + 1)
                V.tensor_tensor(f_act[:, (c % 2) * 4 + j, :], f_silu[:, n % 2, :], ps(use)[:, SEQ:2 * SEQ],
                                ALU.mult).then_inc(drain_sem(use), 1)
            add_to_x([("fdown", n) for n in range(4)])

            norm_scale(2)
            norm_banks(2)
            dve.wait_ge(*filled("mgate"))
            V.tensor_tensor(mu, ps("mgate")[:, 0:T * 2 * ML_H].rearrange("p (t h) -> p t h", t=T),
                            row_bias(b_mgate, 2 * ML_H), ALU.add).then_inc(drain_sem("mgate"), 1)
            dve.wait_ge(*drained("mgate"))
            V.scalar_tensor_tensor(me, mu[:, :, ML_H:], -1.0, mu[:, :, ML_H:], ALU.mult, ALU.min).then_inc(mu_ready, 1)
            dve.wait_ge(mln_ready, 1)
            V.scalar_tensor_tensor(ml_lf, mu[:, :, ML_H:], 0.0, me, ALU.min, ALU.subtract).then_inc(mlf_ready, 1)
            drain_jobs("odd", ODD_JOBS, [n for n in range(len(ODD_JOBS)) if n not in ACT_ODD_JOBS])
            dve.wait_ge(*filled("mcum"))
            V.tensor_copy(m_rn_f, ps("mcum")[:, 0:T * ML_H].rearrange("p (t h) -> p t h", t=T)).then_inc(
                drain_sem("mcum"), 1)
            dve.wait_ge(*drained("mcum"))
            steps.done(V.tensor_tensor(m_an, mu[:, :, 0:ML_H], m_rn_f, ALU.subtract))
            for h in range(ML_H):
                use = ("mrow", h)
                dve.wait_ge(*filled(use))
                steps.done(V.tensor_copy(ml_f[:, 0, :], ps(use)[:, 0:SEQ]))
                V.tensor_tensor(ml_f[:, 1, :], ps(use)[:, SEQ:2 * SEQ], ml_f[:, 0, :], ALU.subtract).then_inc(
                    drain_sem(use), 1)
                dve.wait_ge(*drained(use))
                steps.done(V.tensor_tensor_scan(ml_r[:, h, :], ml_f[:, 1, :], ml_f[:, 1, :], -3e38, ALU.max,
                                                ALU.max))
                V.scalar_tensor_tensor(ml_r[:, h, :], ml_r[:, h, :], -1.0, ml_f[:, 0, :], ALU.mult,
                                       ALU.min).then_inc(mr_ready, 1)
                dve.wait_ge(mr_ready, h + 1)

            def conv_chunk(k):
                src = mq_in[:, k, :] if k < 4 else mk_in[:, k - 4, :]
                dst = mqk[:, k, :]

                def tap(j):
                    return vec[:, V_CONV + 8 * j + k:V_CONV + 8 * j + k + 1]

                n = steps.mark(V.tensor_scalar(dst, src, tap(TAPS - 1), None, ALU.mult))
                for d in range(1, TAPS):
                    steps.wait(n)
                    ins = V.scalar_tensor_tensor(dst[:, d:], src[:, 0:SEQ - d], tap(TAPS - 1 - d), dst[:, d:],
                                                 ALU.mult, ALU.add)
                    if d < TAPS - 1:
                        n = steps.mark(ins)
                    else:
                        ins.then_inc(conv_ready, 1)

            for n in (7, 9):
                dve.wait_ge(*drained(("odd", n)))
            for n in (6, 8):
                dve.wait_ge(*drained(("odd", n)))
            for h in range(SB_H + 1):
                if h < SB_H:
                    use = ("sb_z", h)
                    z = ps(use)[:, 0:384]
                    dve.wait_ge(sbl_ready, h + 1)
                    V.scalar_tensor_tensor(sb_sp[:, h % 3, :], z, 0.0, sb_l[:, h % 2, :], ALU.max,
                                           ALU.add).then_inc(sbsp_ready, 1)
                    V.scalar_tensor_tensor(sb_w[:, h % 4, :], z, 0.0, sb_l[:, h % 2, :], ALU.min,
                                           ALU.subtract).then_inc(drain_sem(use), 1)
                    conv_chunk(h)
                if h == 2:
                    dve.wait_ge(*filled("mr"))
                    V.tensor_tensor(m_em, ps("mr")[:, 0:T * ML_H].rearrange("p (t h) -> p t h", t=T), m_rn_f,
                                    ALU.subtract).then_inc(drain_sem("mr"), 1)
                if h:
                    use = ("sb_lat", h - 1)
                    buf = sb_w[:, (h - 1) % 4, :]
                    dve.wait_ge(*drained(("sb_z", h - 1)))
                    dve.wait_ge(*filled(use))
                    V.tensor_tensor(buf, buf, ps(use)[:, 0:384], ALU.subtract).then_inc(drain_sem(use), 1)

            dve.wait_ge(mem_ready, 1)

            def ml_exponent(h):
                V.tensor_scalar(ml_e[:, h % 3, 0:SEQ], ml_r[:, h, :], m_an[:, 0, h:h + 1], 0.0, ALU.add, ALU.min)
                V.tensor_scalar(ml_e[:, h % 3, SEQ:384], ml_r[:, h, P:SEQ], m_an[:, 1, h:h + 1], 0.0, ALU.add,
                                ALU.min).then_inc(me_in, 1)

            ml_exponent(0)
            for h in range(ML_H + 1):
                if h < ML_H:
                    if h + 1 < ML_H:
                        ml_exponent(h + 1)
                    use = ("ml_s", h)
                    dve.wait_ge(me_ready, h + 1)
                    dve.wait_ge(*filled(use))
                    V.scalar_tensor_tensor(ml_w[:, h % 4, :], ml_e[:, h % 3, :], P ** -0.5, ps(use)[:, 0:384],
                                           ALU.mult, ALU.mult).then_inc(drain_sem(use), 1)
                if h:
                    g = h - 1
                    use = ("ml_n", g)
                    o = ps(use)[:, 0:2 * 129].rearrange("p (t d) -> p t d", t=T)
                    dve.wait_ge(*filled(use))
                    steps.done(V.tensor_copy(m_den[:, g, :], o[:, :, 128]))
                    steps.done(V.scalar_tensor_tensor(m_den[:, g, :], m_den[:, g, :], -1.0, m_den[:, g, :],
                                                      ALU.mult, ALU.max))
                    steps.done(V.tensor_tensor(m_den[:, g, :], m_den[:, g, :], m_em[:, :, g], ALU.max))
                    steps.done(V.reciprocal(m_rden[:, g, :], m_den[:, g, :]))
                    for t in range(T):
                        last = V.tensor_scalar(ml_h[:, t, g * P:(g + 1) * P], o[:, t, 0:P], m_rden[:, g, t:t + 1],
                                               None, ALU.mult)
                    last.then_inc(drain_sem(use), 1)
            dve.wait_ge(mh_sq, T * ML_H)
            steps.done(V.tensor_scalar(m_inv, m_ssq, 1.0 / P, EPS, ALU.mult, ALU.add))
            V.reciprocal(m_inv, m_inv).then_inc(mh_inv, 1)
            dve.wait_ge(mh_rstd, 1)
            for n in (12, 13):
                dve.wait_ge(*drained(("odd", n)))
            for t in range(T):
                heads = ml_h[:, t, :].rearrange("p (h d) -> p h d", h=ML_H)
                steps.done(V.tensor_tensor(heads, heads, m_rstd[:, :, t:t + 1].to_broadcast([P, ML_H, P]),
                                           ALU.mult))
                V.tensor_tensor(ml_h[:, t, :], ml_h[:, t, :], ml_o[:, t, :], ALU.mult).then_inc(md_ready, 1)
            add_to_x([("wout", 1, n) for n in range(4)])

            norm_scale(3)
            norm_banks(3)
            dve.wait_ge(*filled("router"))
            V.tensor_copy(r_log, ps("router")[:, 0:T * NE].rearrange("p (t e) -> p t e", t=T)).then_inc(
                drain_sem("router"), 1)
            dve.wait_ge(*drained("router"))
            steps.done(V.tensor_reduce(r_max, r_log, AX, ALU.max))
            V.tensor_tensor(r_e, r_log, r_max.to_broadcast([P, T, NE]), ALU.subtract).then_inc(r_in, 1)
            for t in range(T):
                other = r_log[:, t, None, :].to_broadcast([P, NE, NE])
                own = r_log[:, t, :, None].to_broadcast([P, NE, NE])
                cmp_t, eq_t = r_cmp[:, t * NE:(t + 1) * NE, :], r_eq[:, t * NE:(t + 1) * NE, :]
                V.tensor_tensor(cmp_t, other, own, ALU.is_gt)
                steps.done(V.tensor_tensor(eq_t, other, own, ALU.is_equal))
                steps.done(V.tensor_tensor(eq_t, eq_t, cst[:, C_TIE:C_TIE + NE * NE].rearrange(
                    "p (a b) -> p a b", a=NE), ALU.mult))
                steps.done(V.tensor_tensor(cmp_t, cmp_t, eq_t, ALU.add))
                steps.done(V.tensor_reduce(r_rank[:, t, :], cmp_t, AX, ALU.add))
            V.tensor_scalar(r_sel, r_rank, 1.5, None, ALU.is_lt).then_inc(rsel_ready, 1)
            dve.wait_ge(rsel_ready, 1)
            dve.wait_ge(r_exp, 1)
            steps.done(V.tensor_tensor(r_e, r_e, r_sel, ALU.mult))
            steps.done(V.tensor_reduce(r_sum, r_e, AX, ALU.add))
            steps.done(V.reciprocal(r_sum, r_sum))
            steps.done(V.tensor_tensor(r_gate, r_e, r_sum.to_broadcast([P, T, NE]), ALU.mult))
            dve.wait_ge(*filled("rank"))
            V.tensor_copy(r_cnt[:, 0, :], ps("rank")[:, 2 * NE:3 * NE])
            V.tensor_tensor(r_pos, ps("rank")[:, 0:T * NE].rearrange("p (t e) -> p t e", t=T), r_sel,
                            ALU.mult).then_inc(drain_sem("rank"), 1)
            dve.wait_ge(*drained("rank"))
            steps.done(V.tensor_scalar(r_pos, r_pos, -1.0, None, ALU.add))
            steps.done(V.tensor_scalar(r_over, r_cnt[:, 0, :], float(P) + 0.5, None, ALU.is_gt))
            steps.done(V.tensor_tensor_scan(r_oc, ones[:, 0:NE], r_over, 0.0, ALU.mult, ALU.add))
            steps.done(V.tensor_scalar(r_eidf[:, 0:1], r_oc[:, NE - 1:NE], float(NE), None, ALU.add))
            steps.done(V.tensor_tensor(r_oc, r_oc, r_over, ALU.subtract))
            for t in range(T):
                V.tensor_copy(pos_i[:, 0:NE, t], r_pos[:, t, :])
                steps.done(V.tensor_copy(gate_i[:, 0:NE, t], r_gate[:, t, :]))
            steps.done(V.tensor_scalar(r_pos, r_pos, -float(P), None, ALU.add))
            for j in range(NOVER):
                steps.done(V.scalar_tensor_tensor(r_tmp[:, 0, :], r_oc, float(j), r_over, ALU.is_equal, ALU.mult))
                pick = r_tmp[:, 0:1, :].to_broadcast([P, T, NE])
                steps.done(V.tensor_tensor(r_tmp[:, 1:3, :], r_pos, pick, ALU.mult))
                steps.done(V.tensor_reduce(pos_i[:, NE + j, :], r_tmp[:, 1:3, :], AX, ALU.add))
                steps.done(V.tensor_tensor(r_tmp[:, 1:3, :], r_gate, pick, ALU.mult))
                steps.done(V.tensor_reduce(gate_i[:, NE + j, :], r_tmp[:, 1:3, :], AX, ALU.add))
                steps.done(V.tensor_tensor(r_tmp[:, 3, :], cst[:, C_EID:C_EID + NE], r_tmp[:, 0, :], ALU.mult))
                steps.done(V.tensor_reduce(r_eidf[:, 1 + j:2 + j], r_tmp[:, 3, :], AX, ALU.add))
            V.tensor_copy(route_i[0:1, 0:1 + NOVER], r_eidf[0:1, 0:1 + NOVER]).then_inc(route_ready, 1)

            def expert_item(item):
                for t in range(T):
                    pos = pos_i[:, bass.ds(item, 1), t]
                    V.tensor_scalar(sel[:, t, :], cst[:, C_IOTA:C_IOTA + P], pos, None, ALU.is_equal)
                    last = V.tensor_scalar(sel_g[:, t, :], cst[:, C_IOTA:C_IOTA + P], pos,
                                           gate_i[:, bass.ds(item, 1), t], ALU.is_equal, ALU.mult)
                last.then_inc(sel_ready, 1)
                use = ("gather", 0)
                dve.wait_ge(*filled(use, item))
                for k in range(4):
                    last = V.tensor_scalar(xg_t[:, k, :], ps(use)[:, k * P:(k + 1) * P],
                                           vec[:, V_NORM + 24 + k:V_NORM + 25 + k], None, ALU.mult)
                last.then_inc(drain_sem(use), 1)
                for c in range(NCH):
                    dve.wait_ge(*drained(("mg", c), item))
                    dve.wait_ge(*filled(("mu", c), item))
                    V.tensor_tensor(m_act[:, c % 2, :], m_silu[:, c % 2, :], ps(("mu", c)), ALU.mult).then_inc(
                        drain_sem(("mu", c)), 1)
                dve.wait_ge(*filled(("my", 1), item))
                V.tensor_copy(y_e[:, 1, :], ps(("my", 1))).then_inc(drain_sem(("my", 1)), 1)
                for n in range(4):
                    t, nh = n // 2, n % 2
                    use = ("mc", n)
                    quarter = x[:, t, nh * 512:(nh + 1) * 512]
                    dve.wait_ge(*filled(use, item))
                    V.tensor_tensor(quarter, quarter, ps(use), ALU.add).then_inc(drain_sem(use), 1)

            dve.wait_ge(route_ready, 1)
            with dve.Fori(0, NE) as item:
                expert_item(item)
            n_items = dve.value_load(route_i[0:1, 0:1], min_val=NE, max_val=NITEM)
            with dve.Fori(NE, NITEM) as item:
                with dve.If(n_items > item):
                    expert_item(item)
            V.memset(r_max, 0.0).then_inc(experts_done, 1)

            norm_scale(4)
            dve.wait_ge(late_loaded, 32)
            for t in range(T):
                V.scalar_tensor_tensor(hn[:, t, :], x[:, t, :], rstd[:, 4, t:t + 1], g_final[:, :], ALU.mult,
                                       ALU.mult).then_inc(out_ready, 1)


_WEIGHTS = ["norm_mix_g", "norm_ffn_g", "norm_final_g", "ev_w_in", "ev_b_forget", "ev_pool_w", "ev_pool_scale",
            "ev_w_out", "ffn_w_gate", "ffn_w_up", "ffn_w_down", "od_w_in", "od_b_igate", "od_b_fgate", "od_conv_w",
            "od_head_norm_g", "od_w_out", "moe_w_router", "moe_w_gate", "moe_w_up", "moe_w_down"]


def kernel(**inputs):
    import concourse.bacc as _bacc
    from concourse.bass_utils import run_bass_kernel_spmd as _run

    nc = _bacc.Bacc("TRN2", target_bir_lowering=False, num_devices=1)
    arrays, aps = {}, {}
    for name in ["x"] + _WEIGHTS:
        a = np.ascontiguousarray(inputs[name])
        arrays[f"in_{name}"] = a
        aps[name] = nc.dram_tensor(f"in_{name}", a.shape, mybir.dt.from_np(a.dtype), kind="ExternalInput").ap()
    arrays["in_constants"] = constants()
    cst_d = nc.dram_tensor("in_constants", (P, C_ALL), F32, kind="ExternalInput").ap()
    out_d = nc.dram_tensor("out_trunk", (1, SEQ, DM), F32, kind="ExternalOutput").ap()
    build_trunk(nc, aps["x"], aps, cst_d, out_d)
    r = _run(nc, [arrays], core_ids=[0])
    return r.results[0]["out_trunk"]
```

```python
from contextlib import ExitStack

import numpy as np
import concourse.bass as bass
from concourse import mybir

F32 = mybir.dt.float32
F32R = mybir.dt.float32r
I32 = mybir.dt.int32
ALU = mybir.AluOpType
ACT = mybir.ActivationFunctionType
AX = mybir.AxisListType.X

P = 128
SEQ = 256
T = SEQ // P
DM = 1024
DK = DM // P
EPS = 1e-6
POOL_WINDOWS = (2, 4, 8, 16)
POOL_W = DM // 4
HD = 64
FOX_H = (DM - POOL_W) // HD
SB_H = 8
ML_H = 4
TAPS = 4
D_FF = 7 * DM // 2
FC = 512
NCH = D_FF // FC
NE = 8
NOVER = (2 * SEQ) // (P + 1)
NITEM = NE + NOVER
RAW = 6
SPLITS = 3
PIECE = DM * SEQ // P
EVEN_PIECES = 10
ODD_PIECES = 14
WO_PIECES = 4
FFN_PIECES = 6 * NCH
N_WO0 = EVEN_PIECES
N_FFN = N_WO0 + WO_PIECES
N_ODD = N_FFN + FFN_PIECES
N_WO1 = N_ODD + ODD_PIECES
N_MOE = N_WO1 + WO_PIECES
assert FFN_PIECES % RAW == 0 and FFN_PIECES % SPLITS == 0
MASKED = -1e30
ARENA = 12288

C_ID = 0
C_UINC = 128
C_ONES = 256
C_USTR = 384
C_LSTR = 512
C_CM = 640
C_IOTA = 896
C_TIE = 1024
C_EID = C_TIE + 64
C_SLOTNO = C_EID + 8
C_BAND = C_SLOTNO + 16
C_ALL = C_BAND + len(POOL_WINDOWS) * 3 * P

V_CONV = 0
V_POOL = 32
V_HEAD = 34
V_ALL = 38

S_F = 0
S_M = FOX_H
S_R = FOX_H + 2 * ML_H
S_ALL = S_R + NE


def constants():
    c = np.zeros((P, C_ALL), np.float32)
    i, o = np.meshgrid(np.arange(P), np.arange(P), indexing="ij")
    c[:, C_ID:C_ID + P] = i == o
    c[:, C_UINC:C_UINC + P] = i <= o
    c[:, C_ONES:C_ONES + P] = 1
    c[:, C_USTR:C_USTR + P] = i < o
    c[:, C_LSTR:C_LSTR + P] = i > o
    c[:, C_CM + P:C_CM + 2 * P] = np.where(o <= i, 0.0, MASKED)
    c[:, C_IOTA:C_IOTA + P] = o
    e, f = np.meshgrid(np.arange(NE), np.arange(NE), indexing="ij")
    c[:, C_TIE:C_TIE + NE * NE] = (f < e).reshape(-1)
    c[:, C_EID:C_EID + NE] = np.arange(NE)
    c[:, C_SLOTNO:C_SLOTNO + NOVER] = np.arange(NOVER)
    ti, to = np.meshgrid(np.arange(SEQ), np.arange(SEQ), indexing="ij")
    for g, w in enumerate(POOL_WINDOWS):
        band = np.where((ti <= to) & (ti > to - w), 1.0 / np.minimum(to + 1, w), 0.0) - (ti == to)
        for b, blk in enumerate((band[:P, :P], band[:P, P:], band[P:, P:])):
            at = C_BAND + (3 * g + b) * P
            c[:, at:at + P] = blk
    return c


class Banks:

    def __init__(self):
        self.count = [0] * 8
        self.uses = {}

    def fill(self, name, bank):
        self.count[bank] += 1
        self.uses[name] = (bank, self.count[bank])


EVEN_JOBS = ([("N", "a", 0)] + [("T", "q", c) for c in (0, 2, 4)] + [("T", "k", c) for c in (0, 2, 4)]
             + [("N", "v", c) for c in range(3)])
ODD_JOBS = ([("T", "sq", c) for c in (0, 2)] + [("T", "sk", c) for c in (0, 2)] + [("N", "sv", c) for c in (0, 1)]
            + [("T", "mq", c) for c in (0, 2)] + [("T", "mk", c) for c in (0, 2)] + [("N", "mv", c) for c in (0, 1)]
            + [("N", "mo", c) for c in (0, 1)])
assert len(EVEN_JOBS) == EVEN_PIECES and len(ODD_JOBS) == ODD_PIECES

FFN_ORDER = []
EXPERT_ORDER = []
for _c in range(NCH + 1):
    if _c < NCH:
        FFN_ORDER += [("g", _c, 0), ("u", _c, 0), ("g", _c, 1), ("u", _c, 1)]
        EXPERT_ORDER += [("g", _c, 0), ("g", _c, 1), ("u", _c, 0), ("u", _c, 1)]
    if _c:
        FFN_ORDER += [("d", _c - 1, 0), ("d", _c - 1, 1)]
        EXPERT_ORDER += [("d", _c - 1, 0), ("d", _c - 1, 1)]


def ends_a_fill(key, experts):
    kind, c, h = key
    if kind == "d":
        return (("my", 1) if experts else ("fdown", 3)) if (c, h) == (NCH - 1, 1) else None
    if experts:
        return ("m" + kind, c) if h else None
    return ("gu", c, 2 * h + 1) if kind == "u" else None


FFN_COUNTED = [k for k in FFN_ORDER if ends_a_fill(k, False) is None]
EXPERT_COUNTED = [k for k in EXPERT_ORDER if ends_a_fill(k, True) is None]


def plan_banks():
    banks = Banks()

    def norm(j):
        for i in range(4):
            banks.fill(("norm", j, i), i)

    banks.fill("vectors", 7)
    norm(0)
    banks.fill("fgate", 4)
    for n in range(len(EVEN_JOBS)):
        banks.fill(("even", n), (5, 6, 7, 4)[n % 4])
    banks.fill("fcum", 2)
    for g in range(2):
        banks.fill(("pool", g), 3)
        banks.fill(("poolmix", g), 3)
    for h in range(FOX_H + 2):
        if h < FOX_H:
            banks.fill(("fox_s", h), h % 2)
        if 1 <= h <= FOX_H:
            banks.fill(("fox_pt", h - 1), 2 + (h - 1) % 2)
        if h >= 2 and h % 2 == 1:
            banks.fill(("fox_o", (h - 2) // 2), 4 + (h - 2) // 2 % 2)
    for n in range(4):
        banks.fill(("wout", 0, n), n)
    norm(1)
    for c in range(NCH):
        for j in range(4):
            banks.fill(("gu", c, j), j)
    for n in range(4):
        banks.fill(("fdown", n), 4 + n)
    norm(2)
    banks.fill("mgate", 4)
    for n in range(len(ODD_JOBS)):
        banks.fill(("odd", n), (5, 6, 7, 4)[n % 4])
    banks.fill("mcum", 2)
    for h in range(ML_H):
        banks.fill(("mrow", h), 6 + h % 2)
    banks.fill("mr", 3)
    for h in range(SB_H + 2):
        if h < SB_H:
            banks.fill(("sb_z", h), h % 2)
        if 1 <= h <= SB_H:
            banks.fill(("sb_lat", h - 1), 2 + (h - 1) % 2)
        if h >= 2 and h % 2 == 1:
            banks.fill(("sb_o", (h - 2) // 2), 4 + (h - 2) // 2 % 2)
    for h in range(ML_H + 1):
        if h < ML_H:
            banks.fill(("ml_s", h), h % 2)
        if h:
            banks.fill(("ml_n", h - 1), 2 + (h - 1) % 2)
    for h in range(ML_H):
        banks.fill(("ml_t", h), 4 + h % 2)
    for n in range(4):
        banks.fill(("wout", 1, n), n)
    norm(3)
    banks.fill("router", 4)
    banks.fill("rank", 5)
    before = list(banks.count)
    for half in range(2):
        banks.fill(("gather", half), 2 * half)
    banks.fill("sgt", 7)
    for c in range(NCH + 1):
        if c < NCH:
            banks.fill(("mg", c), c % 2)
            banks.fill(("mu", c), 2 + c % 2)
        if c:
            banks.fill(("mt", c - 1), 6)
    for n in range(2):
        banks.fill(("my", n), 4 + n)
    for n in range(4):
        banks.fill(("mc", n), 6 + n % 2)
    per_item = [a - b for a, b in zip(banks.count, before)]
    return banks.uses, per_item


def build_trunk(nc, x_d, w, cst_d, out_d):
    uses, bank_fills_per_item = plan_banks()

    with ExitStack() as ctx:
        def sb(name, shape, dt=F32):
            return ctx.enter_context(nc.sbuf_tensor(name, shape, dt))

        def sem(name):
            return ctx.enter_context(nc.semaphore(name))

        bank = [ctx.enter_context(nc.psum_tensor(f"bank{b}", [P, 512], F32)) for b in range(8)]
        s_filled = [sem(f"filled{b}") for b in range(8)]
        s_drained = [sem(f"drained{b}") for b in range(8)]
        raw_full = [sem(f"raw_full{r}") for r in range(RAW)]
        high_ready = sem("high_ready")
        split_ready = sem("split_ready")
        wo_piece_used = sem("wo_piece_used")
        ffn_piece_used = sem("ffn_piece_used")
        expert_piece_used = sem("expert_piece_used")

        def ps(use):
            return bank[uses[use][0]][:, :]

        def filled(use, item=0):
            b, n = uses[use]
            return s_filled[b], n + item * bank_fills_per_item[b]

        def drained(use, item=0):
            b, n = uses[use]
            return s_drained[b], n + item * bank_fills_per_item[b]

        def fill_sem(use):
            return s_filled[uses[use][0]]

        def drain_sem(use):
            return s_drained[uses[use][0]]

        def open_bank(pe, use, item=0):
            b, n = uses[use]
            if n > 1:
                pe.wait_ge(s_drained[b], n - 1 + item * bank_fills_per_item[b])

        raw = sb("raw", [P, RAW, PIECE])
        high = sb("high", [P, SPLITS, PIECE], F32R)
        low = sb("low", [P, SPLITS, PIECE], F32R)
        x = sb("x", [P, T, DM])
        hn = sb("hn", [P, T, DM])
        ht_h = sb("ht_h", [P, DK, SEQ], F32R)
        ht_l = sb("ht_l", [P, DK, SEQ], F32R)
        mix_h = sb("mix_h", [P, DK, SEQ], F32R)
        mix_h_at = nc.sbuf_base - DK * SEQ * 4
        mix_l = sb("mix_l", [P, DK, SEQ], F32R)
        cst = sb("cst", [P, C_BAND])
        g_row = sb("g_row", [P, DM])
        vec_rows = sb("vec_rows", [V_ALL, P])
        vec = sb("vec", [P, V_ALL])
        w_small = sb("w_small", [P, DK, S_ALL])
        ws_h = sb("ws_h", [P, DK, S_ALL], F32R)
        ws_l = sb("ws_l", [P, DK, S_ALL], F32R)
        b_fgate = sb("b_fgate", [P, FOX_H])
        b_mgate = sb("b_mgate", [P, 2 * ML_H])
        ssq = sb("ssq", [P, 5, T])
        inv_ms = sb("inv_ms", [P, 5, T])
        rstd = sb("rstd", [P, 5, T])
        route_i = sb("route_i", [1, 16], I32)
        s_cols = sb("s_cols", [P, 720])
        arena = sb("arena", [P, ARENA])
        arena_at = nc.sbuf_base - ARENA * 4

        f_act_h = nc.alloc_sbuf_tensor_at("f_act_h", [P, 8, SEQ], F32R, offset=arena_at)
        f_act_l = nc.alloc_sbuf_tensor_at("f_act_l", [P, 8, SEQ], F32R, offset=arena_at + 8 * SEQ * 4)
        xg_h = nc.alloc_sbuf_tensor_at("xg_h", [P, DK, P], F32R, offset=arena_at)
        xg_l = nc.alloc_sbuf_tensor_at("xg_l", [P, DK, P], F32R, offset=arena_at + DK * P * 4)
        m_act_h = nc.alloc_sbuf_tensor_at("m_act_h", [P, 8, P], F32R, offset=arena_at + 2 * DK * P * 4)
        m_act_l = nc.alloc_sbuf_tensor_at("m_act_l", [P, 8, P], F32R, offset=arena_at + 3 * DK * P * 4)
        mq_in = nc.alloc_sbuf_tensor_at("mq_in", [P, 4, SEQ], F32, offset=mix_h_at + 4 * SEQ * 4)

        taken = [0, 0]

        def view(region, at, *shape):
            size = int(np.prod(shape))
            v = region[:, at:at + size]
            if len(shape) == 2:
                return v.rearrange("p (a b) -> p a b", a=shape[0])
            if len(shape) == 3:
                return v.rearrange("p (a b c) -> p a b c", a=shape[0], b=shape[1])
            return v

        def layout(region, *parts):
            at, out = 0, []
            for shape in parts:
                out.append(view(region, at, *shape))
                at += int(np.prod(shape))
            taken[0] = max(taken[0], at)
            return out

        bands, pool_a, fq, fk, fv, fp, fpt, pooled, pool_w = layout(
            arena, (len(POOL_WINDOWS) * 3, P), (T, POOL_W), (6, SEQ), (6, SEQ), (T, FOX_H * HD), (3, 384), (4, 384),
            (2, SEQ), (2, P))
        _, f_silu, f_v = layout(arena, (16, SEQ), (2, SEQ), (2, SEQ))
        sq, sk, sv, mk_in, mqk, mv, sb_l, sb_sp, sb_w, ml_r, ml_f = layout(
            arena, (4, SEQ), (4, SEQ), (T, 512), (4, SEQ), (8, SEQ), (T * ML_H, 129), (2, 384), (3, 384), (4, 384),
            (ML_H, SEQ), (2, SEQ))
        assert taken[0] <= ARENA
        ml_e = sb_sp
        ml_w = sb_w
        ml_h = hn[:, :, 0:512]
        ml_o = hn[:, :, 512:1024]
        _, sel, sel_g, sgt, m_silu, m_act, y_e = layout(
            arena, (4 * DK, P), (T, P), (T, P), (T, P), (2, FC), (2, FC), (2, 512))
        taken[0] = 0

        taken[0] = 0
        (fu, fe, flf, fnlf, fcum, fmax, fsum, finv, mu, me, ml_lf, m_rn_f, m_an, m_em, m_den, m_rden, m_ssq, m_inv,
         m_rstd) = layout(
            s_cols, (T, FOX_H), (T, FOX_H), (T, FOX_H), (T, FOX_H), (T, FOX_H), (FOX_H, T), (FOX_H, T), (FOX_H, T),
            (T, 2 * ML_H), (T, ML_H), (T, ML_H), (T, ML_H), (T, ML_H), (T, ML_H), (ML_H, T), (ML_H, T), (ML_H, T),
            (ML_H, T), (ML_H, T))
        (r_log, r_cmp, r_eq, r_rank, r_sel, r_max, r_e, r_sum, r_gate, r_pos, r_cnt, r_over, r_oc, r_tmp, pos_i,
         gate_i, r_eidf) = layout(
            s_cols, (T, NE), (T * NE, NE), (T * NE, NE), (T, NE), (T, NE), (T, 1), (T, NE), (T, 1), (T, NE),
            (T, NE), (T, NE), (NE,), (NE,), (4, NE), (NITEM, T), (NITEM, T), (16,))
        assert taken[0] <= 720

        ident = cst[:, C_ID:C_ID + P]
        u_inc = cst[:, C_UINC:C_UINC + P]
        u_inc_ones = cst[:, C_UINC:C_UINC + 2 * P]
        ones = cst[:, C_ONES:C_ONES + P]
        u_str = cst[:, C_USTR:C_USTR + P]
        l_str = cst[:, C_LSTR:C_LSTR + P]

        x_loaded = sem("x_loaded")
        cst_loaded = sem("cst_loaded")
        vec_loaded = sem("vec_loaded")
        gate_w_loaded = sem("gate_w_loaded")
        bias_loaded = sem("bias_loaded")
        pool_w_zero = sem("pool_w_zero")
        pool_w_loaded = sem("pool_w_loaded")
        g_loaded = sem("g_loaded")
        ws_high = sem("ws_high")
        ws_ready = sem("ws_ready")
        ht_high = sem("ht_high")
        mix_high = sem("mix_high")
        fact_high = sem("fact_high")
        fact_ready = sem("fact_ready")
        xg_high = sem("xg_high")
        mact_high = sem("mact_high")
        x_updated = sem("x_updated")
        ssq_ready = sem("ssq_ready")
        inv_ready = sem("inv_ready")
        rstd_ready = sem("rstd_ready")
        hn_ready = sem("hn_ready")
        dve_step = sem("dve_step")
        act_step = sem("act_step")
        fu_ready = sem("fu_ready")
        fln_ready = sem("fln_ready")
        flf_ready = sem("flf_ready")
        fmax_ready = sem("fmax_ready")
        fexp_ready = sem("fexp_ready")
        fprob_ready = sem("fprob_ready")
        fsilu_ready = sem("fsilu_ready")
        mu_ready = sem("mu_ready")
        mln_ready = sem("mln_ready")
        mlf_ready = sem("mlf_ready")
        mv_ones = sem("mv_ones")
        conv_ready = sem("conv_ready")
        conv_silu = sem("conv_silu")
        mr_ready = sem("mr_ready")
        mem_ready = sem("mem_ready")
        sbl_ready = sem("sbl_ready")
        sbsp_ready = sem("sbsp_ready")
        sbsp_masked = sem("sbsp_masked")
        sbw_exp = sem("sbw_exp")
        sbw_masked = sem("sbw_masked")
        me_in = sem("me_in")
        me_ready = sem("me_ready")
        mw_masked = sem("mw_masked")
        mh_sq = sem("mh_sq")
        mh_inv = sem("mh_inv")
        mh_rstd = sem("mh_rstd")
        md_ready = sem("md_ready")
        r_in = sem("r_in")
        r_exp = sem("r_exp")
        rsel_ready = sem("rsel_ready")
        route_ready = sem("route_ready")
        sel_ready = sem("sel_ready")
        experts_done = sem("experts_done")
        out_ready = sem("out_ready")
        out_done = sem("out_done")

        def piece(buf, n, rows):
            return buf[:, n % (RAW if buf is raw else SPLITS), :].rearrange("p (k f) -> p k f", k=rows)

        def used(n, item=0):
            if n < N_WO0:
                return filled(("even", n))
            if N_ODD <= n < N_WO1:
                return filled(("odd", n - N_ODD))
            for layer, base in enumerate((N_WO0, N_WO1)):
                if base <= n < base + WO_PIECES - 1:
                    return wo_piece_used, layer * (WO_PIECES - 1) + n - base + 1
                if n == base + WO_PIECES - 1:
                    return filled(("wout", layer, 3))
            experts = n >= N_MOE
            key = (EXPERT_ORDER if experts else FFN_ORDER)[n - (N_MOE if experts else N_FFN)]
            fill = ends_a_fill(key, experts)
            if fill is not None:
                return filled(fill, item)
            if experts:
                return expert_piece_used, len(EXPERT_COUNTED) * item + EXPERT_COUNTED.index(key) + 1
            return ffn_piece_used, FFN_COUNTED.index(key) + 1

        def split_done(n, item=0):
            return split_ready, n + 1 + FFN_PIECES * item

        def make_high(act, n, item=0):
            act.wait_ge(raw_full[n % RAW], 16 * (n // RAW + 1) + item * (16 * FFN_PIECES // RAW))
            if n - SPLITS >= N_MOE or SPLITS <= n < N_MOE:
                act.wait_ge(*used(n - SPLITS, item))
            elif n == N_MOE + SPLITS - 1:
                b, count = uses[("my", 1)]
                act.wait_ge(s_filled[b], count - 1 + item * bank_fills_per_item[b])
            nc.scalar.activation(high[:, n % SPLITS, :], raw[:, n % RAW, :], ACT.Copy).then_inc(high_ready, 1)

        def make_low(dve, n, item=0):
            dve.wait_ge(high_ready, n + 1 + FFN_PIECES * item)
            nc.vector.tensor_tensor(low[:, n % SPLITS, :], raw[:, n % RAW, :], high[:, n % SPLITS, :].bitcast(F32),
                                    ALU.subtract).then_inc(split_ready, 1)

        class Steps:

            def __init__(self, eng, s):
                self.eng, self.s, self.n, self.item, self.per_item = eng, s, 0, 0, 0

            def mark(self, ins):
                self.n += 1
                ins.then_inc(self.s, 1)
                return self.n

            def wait(self, n):
                self.eng.wait_ge(self.s, n + self.item * self.per_item)

            def done(self, ins):
                self.wait(self.mark(ins))

        def job_target(job):
            _, what, idx = job

            def pairs(b):
                return b[:, :].rearrange("p (c n) -> p c n", c=2)

            cols = slice(idx * SEQ, (idx + 1) * SEQ)
            if what == "a":
                return pool_a, 1.0, pairs
            if what == "v":
                return fv[:, :, cols], 1.0, pairs
            if what == "sv":
                return sv[:, :, cols], 1.0, pairs
            if what == "mo":
                return ml_o[:, :, cols], 1.0, pairs
            if what == "mv":
                return (mv.rearrange("p (t h) d -> p t h d", t=T)[:, :, 2 * idx:2 * idx + 2, 0:P], 1.0,
                        lambda b: b[:, :].rearrange("p (t h d) -> p t h d", t=T, h=2))
            dst = {"q": fq, "k": fk, "sq": sq, "sk": sk, "mq": mq_in, "mk": mk_in}[what]
            return dst[:, idx:idx + 2, :], (HD ** -0.5 if what in ("q", "sq") else 1.0), pairs

        ACT_ODD_JOBS = [n for n, job in enumerate(ODD_JOBS) if n % 2 or job[1] == "mo"]

        block = ctx.enter_context(nc.Block())

        @block.sync
        def _(sp):
            def load(n, src, item=0):
                if n >= RAW:
                    sp.wait_ge(*split_done(n - RAW, item))
                sp.dma_start(piece(raw, n, src.shape[1]), src).then_inc(raw_full[n % RAW], 16)

            def columns(wt, c0, k0=0, k1=DK, width=SEQ):
                return wt.rearrange("(k p) c -> p k c", p=P)[:, k0:k1, c0:c0 + width]

            def ffn_pieces(wg, wu, wd):
                for j, (kind, c, h) in enumerate(FFN_ORDER):
                    if kind == "d":
                        src = columns(wd, 0, 4 * c + 2 * h, 4 * c + 2 * h + 2, DM)
                    else:
                        src = columns(wg if kind == "g" else wu, c * FC + h * SEQ)
                    load(N_FFN + j, src)

            def expert_pieces(item, expert):
                def of(name):
                    return w[name][0][bass.ds(expert, 1)].rearrange("o r c -> (o r) c")
                wg, wu, wd = of("moe_w_gate"), of("moe_w_up"), of("moe_w_down")
                for j, (kind, c, h) in enumerate(EXPERT_ORDER):
                    if kind == "d":
                        src = columns(wd, 0, 4 * c + 2 * h, 4 * c + 2 * h + 2, DM)
                    else:
                        src = columns(wg if kind == "g" else wu, c * FC, 4 * h, 4 * h + 4, FC)
                    load(N_MOE + j, src, item)

            for t in range(T):
                sp.dma_start(x[:, t, :], x_d[0, t * P:(t + 1) * P, :]).then_inc(x_loaded, 16)
            sp.dma_start(cst[:, :], cst_d[:, 0:C_BAND]).then_inc(cst_loaded, 16)
            for name, col, width, src_col in (("ev_w_in", S_F, FOX_H, EVEN_PIECES * SEQ),
                                              ("od_w_in", S_M, 2 * ML_H, ODD_PIECES * SEQ),
                                              ("moe_w_router", S_R, NE, 0)):
                sp.dma_start(w_small[:, :, col:col + width], columns(w[name][0], src_col, width=width)).then_inc(
                    gate_w_loaded, 16)
            for j in range(EVEN_PIECES):
                load(j, columns(w["ev_w_in"][0], j * SEQ))
            for j in range(WO_PIECES):
                load(N_WO0 + j, columns(w["ev_w_out"][0], 0, 2 * j, 2 * j + 2, DM))
            ffn_pieces(w["ffn_w_gate"][0], w["ffn_w_up"][0], w["ffn_w_down"][0])
            for j in range(ODD_PIECES):
                load(N_ODD + j, columns(w["od_w_in"][0], j * SEQ))
            for j in range(WO_PIECES):
                load(N_WO1 + j, columns(w["od_w_out"][0], 0, 2 * j, 2 * j + 2, DM))

            with sp.Fori(0, NE) as item:
                expert_pieces(item, item)
            sp.wait_ge(route_ready, 1)
            n_items = sp.value_load(route_i[0:1, 0:1], min_val=NE, max_val=NITEM)
            for over in range(NOVER):
                expert = sp.value_load(route_i[0:1, 1 + over:2 + over], min_val=0, max_val=NE - 1)
                with sp.If(n_items > NE + over):
                    expert_pieces(NE + over, expert)
            for t in range(T):
                sp.wait_ge(out_ready, t + 1)
                sp.dma_start(out_d[0, t * P:(t + 1) * P, :], hn[:, t, :]).then_inc(out_done, 16)
            sp.wait_ge(out_done, 16 * T)

        @block.tensor
        def _(pe):
            mm = nc.tensor.matmul

            def transposes_of_norm(j):
                for i in range(4):
                    open_bank(pe, ("norm", j, i))
                    for c in range(2):
                        for t in range(T):
                            if i == 0 and c == 0:
                                pe.wait_ge(hn_ready, T * j + t + 1)
                            last = nc.tensor.transpose(
                                ps(("norm", j, i))[:, (c * T + t) * P:(c * T + t + 1) * P],
                                hn[:, t, (2 * i + c) * P:(2 * i + c + 1) * P], ident)
                    last.then_inc(fill_sem(("norm", j, i)), 1)

            def mm3(out, l_high, l_low, r_high, r_low, start, stop):
                mm(out, l_high, r_high, start=start, stop=False)
                mm(out, l_high, r_low, start=False, stop=False)
                return mm(out, l_low, r_high, start=False, stop=stop)

            def ht_ready(j):
                for i in range(4):
                    pe.wait_ge(*drained(("norm", j, i)))

            def project(stage, jobs, base):
                for n, (kind, _, _) in enumerate(jobs):
                    use = (stage, n)
                    pe.wait_ge(*split_done(base + n))
                    open_bank(pe, use)
                    wh, wl = piece(high, base + n, DK), piece(low, base + n, DK)
                    for c in range(2):
                        for k in range(DK):
                            out = ps(use)[:, c * SEQ:(c + 1) * SEQ]
                            half = slice(c * P, (c + 1) * P)
                            first, final = k == 0, k == DK - 1
                            if kind == "T":
                                last = mm3(out, wh[:, k, half], wl[:, k, half], ht_h[:, k, :], ht_l[:, k, :], first,
                                           final)
                            else:
                                last = mm3(out, ht_h[:, k, half], ht_l[:, k, half], wh[:, k, :], wl[:, k, :], first,
                                           final)
                    last.then_inc(fill_sem(use), 1)

            def small_projection(use, col, width):
                open_bank(pe, use)
                pe.wait_ge(ws_ready, 1)
                for t in range(T):
                    for k in range(DK):
                        last = mm3(ps(use)[:, t * width:(t + 1) * width], ht_h[:, k, t * P:(t + 1) * P],
                                   ht_l[:, k, t * P:(t + 1) * P], ws_h[:, k, col:col + width],
                                   ws_l[:, k, col:col + width], k == 0, k == DK - 1)
                last.then_inc(fill_sem(use), 1)

            def prefix_sums(use, src, width):
                open_bank(pe, use)
                mm(ps(use)[:, 0:width], u_inc, src[:, 0, :], start=True, stop=True)
                mm(ps(use)[:, width:2 * width], ones, src[:, 0, :], start=True, stop=False)
                mm(ps(use)[:, width:2 * width], u_inc, src[:, 1, :], start=False,
                   stop=True).then_inc(fill_sem(use), 1)

            def output_projection(layer, base):
                for j in range(WO_PIECES):
                    pe.wait_ge(*split_done(base + j))
                    wh, wl = piece(high, base + j, 2), piece(low, base + j, 2)
                    for n in range(4):
                        t, cols = n // 2, slice(n % 2 * 512, n % 2 * 512 + 512)
                        use = ("wout", layer, n)
                        if j == 0:
                            open_bank(pe, use)
                        for k in range(2):
                            last = mm3(ps(use), mix_h[:, 2 * j + k, t * P:(t + 1) * P],
                                       mix_l[:, 2 * j + k, t * P:(t + 1) * P], wh[:, k, cols], wl[:, k, cols],
                                       j == 0 and k == 0, j == WO_PIECES - 1 and k == 1)
                        if j == WO_PIECES - 1:
                            last.then_inc(fill_sem(use), 1)
                        elif n == 3:
                            last.then_inc(wo_piece_used, 1)

            pe.wait_ge(cst_loaded, 16)
            pe.wait_ge(vec_loaded, 16 * 3)
            nc.tensor.transpose(ps("vectors")[:, 0:V_ALL], vec_rows[:, :], ident[0:V_ALL, 0:V_ALL]).then_inc(
                fill_sem("vectors"), 1)

            transposes_of_norm(0)
            ht_ready(0)
            small_projection("fgate", S_F, FOX_H)
            project("even", EVEN_JOBS, 0)
            for n in range(len(EVEN_JOBS) - 4, len(EVEN_JOBS)):
                pe.wait_ge(*drained(("even", n)))
            pe.wait_ge(flf_ready, 1)
            prefix_sums("fcum", flf, FOX_H)
            pe.wait_ge(*drained(("even", 0)))
            pe.wait_ge(pool_w_loaded, 16 * 5)
            for g2 in range(2):
                use = ("pool", g2)
                open_bank(pe, use)
                for g in range(2):
                    grp = 2 * g2 + g
                    o = ps(use)[g * HD:(g + 1) * HD, :]
                    cols = slice(grp * HD, (grp + 1) * HD)
                    mm(o[:, 0:P], pool_a[:, 0, cols], bands[:, 3 * grp, :], start=True, stop=True)
                    mm(o[:, P:2 * P], pool_a[:, 0, cols], bands[:, 3 * grp + 1, :], start=True, stop=False)
                    last = mm(o[:, P:2 * P], pool_a[:, 1, cols], bands[:, 3 * grp + 2, :], start=False, stop=True)
                last.then_inc(fill_sem(use), 1)
                pe.wait_ge(*drained(use))
                use = ("poolmix", g2)
                mm(ps(use)[:, 0:SEQ], pool_w[:, g2, :], pooled[:, g2, :], start=True, stop=True).then_inc(
                    fill_sem(use), 1)

            def values(use, h, v, p0, q01, q1):
                o = ps(use)[(h % 2) * HD:(h % 2 + 1) * HD, 0:SEQ]
                mm(o, v[:, 0, h * HD:(h + 1) * HD], q01, start=True, stop=False)
                return mm(o[:, P:SEQ], v[:, 1, h * HD:(h + 1) * HD], q1, start=False, stop=True)

            for h in range(FOX_H + 2):
                if h < FOX_H:
                    use = ("fox_s", h)
                    rows_h = slice((h % 2) * HD, (h % 2 + 1) * HD)
                    open_bank(pe, use)
                    lf0 = fnlf[:, 0, h:h + 1].to_broadcast([P, P])
                    lf1 = fnlf[:, 1, h:h + 1].to_broadcast([P, P])
                    mm(ps(use)[:, 0:P], fq[rows_h, h // 2, 0:P], fk[rows_h, h // 2, 0:P], start=True, stop=False)
                    mm(ps(use)[:, 0:P], lf0, u_inc, start=False, stop=True)
                    mm(ps(use)[:, P:384], fq[rows_h, h // 2, P:SEQ], fk[rows_h, h // 2, :], start=True, stop=False)
                    mm(ps(use)[:, P:384], lf0, u_inc_ones, start=False, stop=False)
                    mm(ps(use)[:, 2 * P:384], lf1, u_inc, start=False, stop=True).then_inc(fill_sem(use), 1)
                if 1 <= h <= FOX_H:
                    use = ("fox_pt", h - 1)
                    open_bank(pe, use)
                    pe.wait_ge(fprob_ready, h)
                    for b in range(3):
                        last = nc.tensor.transpose(ps(use)[:, b * P:(b + 1) * P],
                                                   fp[:, (h - 1) % 3, b * P:(b + 1) * P], ident)
                    last.then_inc(fill_sem(use), 1)
                if h >= 2:
                    g = h - 2
                    use = ("fox_o", g // 2)
                    if g % 2 == 0:
                        open_bank(pe, use)
                    pe.wait_ge(*drained(("fox_pt", g)))
                    last = values(use, g, fv, 0, fpt[:, g % 4, 0:SEQ], fpt[:, g % 4, SEQ:384])
                    if g % 2 == 1:
                        last.then_inc(fill_sem(use), 1)
            pe.wait_ge(*drained(("poolmix", 1)))
            for g in range(FOX_H // 2 - 2, FOX_H // 2):
                pe.wait_ge(*drained(("fox_o", g)))
            output_projection(0, N_WO0)

            transposes_of_norm(1)
            ht_ready(1)

            def ffn_gate_up(n, kind, c, h):
                g = 0 if kind == "g" else 1
                wh, wl = piece(high, n, DK), piece(low, n, DK)
                for j in (2 * h, 2 * h + 1):
                    use = ("gu", c, j)
                    if g == 0:
                        open_bank(pe, use)
                    cols = slice((j % 2) * P, (j % 2 + 1) * P)
                    for k in range(DK):
                        last = mm3(ps(use)[:, g * SEQ:(g + 1) * SEQ], wh[:, k, cols], wl[:, k, cols], ht_h[:, k, :],
                                   ht_l[:, k, :], k == 0, k == DK - 1)
                    if g:
                        last.then_inc(fill_sem(use), 1)
                return last

            def ffn_down(n, c, h):
                wh, wl = piece(high, n, 2), piece(low, n, 2)
                pe.wait_ge(fact_ready, 4 * c + 2 * h + 2)
                for q in range(4):
                    t, cols = q // 2, slice(q % 2 * 512, q % 2 * 512 + 512)
                    if c == 0 and h == 0:
                        open_bank(pe, ("fdown", q))
                    for k in range(2):
                        a = (c % 2) * 4 + 2 * h + k
                        last = mm3(ps(("fdown", q)), f_act_h[:, a, t * P:(t + 1) * P], f_act_l[:, a, t * P:(t + 1) * P],
                                   wh[:, k, cols], wl[:, k, cols], c == 0 and h == 0 and k == 0,
                                   c == NCH - 1 and h == 1 and k == 1)
                    if c == NCH - 1 and h == 1:
                        last.then_inc(fill_sem(("fdown", q)), 1)
                return last

            for j, key in enumerate(FFN_ORDER):
                kind, c, h = key
                pe.wait_ge(*split_done(N_FFN + j))
                last = ffn_down(N_FFN + j, c, h) if kind == "d" else ffn_gate_up(N_FFN + j, kind, c, h)
                if key in FFN_COUNTED:
                    last.then_inc(ffn_piece_used, 1)

            transposes_of_norm(2)
            ht_ready(2)
            small_projection("mgate", S_M, 2 * ML_H)
            project("odd", ODD_JOBS, N_ODD)
            pe.wait_ge(mlf_ready, 1)
            prefix_sums("mcum", ml_lf, ML_H)
            for h in range(ML_H):
                use = ("mrow", h)
                open_bank(pe, use)
                lf = [ml_lf[:, t, h:h + 1].to_broadcast([P, P]) for t in range(T)]
                li = [mu[:, t, h:h + 1].to_broadcast([P, P]) for t in range(T)]
                mm(ps(use)[:, 0:SEQ], lf[0], u_inc_ones, start=True, stop=False)
                mm(ps(use)[:, P:SEQ], lf[1], u_inc, start=False, stop=True)
                for t in range(T):
                    last = mm(ps(use)[:, SEQ + t * P:SEQ + (t + 1) * P], li[t], ident, start=True, stop=True)
                last.then_inc(fill_sem(use), 1)

            def rows_to_columns():
                open_bank(pe, "mr")
                pe.wait_ge(mr_ready, ML_H)
                for t in range(T):
                    for h in range(ML_H):
                        last = mm(ps("mr")[:, t * ML_H + h:t * ML_H + h + 1], ml_r[0:1, h, t * P:(t + 1) * P],
                                  ones[0:1, 0:1], start=True, stop=True)
                last.then_inc(fill_sem("mr"), 1)

            for n in range(6):
                pe.wait_ge(*drained(("odd", n)))
            for h in range(SB_H + 2):
                if h < SB_H:
                    use = ("sb_z", h)
                    rows_h = slice((h % 2) * HD, (h % 2 + 1) * HD)
                    open_bank(pe, use)
                    mm(ps(use)[:, 0:SEQ], sk[rows_h, h // 2, 0:P], sq[rows_h, h // 2, :], start=True, stop=True)
                    mm(ps(use)[:, SEQ:384], sk[rows_h, h // 2, P:SEQ], sq[rows_h, h // 2, P:SEQ], start=True,
                       stop=True).then_inc(fill_sem(use), 1)
                if 1 <= h <= SB_H:
                    use = ("sb_lat", h - 1)
                    sp_h = sb_sp[:, (h - 1) % 3, :]
                    open_bank(pe, use)
                    pe.wait_ge(sbsp_masked, h)
                    mm(ps(use)[:, 0:SEQ], l_str, sp_h[:, 0:SEQ], start=True, stop=False)
                    mm(ps(use)[:, P:SEQ], ones, sp_h[:, SEQ:384], start=False, stop=True)
                    mm(ps(use)[:, SEQ:384], l_str, sp_h[:, SEQ:384], start=True, stop=True).then_inc(
                        fill_sem(use), 1)
                if h >= 2:
                    g = h - 2
                    use = ("sb_o", g // 2)
                    if g % 2 == 0:
                        open_bank(pe, use)
                    pe.wait_ge(sbw_masked, g + 1)
                    last = values(use, g, sv, 0, sb_w[:, g % 4, 0:SEQ], sb_w[:, g % 4, SEQ:384])
                    if g % 2 == 1:
                        last.then_inc(fill_sem(use), 1)
                if h == 1:
                    rows_to_columns()

            pe.wait_ge(conv_silu, 2)
            for n in range(10, 12):
                pe.wait_ge(*drained(("odd", n)))
            pe.wait_ge(mv_ones, 1)
            for h in range(ML_H + 1):
                if h < ML_H:
                    use = ("ml_s", h)
                    open_bank(pe, use)
                    mm(ps(use)[:, 0:SEQ], mqk[:, 4 + h, 0:P], mqk[:, h, :], start=True, stop=True)
                    mm(ps(use)[:, SEQ:384], mqk[:, 4 + h, P:SEQ], mqk[:, h, P:SEQ], start=True, stop=True).then_inc(
                        fill_sem(use), 1)
                if h:
                    g = h - 1
                    use = ("ml_n", g)
                    open_bank(pe, use)
                    pe.wait_ge(mw_masked, g + 1)
                    o = ps(use)[:, 0:2 * 129].rearrange("p (t d) -> p t d", t=T)
                    wt = ml_w[:, g % 4, :]
                    mm(o[:, 0, :], wt[:, 0:P], mv[:, g, :], start=True, stop=True)
                    mm(o[:, 1, :], wt[:, P:SEQ], mv[:, g, :], start=True, stop=False)
                    mm(o[:, 1, :], wt[:, SEQ:384], mv[:, ML_H + g, :], start=False, stop=True).then_inc(
                        fill_sem(use), 1)
            for h in range(ML_H):
                use = ("ml_t", h)
                open_bank(pe, use)
                for t in range(T):
                    pe.wait_ge(md_ready, t + 1)
                    last = nc.tensor.transpose(ps(use)[:, t * P:(t + 1) * P], ml_h[:, t, h * P:(h + 1) * P], ident)
                last.then_inc(fill_sem(use), 1)
            for g in range(SB_H // 2 - 2, SB_H // 2):
                pe.wait_ge(*drained(("sb_o", g)))
            for h in range(ML_H - 2, ML_H):
                pe.wait_ge(*drained(("ml_t", h)))
            output_projection(1, N_WO1)

            transposes_of_norm(3)
            ht_ready(3)
            small_projection("router", S_R, NE)
            pe.wait_ge(rsel_ready, 1)
            open_bank(pe, "rank")
            rk = ps("rank")
            mm(rk[:, 0:NE], u_inc, r_sel[:, 0, :], start=True, stop=True)
            mm(rk[:, NE:2 * NE], ones, r_sel[:, 0, :], start=True, stop=False)
            mm(rk[:, NE:2 * NE], u_inc, r_sel[:, 1, :], start=False, stop=True)
            mm(rk[:, 2 * NE:3 * NE], ones, r_sel[:, 0, :], start=True, stop=False)
            mm(rk[:, 2 * NE:3 * NE], ones, r_sel[:, 1, :], start=False, stop=True).then_inc(fill_sem("rank"), 1)

            def act_transposes(c, item):
                use = ("mt", c)
                open_bank(pe, use, item)
                pe.wait_ge(*drained(("mu", c), item))
                for j in range(4):
                    last = nc.tensor.transpose(ps(use)[:, j * P:(j + 1) * P], m_act[:, c % 2, j * P:(j + 1) * P],
                                               ident)
                last.then_inc(fill_sem(use), 1)

            def expert_gate_up(n, kind, c, h, item):
                use = ("m" + kind, c)
                if h == 0:
                    open_bank(pe, use, item)
                wh, wl = piece(high, n, 4), piece(low, n, 4)
                for k in range(4):
                    last = mm3(ps(use), xg_h[:, 4 * h + k, :], xg_l[:, 4 * h + k, :], wh[:, k, :], wl[:, k, :],
                               h == 0 and k == 0, h == 1 and k == 3)
                if h:
                    last.then_inc(fill_sem(use), 1)
                return last

            def expert_down(n, c, h, item):
                pe.wait_ge(*drained(("mt", c), item))
                wh, wl = piece(high, n, 2), piece(low, n, 2)
                for nh in range(2):
                    use, cols = ("my", nh), slice(nh * 512, (nh + 1) * 512)
                    if c == 0 and h == 0:
                        open_bank(pe, use, item)
                    for k in range(2):
                        a = (c % 2) * 4 + 2 * h + k
                        last = mm3(ps(use), m_act_h[:, a, :], m_act_l[:, a, :], wh[:, k, cols], wl[:, k, cols],
                                   c == 0 and h == 0 and k == 0, c == NCH - 1 and h == 1 and k == 1)
                    if c == NCH - 1 and h == 1:
                        last.then_inc(fill_sem(use), 1)
                return last

            def expert_item(item):
                pe.wait_ge(sel_ready, item + 1)
                for half in range(2):
                    use = ("gather", half)
                    open_bank(pe, use, item)
                    for k in range(4):
                        for t in range(T):
                            last = mm(ps(use)[:, k * P:(k + 1) * P],
                                      hn[:, t, (half * 4 + k) * P:(half * 4 + k + 1) * P], sel[:, t, :],
                                      start=t == 0, stop=t == T - 1)
                    last.then_inc(fill_sem(use), 1)
                open_bank(pe, "sgt", item)
                for t in range(T):
                    last = nc.tensor.transpose(ps("sgt")[:, t * P:(t + 1) * P], sel_g[:, t, :], ident)
                last.then_inc(fill_sem("sgt"), 1)
                for half in range(2):
                    pe.wait_ge(*drained(("gather", half), item))
                for j, key in enumerate(EXPERT_ORDER):
                    kind, c, h = key
                    if key == ("u", c, 0) and c:
                        act_transposes(c - 1, item)
                    if key == ("d", NCH - 1, 0):
                        act_transposes(NCH - 1, item)
                    pe.wait_ge(*split_done(N_MOE + j, item))
                    if kind == "d":
                        last = expert_down(N_MOE + j, c, h, item)
                    else:
                        last = expert_gate_up(N_MOE + j, kind, c, h, item)
                    if key in EXPERT_COUNTED:
                        last.then_inc(expert_piece_used, 1)
                for n in range(4):
                    t, nh = n // 2, n % 2
                    use = ("mc", n)
                    open_bank(pe, use, item)
                    pe.wait_ge(*drained(("my", nh), item))
                    mm(ps(use), sgt[:, t, :], y_e[:, nh, :], start=True, stop=True).then_inc(fill_sem(use), 1)

            with pe.Fori(0, NE) as item:
                expert_item(item)
            pe.wait_ge(route_ready, 1)
            n_items = pe.value_load(route_i[0:1, 0:1], min_val=NE, max_val=NITEM)
            with pe.Fori(NE, NITEM) as item:
                with pe.If(n_items > item):
                    expert_item(item)

        @block.scalar
        def _(act):
            fn = nc.scalar.activation
            steps = Steps(act, act_step)

            def as_rows(v):
                return v.rearrange("(k p) -> k p", p=P)

            for row, src in ((V_CONV, w["od_conv_w"][0].rearrange("t (k p) -> (t k) p", p=P)),
                             (V_POOL, as_rows(w["ev_pool_scale"][0])), (V_HEAD, w["od_head_norm_g"][0])):
                act.dma_start(vec_rows[row:row + src.shape[0], :], src).then_inc(vec_loaded, 16)
            act.dma_start(b_fgate[:, :], w["ev_b_forget"][0].partition_broadcast(P)).then_inc(bias_loaded, 16)
            act.dma_start(b_mgate[:, 0:ML_H], w["od_b_igate"][0].partition_broadcast(P)).then_inc(bias_loaded, 16)
            act.dma_start(b_mgate[:, ML_H:], w["od_b_fgate"][0].partition_broadcast(P)).then_inc(bias_loaded, 16)
            act.dma_start(bands, cst_d[:, C_BAND:C_ALL].rearrange("p (b c) -> p b c", c=P)
                          ).then_inc(pool_w_loaded, 16)
            act.wait_ge(pool_w_zero, 1)
            for g in range(4):
                half = slice((g % 2) * HD, (g % 2 + 1) * HD)
                act.dma_start(pool_w[half, g // 2, half], w["ev_pool_w"][0, g]).then_inc(pool_w_loaded, 16)

            def high_parts(first, count=1):
                for n in range(first, first + count):
                    make_high(act, n)

            def mix_high_part(chunk, use, scale=1.0):
                act.wait_ge(*filled(use))
                fn(mix_h[:, chunk, :], ps(use)[:, 0:SEQ], ACT.Copy, scale=scale).then_inc(mix_high, 1)

            def squares(j):
                for t in range(T):
                    fn(hn[:, t, :], x[:, t, :], ACT.Square, accum_out=ssq[:, j, t:t + 1]).then_inc(ssq_ready, 1)
                act.wait_ge(inv_ready, j + 1)
                fn(rstd[:, j, :], inv_ms[:, j, :], ACT.Sqrt).then_inc(rstd_ready, 1)

            def norm_banks(j):
                for i in range(4):
                    act.wait_ge(*filled(("norm", j, i)))
                    fn(ht_h[:, 2 * i:2 * i + 2, :], ps(("norm", j, i)).rearrange("p (k c) -> p k c", k=2),
                       ACT.Copy).then_inc(ht_high, 1)

            def log_of_1_plus_exp(v, ready, n, out_sem):
                act.wait_ge(ready, n)
                steps.done(fn(v, v, ACT.Exp))
                fn(v, v, ACT.Ln, bias=1.0).then_inc(out_sem, 1)

            act.wait_ge(x_loaded, 32)
            squares(0)
            act.wait_ge(gate_w_loaded, 48)
            fn(ws_h[:, :, :], w_small[:, :, :], ACT.Copy).then_inc(ws_high, 1)
            high_parts(0)
            norm_banks(0)
            high_parts(1, 2)
            log_of_1_plus_exp(fe, fu_ready, 1, fln_ready)
            for n in range(len(EVEN_JOBS)):
                if n % 2:
                    act.wait_ge(*filled(("even", n)))
                    dst, scale, shape = job_target(EVEN_JOBS[n])
                    fn(dst, shape(ps(("even", n))), ACT.Copy, scale=scale).then_inc(drain_sem(("even", n)), 1)
                high_parts(n + SPLITS)
            for h in range(FOX_H + 2):
                if h < FOX_H:
                    act.wait_ge(fmax_ready, 2 * h + 2)
                    fn(fp[:, h % 3, 0:P], fp[:, h % 3, 0:P], ACT.Exp, bias=fmax[:, h, 0:1],
                       accum_out=fsum[:, h, 0:1])
                    fn(fp[:, h % 3, P:384], fp[:, h % 3, P:384], ACT.Exp, bias=fmax[:, h, 1:2],
                       accum_out=fsum[:, h, 1:2]).then_inc(fexp_ready, 1)
                if 1 <= h <= FOX_H:
                    use = ("fox_pt", h - 1)
                    act.wait_ge(*filled(use))
                    fn(fpt[:, (h - 1) % 4, :], ps(use)[:, 0:384], ACT.Copy).then_inc(drain_sem(use), 1)
                if h >= 2 and h % 2 == 1:
                    mix_high_part(2 + (h - 2) // 2, ("fox_o", (h - 2) // 2))
            high_parts(N_WO0 + SPLITS)

            high_parts(N_FFN)
            for n in range(4):
                act.wait_ge(*drained(("wout", 0, n)))
            squares(1)
            high_parts(N_FFN + 1)
            norm_banks(1)
            high_parts(N_FFN + 2)

            def silu_pair(c, h):
                for j in (2 * h, 2 * h + 1):
                    act.wait_ge(*filled(("gu", c, j)))
                    if (c, h) != (0, 0):
                        b = (c, j - 2) if h else (c - 1, j + 2)
                        act.wait_ge(*drained(("gu",) + b))
                    fn(f_silu[:, j % 2, :], ps(("gu", c, j))[:, 0:SEQ], ACT.Silu).then_inc(fsilu_ready, 1)

            def act_high_pair(c, h):
                for j in (2 * h, 2 * h + 1):
                    act.wait_ge(*drained(("gu", c, j)))
                    fn(f_act_h[:, (c % 2) * 4 + j, :], f_v[:, j % 2, :], ACT.Copy).then_inc(fact_high, 1)

            for j, (kind, c, h) in enumerate(FFN_ORDER):
                if j >= SPLITS:
                    high_parts(N_FFN + j)
                    kind, c, h = FFN_ORDER[j - SPLITS]
                    if kind == "u":
                        silu_pair(c, h)
                    kind, c, h = FFN_ORDER[j - SPLITS - 1] if j > SPLITS else ("", 0, 0)
                    if kind == "u":
                        act_high_pair(c, h)

            high_parts(N_ODD)
            for n in range(4):
                act.wait_ge(*drained(("fdown", n)))
            squares(2)
            high_parts(N_ODD + 1)
            norm_banks(2)
            high_parts(N_ODD + 2)
            log_of_1_plus_exp(me, mu_ready, 1, mln_ready)
            for n in range(len(ODD_JOBS)):
                if n in ACT_ODD_JOBS:
                    act.wait_ge(*filled(("odd", n)))
                    dst, scale, shape = job_target(ODD_JOBS[n])
                    func = ACT.Sigmoid if ODD_JOBS[n][1] == "mo" else ACT.Copy
                    fn(dst, shape(ps(("odd", n))), func, scale=scale).then_inc(drain_sem(("odd", n)), 1)
                high_parts(N_ODD + n + SPLITS)
            for h in range(SB_H + 2):
                if h < SB_H:
                    use = ("sb_z", h)
                    lb = sb_l[:, h % 2, :]
                    act.wait_ge(*filled(use))
                    if h >= 2:
                        act.wait_ge(*drained(("sb_z", h - 2)))
                    steps.done(fn(lb, ps(use)[:, 0:384], ACT.Abs))
                    steps.done(fn(lb, lb, ACT.Exp, scale=-1.0))
                    fn(lb, lb, ACT.Ln, bias=1.0).then_inc(sbl_ready, 1)
                if 1 <= h <= SB_H:
                    act.wait_ge(*drained(("sb_lat", h - 1)))
                    fn(sb_w[:, (h - 1) % 4, :], sb_w[:, (h - 1) % 4, :], ACT.Exp).then_inc(sbw_exp, 1)
                if h >= 2 and h % 2 == 1:
                    mix_high_part((h - 2) // 2, ("sb_o", (h - 2) // 2))
            act.wait_ge(*drained("mr"))
            fn(m_em, m_em, ACT.Exp).then_inc(mem_ready, 1)
            act.wait_ge(conv_ready, 8)
            for half in range(2):
                v = mqk[:, 4 * half:4 * half + 4, :]
                fn(v, v, ACT.Silu).then_inc(conv_silu, 1)
            for h in range(ML_H + 1):
                if h < ML_H:
                    act.wait_ge(me_in, h + 1)
                    fn(ml_e[:, h % 3, :], ml_e[:, h % 3, :], ACT.Exp).then_inc(me_ready, 1)
                if h:
                    g = h - 1
                    act.wait_ge(*drained(("ml_n", g)))
                    for t in range(T):
                        fn(sb_l[:, t, 0:P], ml_h[:, t, g * P:(g + 1) * P], ACT.Square,
                           accum_out=m_ssq[:, g, t:t + 1]).then_inc(mh_sq, 1)
                        act.wait_ge(mh_sq, 2 * g + t + 1)
            act.wait_ge(mh_inv, 1)
            fn(m_rstd, m_inv, ACT.Sqrt).then_inc(mh_rstd, 1)
            for h in range(ML_H):
                mix_high_part(4 + h, ("ml_t", h), vec[:, V_HEAD + h:V_HEAD + h + 1])
            high_parts(N_WO1 + SPLITS)

            for n in range(4):
                act.wait_ge(*drained(("wout", 1, n)))
            squares(3)
            norm_banks(3)
            act.wait_ge(r_in, 1)
            fn(r_e, r_e, ACT.Exp).then_inc(r_exp, 1)

            def expert_item(item):
                for n in range(SPLITS):
                    if n == 1:
                        for half in range(2):
                            act.wait_ge(*filled(("gather", half), item))
                            fn(xg_h[:, 4 * half:4 * half + 4, :],
                               ps(("gather", half)).rearrange("p (k c) -> p k c", k=4), ACT.Copy).then_inc(
                                   xg_high, 1)
                    make_high(act, N_MOE + n, item)
                act.wait_ge(*filled("sgt", item))
                fn(sgt, ps("sgt")[:, 0:SEQ].rearrange("p (t c) -> p t c", t=T), ACT.Copy).then_inc(
                    drain_sem("sgt"), 1)

                def act_high(c):
                    act.wait_ge(*filled(("mt", c), item))
                    at = (c % 2) * 4
                    fn(m_act_h[:, at:at + 4, :], ps(("mt", c)).rearrange("p (j c) -> p j c", j=4),
                       ACT.Copy).then_inc(mact_high, 1)

                for j in range(SPLITS, FFN_PIECES):
                    make_high(act, N_MOE + j, item)
                    kind, c, h = EXPERT_ORDER[j - SPLITS]
                    if (kind, h) == ("g", 1):
                        if c:
                            act_high(c - 1)
                        b, n = uses[("mu", c)]
                        act.wait_ge(*filled(("mg", c), item))
                        act.wait_ge(s_drained[b], n - 1 + item * bank_fills_per_item[b])
                        fn(m_silu[:, c % 2, :], ps(("mg", c)), ACT.Silu).then_inc(drain_sem(("mg", c)), 1)
                act_high(NCH - 1)
                act.wait_ge(*filled(("my", 0), item))
                fn(y_e[:, 0, :], ps(("my", 0)), ACT.Copy).then_inc(drain_sem(("my", 0)), 1)

            with act.Fori(0, NE) as item:
                expert_item(item)
            act.wait_ge(route_ready, 1)
            n_items = act.value_load(route_i[0:1, 0:1], min_val=NE, max_val=NITEM)
            with act.Fori(NE, NITEM) as item:
                with act.If(n_items > item):
                    expert_item(item)
            act.wait_ge(experts_done, 1)
            squares(4)

        @block.gpsimd
        def _(pool):
            def load_gain(j, src):
                if j:
                    pool.wait_ge(hn_ready, T * j)
                pool.dma_start(g_row[:, :], src.partition_broadcast(P)).then_inc(g_loaded, 16)

            load_gain(0, w["norm_mix_g"][0])
            nc.gpsimd.memset(pool_w, 0.0).then_inc(pool_w_zero, 1)
            load_gain(1, w["norm_ffn_g"][0])
            load_gain(2, w["norm_mix_g"][1])

            def mask_diagonals(v, mask, s):
                blocks = v.rearrange("p (b c) -> p b c", b=3)[:, 0:3:2, :]
                nc.gpsimd.tensor_tensor(blocks, blocks, mask[:, None, :].to_broadcast([P, 2, P]),
                                        ALU.mult).then_inc(s, 1)

            pool.wait_ge(*filled(("odd", 0)))
            nc.gpsimd.memset(mv[:, :, 128:129], 1.0).then_inc(mv_ones, 1)
            for h in range(SB_H + 1):
                if h < SB_H:
                    pool.wait_ge(sbsp_ready, h + 1)
                    mask_diagonals(sb_sp[:, h % 3, :], u_str, sbsp_masked)
                if h:
                    pool.wait_ge(sbw_exp, h)
                    mask_diagonals(sb_w[:, (h - 1) % 4, :], u_str, sbw_masked)
                if h == 0:
                    load_gain(3, w["norm_ffn_g"][1])
            for h in range(ML_H):
                pool.wait_ge(*drained(("ml_s", h)))
                mask_diagonals(ml_w[:, h % 4, :], u_inc, mw_masked)
            load_gain(4, w["norm_final_g"])

        @block.vector
        def _(dve):
            V = nc.vector
            steps = Steps(dve, dve_step)

            def norm_scale(j):
                dve.wait_ge(ssq_ready, T * (j + 1))
                steps.done(V.tensor_scalar(inv_ms[:, j, :], ssq[:, j, :], 1.0 / DM, EPS, ALU.mult, ALU.add))
                V.reciprocal(inv_ms[:, j, :], inv_ms[:, j, :]).then_inc(inv_ready, 1)
                dve.wait_ge(rstd_ready, j + 1)
                dve.wait_ge(g_loaded, 16 * (j + 1))
                if j == 4:
                    return
                for t in range(T):
                    V.scalar_tensor_tensor(hn[:, t, :], x[:, t, :], rstd[:, j, t:t + 1], g_row[:, :], ALU.mult,
                                           ALU.mult).then_inc(hn_ready, 1)

            def norm_banks(j):
                for i in range(4):
                    dve.wait_ge(ht_high, 4 * j + i + 1)
                    V.tensor_tensor(ht_l[:, 2 * i:2 * i + 2, :], ps(("norm", j, i)).rearrange("p (k c) -> p k c", k=2),
                                    ht_h[:, 2 * i:2 * i + 2, :].bitcast(F32), ALU.subtract).then_inc(
                                        drain_sem(("norm", j, i)), 1)

            def low_parts(first, count=1):
                for n in range(first, first + count):
                    make_low(dve, n)

            def mix_low_part(chunk, use, number, scale=1.0):
                if number:
                    dve.wait_ge(mix_high, number)
                V.scalar_tensor_tensor(mix_l[:, chunk, :], ps(use)[:, 0:SEQ], scale, mix_h[:, chunk, :].bitcast(F32),
                                       ALU.mult, ALU.subtract).then_inc(drain_sem(use), 1)

            def drain_job(stage, jobs, n):
                dve.wait_ge(*filled((stage, n)))
                dst, scale, shape = job_target(jobs[n])
                V.tensor_scalar(dst, shape(ps((stage, n))), scale, None, ALU.mult).then_inc(
                    drain_sem((stage, n)), 1)

            def add_to_x(names):
                for n, use in enumerate(names):
                    t, nh = n // 2, n % 2
                    quarter = x[:, t, nh * 512:(nh + 1) * 512]
                    dve.wait_ge(*filled(use))
                    V.tensor_tensor(quarter, quarter, ps(use), ALU.add).then_inc(drain_sem(use), 1)

            def row_bias(b, n):
                return b[:, None, :].to_broadcast([P, T, n])

            dve.wait_ge(x_loaded, 32)
            dve.wait_ge(*filled("vectors"))
            V.tensor_copy(vec[:, :], ps("vectors")[:, 0:V_ALL]).then_inc(drain_sem("vectors"), 1)
            norm_scale(0)
            dve.wait_ge(*drained("vectors"))
            dve.wait_ge(ws_high, 1)
            V.tensor_tensor(ws_l[:, :, :], w_small[:, :, :], ws_h[:, :, :].bitcast(F32), ALU.subtract).then_inc(
                ws_ready, 1)
            norm_banks(0)
            low_parts(0, SPLITS)
            dve.wait_ge(bias_loaded, 48)
            dve.wait_ge(*filled("fgate"))
            V.tensor_tensor(fu, ps("fgate")[:, 0:T * FOX_H].rearrange("p (t h) -> p t h", t=T),
                            row_bias(b_fgate, FOX_H), ALU.add).then_inc(drain_sem("fgate"), 1)
            dve.wait_ge(*drained("fgate"))
            V.scalar_tensor_tensor(fe, fu, -1.0, fu, ALU.mult, ALU.min).then_inc(fu_ready, 1)
            dve.wait_ge(fln_ready, 1)
            steps.done(V.scalar_tensor_tensor(flf, fu, 0.0, fe, ALU.min, ALU.subtract))
            V.tensor_scalar(fnlf, flf, -1.0, None, ALU.mult).then_inc(flf_ready, 1)
            for n in range(len(EVEN_JOBS)):
                if n % 2 == 0:
                    drain_job("even", EVEN_JOBS, n)
                low_parts(n + SPLITS)
            dve.wait_ge(*filled("fcum"))
            V.tensor_copy(fcum, ps("fcum")[:, 0:T * FOX_H].rearrange("p (t h) -> p t h", t=T)).then_inc(
                drain_sem("fcum"), 1)
            dve.wait_ge(*drained("fcum"))
            for g2 in range(2):
                dve.wait_ge(*filled(("pool", g2)))
                V.tensor_copy(pooled[:, g2, :], ps(("pool", g2))[:, 0:SEQ]).then_inc(drain_sem(("pool", g2)), 1)
                dve.wait_ge(*filled(("poolmix", g2)))
                scale = vec[:, V_POOL + g2:V_POOL + g2 + 1]
                steps.done(V.tensor_scalar(mix_h[:, g2, :], ps(("poolmix", g2))[:, 0:SEQ], scale, None, ALU.mult))
                mix_low_part(g2, ("poolmix", g2), 0, scale)
            for h in range(FOX_H + 2):
                if h < FOX_H:
                    use = ("fox_s", h)
                    buf = fp[:, h % 3, :]
                    dve.wait_ge(*filled(use))
                    V.scalar_tensor_tensor(buf[:, 0:P], ps(use)[:, 0:P], fcum[:, 0, h:h + 1],
                                           cst[:, C_CM + P:C_CM + 2 * P], ALU.add, ALU.add)
                    V.scalar_tensor_tensor(buf[:, P:384], ps(use)[:, P:384], fcum[:, 1, h:h + 1],
                                           cst[:, C_CM:C_CM + 2 * P], ALU.add, ALU.add).then_inc(drain_sem(use), 1)
                    dve.wait_ge(*drained(use))
                    V.tensor_reduce(fmax[:, h, 0:1], buf[:, 0:P], AX, ALU.max, negate=True).then_inc(fmax_ready, 1)
                    V.tensor_reduce(fmax[:, h, 1:2], buf[:, P:384], AX, ALU.max, negate=True).then_inc(
                        fmax_ready, 1)
                if 1 <= h <= FOX_H:
                    g = h - 1
                    buf = fp[:, g % 3, :]
                    dve.wait_ge(fexp_ready, h)
                    steps.done(V.reciprocal(finv[:, g, :], fsum[:, g, :]))
                    V.tensor_scalar(buf[:, 0:P], buf[:, 0:P], finv[:, g, 0:1], None, ALU.mult)
                    V.tensor_scalar(buf[:, P:384], buf[:, P:384], finv[:, g, 1:2], None, ALU.mult).then_inc(
                        fprob_ready, 1)
                if h >= 3 and h % 2 == 1:
                    mix_low_part(2 + (h - 3) // 2, ("fox_o", (h - 3) // 2), (h - 3) // 2 + 1)
            low_parts(N_WO0 + SPLITS)
            add_to_x([("wout", 0, n) for n in range(4)])

            low_parts(N_FFN)
            norm_scale(1)
            norm_banks(1)
            low_parts(N_FFN + 1, 2)

            def gated_pair(c, h):
                for j in (2 * h, 2 * h + 1):
                    use = ("gu", c, j)
                    dve.wait_ge(fsilu_ready, 4 * c + j + 1)
                    if (c, h) != (0, 0):
                        dve.wait_ge(fact_ready, 4 * c + j - 1)
                    V.tensor_tensor(f_v[:, j % 2, :], f_silu[:, j % 2, :], ps(use)[:, SEQ:2 * SEQ],
                                    ALU.mult).then_inc(drain_sem(use), 1)

            def act_low_pair(c, h):
                for j in (2 * h, 2 * h + 1):
                    a = (c % 2) * 4 + j
                    dve.wait_ge(fact_high, 4 * c + j + 1)
                    V.tensor_tensor(f_act_l[:, a, :], f_v[:, j % 2, :], f_act_h[:, a, :].bitcast(F32),
                                    ALU.subtract).then_inc(fact_ready, 1)

            for j in range(SPLITS, FFN_PIECES):
                low_parts(N_FFN + j)
                kind, c, h = FFN_ORDER[j - SPLITS]
                if kind == "u":
                    gated_pair(c, h)
                kind, c, h = FFN_ORDER[j - SPLITS - 1] if j > SPLITS else ("", 0, 0)
                if kind == "u":
                    act_low_pair(c, h)
            add_to_x([("fdown", n) for n in range(4)])
            low_parts(N_ODD)

            norm_scale(2)
            norm_banks(2)
            low_parts(N_ODD + 1, 2)
            dve.wait_ge(*filled("mgate"))
            V.tensor_tensor(mu, ps("mgate")[:, 0:T * 2 * ML_H].rearrange("p (t h) -> p t h", t=T),
                            row_bias(b_mgate, 2 * ML_H), ALU.add).then_inc(drain_sem("mgate"), 1)
            dve.wait_ge(*drained("mgate"))
            V.scalar_tensor_tensor(me, mu[:, :, ML_H:], -1.0, mu[:, :, ML_H:], ALU.mult, ALU.min).then_inc(mu_ready, 1)
            dve.wait_ge(mln_ready, 1)
            V.scalar_tensor_tensor(ml_lf, mu[:, :, ML_H:], 0.0, me, ALU.min, ALU.subtract).then_inc(mlf_ready, 1)
            for n in range(len(ODD_JOBS)):
                if n not in ACT_ODD_JOBS:
                    drain_job("odd", ODD_JOBS, n)
                low_parts(N_ODD + n + SPLITS)
            dve.wait_ge(*filled("mcum"))
            V.tensor_copy(m_rn_f, ps("mcum")[:, 0:T * ML_H].rearrange("p (t h) -> p t h", t=T)).then_inc(
                drain_sem("mcum"), 1)
            dve.wait_ge(*drained("mcum"))
            steps.done(V.tensor_tensor(m_an, mu[:, :, 0:ML_H], m_rn_f, ALU.subtract))
            for h in range(ML_H):
                use = ("mrow", h)
                dve.wait_ge(*filled(use))
                steps.done(V.tensor_copy(ml_f[:, 0, :], ps(use)[:, 0:SEQ]))
                V.tensor_tensor(ml_f[:, 1, :], ps(use)[:, SEQ:2 * SEQ], ml_f[:, 0, :], ALU.subtract).then_inc(
                    drain_sem(use), 1)
                dve.wait_ge(*drained(use))
                steps.done(V.tensor_tensor_scan(ml_r[:, h, :], ml_f[:, 1, :], ml_f[:, 1, :], -3e38, ALU.max,
                                                ALU.max))
                V.scalar_tensor_tensor(ml_r[:, h, :], ml_r[:, h, :], -1.0, ml_f[:, 0, :], ALU.mult,
                                       ALU.min).then_inc(mr_ready, 1)
                dve.wait_ge(mr_ready, h + 1)

            def conv_chunk(k):
                src = mq_in[:, k, :] if k < 4 else mk_in[:, k - 4, :]
                dst = mqk[:, k, :]

                def tap(j):
                    return vec[:, V_CONV + 8 * j + k:V_CONV + 8 * j + k + 1]

                n = steps.mark(V.tensor_scalar(dst, src, tap(TAPS - 1), None, ALU.mult))
                for d in range(1, TAPS):
                    steps.wait(n)
                    ins = V.scalar_tensor_tensor(dst[:, d:], src[:, 0:SEQ - d], tap(TAPS - 1 - d), dst[:, d:],
                                                 ALU.mult, ALU.add)
                    if d < TAPS - 1:
                        n = steps.mark(ins)
                    else:
                        ins.then_inc(conv_ready, 1)

            for n in (7, 9):
                dve.wait_ge(*drained(("odd", n)))
            for n in (6, 8):
                dve.wait_ge(*drained(("odd", n)))
            for h in range(SB_H + 2):
                if h < SB_H:
                    use = ("sb_z", h)
                    z = ps(use)[:, 0:384]
                    dve.wait_ge(sbl_ready, h + 1)
                    V.scalar_tensor_tensor(sb_sp[:, h % 3, :], z, 0.0, sb_l[:, h % 2, :], ALU.max,
                                           ALU.add).then_inc(sbsp_ready, 1)
                    V.scalar_tensor_tensor(sb_w[:, h % 4, :], z, 0.0, sb_l[:, h % 2, :], ALU.min,
                                           ALU.subtract).then_inc(drain_sem(use), 1)
                    conv_chunk(h)
                if h == 2:
                    dve.wait_ge(*filled("mr"))
                    V.tensor_tensor(m_em, ps("mr")[:, 0:T * ML_H].rearrange("p (t h) -> p t h", t=T), m_rn_f,
                                    ALU.subtract).then_inc(drain_sem("mr"), 1)
                if 1 <= h <= SB_H:
                    use = ("sb_lat", h - 1)
                    buf = sb_w[:, (h - 1) % 4, :]
                    dve.wait_ge(*drained(("sb_z", h - 1)))
                    dve.wait_ge(*filled(use))
                    V.tensor_tensor(buf, buf, ps(use)[:, 0:384], ALU.subtract).then_inc(drain_sem(use), 1)
                if h >= 3 and h % 2 == 1:
                    mix_low_part((h - 3) // 2, ("sb_o", (h - 3) // 2), FOX_H // 2 + (h - 3) // 2 + 1)

            dve.wait_ge(mem_ready, 1)

            def ml_exponent(h):
                V.tensor_scalar(ml_e[:, h % 3, 0:SEQ], ml_r[:, h, :], m_an[:, 0, h:h + 1], 0.0, ALU.add, ALU.min)
                V.tensor_scalar(ml_e[:, h % 3, SEQ:384], ml_r[:, h, P:SEQ], m_an[:, 1, h:h + 1], 0.0, ALU.add,
                                ALU.min).then_inc(me_in, 1)

            ml_exponent(0)
            for h in range(ML_H + 1):
                if h < ML_H:
                    if h + 1 < ML_H:
                        ml_exponent(h + 1)
                    use = ("ml_s", h)
                    dve.wait_ge(me_ready, h + 1)
                    dve.wait_ge(*filled(use))
                    V.scalar_tensor_tensor(ml_w[:, h % 4, :], ml_e[:, h % 3, :], P ** -0.5, ps(use)[:, 0:384],
                                           ALU.mult, ALU.mult).then_inc(drain_sem(use), 1)
                if h:
                    g = h - 1
                    use = ("ml_n", g)
                    o = ps(use)[:, 0:2 * 129].rearrange("p (t d) -> p t d", t=T)
                    dve.wait_ge(*filled(use))
                    steps.done(V.tensor_copy(m_den[:, g, :], o[:, :, 128]))
                    steps.done(V.scalar_tensor_tensor(m_den[:, g, :], m_den[:, g, :], -1.0, m_den[:, g, :],
                                                      ALU.mult, ALU.max))
                    steps.done(V.tensor_tensor(m_den[:, g, :], m_den[:, g, :], m_em[:, :, g], ALU.max))
                    steps.done(V.reciprocal(m_rden[:, g, :], m_den[:, g, :]))
                    for t in range(T):
                        last = V.tensor_scalar(ml_h[:, t, g * P:(g + 1) * P], o[:, t, 0:P], m_rden[:, g, t:t + 1],
                                               None, ALU.mult)
                    last.then_inc(drain_sem(use), 1)
            dve.wait_ge(mh_sq, T * ML_H)
            steps.done(V.tensor_scalar(m_inv, m_ssq, 1.0 / P, EPS, ALU.mult, ALU.add))
            V.reciprocal(m_inv, m_inv).then_inc(mh_inv, 1)
            dve.wait_ge(mh_rstd, 1)
            for n in (12, 13):
                dve.wait_ge(*drained(("odd", n)))
            for t in range(T):
                heads = ml_h[:, t, :].rearrange("p (h d) -> p h d", h=ML_H)
                steps.done(V.tensor_tensor(heads, heads, m_rstd[:, :, t:t + 1].to_broadcast([P, ML_H, P]),
                                           ALU.mult))
                V.tensor_tensor(ml_h[:, t, :], ml_h[:, t, :], ml_o[:, t, :], ALU.mult).then_inc(md_ready, 1)
            for h in range(ML_H):
                mix_low_part(4 + h, ("ml_t", h), FOX_H // 2 + SB_H // 2 + h + 1, vec[:, V_HEAD + h:V_HEAD + h + 1])
            low_parts(N_WO1 + SPLITS)
            add_to_x([("wout", 1, n) for n in range(4)])

            norm_scale(3)
            norm_banks(3)
            dve.wait_ge(*filled("router"))
            V.tensor_copy(r_log, ps("router")[:, 0:T * NE].rearrange("p (t e) -> p t e", t=T)).then_inc(
                drain_sem("router"), 1)
            dve.wait_ge(*drained("router"))
            steps.done(V.tensor_reduce(r_max, r_log, AX, ALU.max))
            V.tensor_tensor(r_e, r_log, r_max.to_broadcast([P, T, NE]), ALU.subtract).then_inc(r_in, 1)
            for t in range(T):
                other = r_log[:, t, None, :].to_broadcast([P, NE, NE])
                own = r_log[:, t, :, None].to_broadcast([P, NE, NE])
                cmp_t, eq_t = r_cmp[:, t * NE:(t + 1) * NE, :], r_eq[:, t * NE:(t + 1) * NE, :]
                V.tensor_tensor(cmp_t, other, own, ALU.is_gt)
                steps.done(V.tensor_tensor(eq_t, other, own, ALU.is_equal))
                steps.done(V.tensor_tensor(eq_t, eq_t, cst[:, C_TIE:C_TIE + NE * NE].rearrange(
                    "p (a b) -> p a b", a=NE), ALU.mult))
                steps.done(V.tensor_tensor(cmp_t, cmp_t, eq_t, ALU.add))
                steps.done(V.tensor_reduce(r_rank[:, t, :], cmp_t, AX, ALU.add))
            V.tensor_scalar(r_sel, r_rank, 1.5, None, ALU.is_lt).then_inc(rsel_ready, 1)
            dve.wait_ge(rsel_ready, 1)
            dve.wait_ge(r_exp, 1)
            steps.done(V.tensor_tensor(r_e, r_e, r_sel, ALU.mult))
            steps.done(V.tensor_reduce(r_sum, r_e, AX, ALU.add))
            steps.done(V.reciprocal(r_sum, r_sum))
            steps.done(V.tensor_tensor(r_gate, r_e, r_sum.to_broadcast([P, T, NE]), ALU.mult))
            dve.wait_ge(*filled("rank"))
            V.tensor_copy(r_cnt[:, 0, :], ps("rank")[:, 2 * NE:3 * NE])
            V.tensor_tensor(r_pos, ps("rank")[:, 0:T * NE].rearrange("p (t e) -> p t e", t=T), r_sel,
                            ALU.mult).then_inc(drain_sem("rank"), 1)
            dve.wait_ge(*drained("rank"))
            steps.done(V.tensor_scalar(r_pos, r_pos, -1.0, None, ALU.add))
            steps.done(V.tensor_scalar(r_over, r_cnt[:, 0, :], float(P) + 0.5, None, ALU.is_gt))
            steps.done(V.tensor_tensor_scan(r_oc, ones[:, 0:NE], r_over, 0.0, ALU.mult, ALU.add))
            steps.done(V.tensor_scalar(r_eidf[:, 0:1], r_oc[:, NE - 1:NE], float(NE), None, ALU.add))
            steps.done(V.tensor_tensor(r_oc, r_oc, r_over, ALU.subtract))
            for t in range(T):
                V.tensor_copy(pos_i[:, 0:NE, t], r_pos[:, t, :])
                steps.done(V.tensor_copy(gate_i[:, 0:NE, t], r_gate[:, t, :]))
            steps.done(V.tensor_scalar(r_pos, r_pos, -float(P), None, ALU.add))
            for j in range(NOVER):
                steps.done(V.scalar_tensor_tensor(r_tmp[:, 0, :], r_oc, float(j), r_over, ALU.is_equal, ALU.mult))
                pick = r_tmp[:, 0:1, :].to_broadcast([P, T, NE])
                steps.done(V.tensor_tensor(r_tmp[:, 1:3, :], r_pos, pick, ALU.mult))
                steps.done(V.tensor_reduce(pos_i[:, NE + j, :], r_tmp[:, 1:3, :], AX, ALU.add))
                steps.done(V.tensor_tensor(r_tmp[:, 1:3, :], r_gate, pick, ALU.mult))
                steps.done(V.tensor_reduce(gate_i[:, NE + j, :], r_tmp[:, 1:3, :], AX, ALU.add))
                steps.done(V.tensor_tensor(r_tmp[:, 3, :], cst[:, C_EID:C_EID + NE], r_tmp[:, 0, :], ALU.mult))
                steps.done(V.tensor_reduce(r_eidf[:, 1 + j:2 + j], r_tmp[:, 3, :], AX, ALU.add))
            V.tensor_copy(route_i[0:1, 0:1 + NOVER], r_eidf[0:1, 0:1 + NOVER]).then_inc(route_ready, 1)

            def expert_item(item):
                for t in range(T):
                    pos = pos_i[:, bass.ds(item, 1), t]
                    V.tensor_scalar(sel[:, t, :], cst[:, C_IOTA:C_IOTA + P], pos, None, ALU.is_equal)
                    last = V.tensor_scalar(sel_g[:, t, :], cst[:, C_IOTA:C_IOTA + P], pos,
                                           gate_i[:, bass.ds(item, 1), t], ALU.is_equal, ALU.mult)
                last.then_inc(sel_ready, 1)
                for n in range(SPLITS):
                    if n == 1:
                        for half in range(2):
                            use = ("gather", half)
                            dve.wait_ge(xg_high, 2 * item + half + 1)
                            V.tensor_tensor(xg_l[:, 4 * half:4 * half + 4, :],
                                            ps(use).rearrange("p (k c) -> p k c", k=4),
                                            xg_h[:, 4 * half:4 * half + 4, :].bitcast(F32), ALU.subtract).then_inc(
                                                drain_sem(use), 1)
                    make_low(dve, N_MOE + n, item)

                def act_low(c):
                    at = (c % 2) * 4
                    dve.wait_ge(mact_high, NCH * item + c + 1)
                    V.tensor_tensor(m_act_l[:, at:at + 4, :], ps(("mt", c)).rearrange("p (j c) -> p j c", j=4),
                                    m_act_h[:, at:at + 4, :].bitcast(F32), ALU.subtract).then_inc(
                                        drain_sem(("mt", c)), 1)

                for j in range(SPLITS, FFN_PIECES):
                    make_low(dve, N_MOE + j, item)
                    kind, c, h = EXPERT_ORDER[j - SPLITS]
                    if (kind, h) == ("g", 1) and c:
                        act_low(c - 1)
                    if (kind, h) == ("u", 1):
                        dve.wait_ge(*drained(("mg", c), item))
                        dve.wait_ge(*filled(("mu", c), item))
                        V.tensor_tensor(m_act[:, c % 2, :], m_silu[:, c % 2, :], ps(("mu", c)), ALU.mult).then_inc(
                            drain_sem(("mu", c)), 1)
                act_low(NCH - 1)
                dve.wait_ge(*filled(("my", 1), item))
                V.tensor_copy(y_e[:, 1, :], ps(("my", 1))).then_inc(drain_sem(("my", 1)), 1)
                for n in range(4):
                    t, nh = n // 2, n % 2
                    use = ("mc", n)
                    quarter = x[:, t, nh * 512:(nh + 1) * 512]
                    dve.wait_ge(*filled(use, item))
                    V.tensor_tensor(quarter, quarter, ps(use), ALU.add).then_inc(drain_sem(use), 1)

            dve.wait_ge(route_ready, 1)
            with dve.Fori(0, NE) as item:
                expert_item(item)
            n_items = dve.value_load(route_i[0:1, 0:1], min_val=NE, max_val=NITEM)
            with dve.Fori(NE, NITEM) as item:
                with dve.If(n_items > item):
                    expert_item(item)
            V.memset(r_max, 0.0).then_inc(experts_done, 1)

            norm_scale(4)
            for t in range(T):
                V.scalar_tensor_tensor(hn[:, t, :], x[:, t, :], rstd[:, 4, t:t + 1], g_row[:, :], ALU.mult,
                                       ALU.mult).then_inc(out_ready, 1)


_WEIGHTS = ["norm_mix_g", "norm_ffn_g", "norm_final_g", "ev_w_in", "ev_b_forget", "ev_pool_w", "ev_pool_scale",
            "ev_w_out", "ffn_w_gate", "ffn_w_up", "ffn_w_down", "od_w_in", "od_b_igate", "od_b_fgate", "od_conv_w",
            "od_head_norm_g", "od_w_out", "moe_w_router", "moe_w_gate", "moe_w_up", "moe_w_down"]


def kernel(**inputs):
    import concourse.bacc as _bacc
    from concourse.bass_utils import run_bass_kernel_spmd as _run

    nc = _bacc.Bacc("TRN2", target_bir_lowering=False, num_devices=1)
    arrays, aps = {}, {}
    for name in ["x"] + _WEIGHTS:
        a = np.ascontiguousarray(inputs[name])
        arrays[f"in_{name}"] = a
        aps[name] = nc.dram_tensor(f"in_{name}", a.shape, mybir.dt.from_np(a.dtype), kind="ExternalInput").ap()
    arrays["in_constants"] = constants()
    cst_d = nc.dram_tensor("in_constants", (P, C_ALL), F32, kind="ExternalInput").ap()
    out_d = nc.dram_tensor("out_trunk", (1, SEQ, DM), F32, kind="ExternalOutput").ap()
    build_trunk(nc, aps["x"], aps, cst_d, out_d)
    r = _run(nc, [arrays], core_ids=[0])
    return r.results[0]["out_trunk"]
```

```python
from contextlib import ExitStack

import numpy as np
import concourse.bass as bass
from concourse import mybir

F32 = mybir.dt.float32
F32R = mybir.dt.float32r
I32 = mybir.dt.int32
ALU = mybir.AluOpType
ACT = mybir.ActivationFunctionType
AX = mybir.AxisListType.X

P = 128
SEQ = 256
T = SEQ // P
DM = 1024
DK = DM // P
EPS = 1e-6
POOL_WINDOWS = (2, 4, 8, 16)
POOL_W = DM // 4
HD = 64
FOX_H = (DM - POOL_W) // HD
SB_H = 8
ML_H = 4
TAPS = 4
D_FF = 7 * DM // 2
FC = 512
NCH = D_FF // FC
NE = 8
NOVER = (2 * SEQ) // (P + 1)
NITEM = NE + NOVER
NEXTRA = NOVER + 1
RAW = 6
SPLITS = 3
PIECE = DM * SEQ // P
EVEN_PIECES = 10
ODD_PIECES = 14
WO_PIECES = 4
FFN_PIECES = 6 * NCH
N_WO0 = EVEN_PIECES
N_FFN = N_WO0 + WO_PIECES
N_ODD = N_FFN + FFN_PIECES
N_WO1 = N_ODD + ODD_PIECES
N_MOE = N_WO1 + WO_PIECES
assert FFN_PIECES % RAW == 0 and FFN_PIECES % SPLITS == 0
MASKED = -1e30
ARENA = 12288

C_ID = 0
C_UINC = 128
C_ONES = 256
C_USTR = 384
C_LSTR = 512
C_CM = 640
C_IOTA = 896
C_TIE = 1024
C_EID = C_TIE + 64
C_SLOTNO = C_EID + 8
C_BAND = C_SLOTNO + 16
C_ALL = C_BAND + len(POOL_WINDOWS) * 3 * P

V_CONV = 0
V_POOL = 32
V_HEAD = 34
V_ALL = 38

S_F = 0
S_M = FOX_H
S_R = FOX_H + 2 * ML_H
S_ALL = S_R + NE


def constants():
    c = np.zeros((P, C_ALL), np.float32)
    i, o = np.meshgrid(np.arange(P), np.arange(P), indexing="ij")
    c[:, C_ID:C_ID + P] = i == o
    c[:, C_UINC:C_UINC + P] = i <= o
    c[:, C_ONES:C_ONES + P] = 1
    c[:, C_USTR:C_USTR + P] = i < o
    c[:, C_LSTR:C_LSTR + P] = i > o
    c[:, C_CM + P:C_CM + 2 * P] = np.where(o <= i, 0.0, MASKED)
    c[:, C_IOTA:C_IOTA + P] = o
    e, f = np.meshgrid(np.arange(NE), np.arange(NE), indexing="ij")
    c[:, C_TIE:C_TIE + NE * NE] = (f < e).reshape(-1)
    c[:, C_EID:C_EID + NE] = np.arange(NE)
    c[:, C_SLOTNO:C_SLOTNO + NEXTRA] = np.arange(NEXTRA)
    ti, to = np.meshgrid(np.arange(SEQ), np.arange(SEQ), indexing="ij")
    for g, w in enumerate(POOL_WINDOWS):
        band = np.where((ti <= to) & (ti > to - w), 1.0 / np.minimum(to + 1, w), 0.0) - (ti == to)
        for b, blk in enumerate((band[:P, :P], band[:P, P:], band[P:, P:])):
            at = C_BAND + (3 * g + b) * P
            c[:, at:at + P] = blk
    return c


class Banks:

    def __init__(self):
        self.count = [0] * 8
        self.uses = {}

    def fill(self, name, bank):
        self.count[bank] += 1
        self.uses[name] = (bank, self.count[bank])


EVEN_COLUMNS = ([("N", "a", 0)] + [("T", "q", c) for c in (0, 2, 4)] + [("T", "k", c) for c in (0, 2, 4)]
                + [("N", "v", c) for c in range(3)])
ODD_COLUMNS = ([("T", "sq", c) for c in (0, 2)] + [("T", "sk", c) for c in (0, 2)] + [("N", "sv", c) for c in (0, 1)]
            + [("T", "mq", c) for c in (0, 2)] + [("T", "mk", c) for c in (0, 2)] + [("N", "mv", c) for c in (0, 1)]
            + [("N", "mo", c) for c in (0, 1)])
EVEN_JOBS = [EVEN_COLUMNS[c] for c in (1, 4, 7, 2, 5, 8, 3, 6, 9, 0)]
ODD_JOBS = [ODD_COLUMNS[c] for c in (0, 2, 4, 1, 3, 5) + tuple(range(6, ODD_PIECES))]
EVEN_SUMS_AFTER = 1
FOX_AFTER = 3
POOL_STEP = len(EVEN_JOBS) - FOX_AFTER
WOUT_STEPS = {FOX_H - 2: 0, FOX_H - 1: 1, FOX_H: 2}
ODD_SUMS_AFTER = 1
ODD_ROWS_AFTER = {1: (0, 1), 2: (2, 3)}
SB_AFTER = 3
ROWS_TURNED_AT = 5
CONV_AFTER = 8
assert SB_AFTER + SB_H + 2 <= len(ODD_JOBS) and ML_H == 4
assert len(EVEN_JOBS) == EVEN_PIECES and len(ODD_JOBS) == ODD_PIECES

FFN_ORDER = []
EXPERT_ORDER = []
for _c in range(NCH + 1):
    if _c < NCH:
        FFN_ORDER += [("g", _c, 0), ("u", _c, 0), ("g", _c, 1), ("u", _c, 1)]
        EXPERT_ORDER += ([("g", _c, 0), ("g", _c, 1), ("u", _c, 0), ("u", _c, 1)] if _c else
                         [("g", _c, 0), ("u", _c, 0), ("g", _c, 1), ("u", _c, 1)])
    if _c:
        FFN_ORDER += [("d", _c - 1, 0), ("d", _c - 1, 1)]
        EXPERT_ORDER += [("d", _c - 1, 0), ("d", _c - 1, 1)]


def ends_a_fill(key, experts):
    kind, c, h = key
    if kind == "d":
        return (("my", 1) if experts else ("fdown", 3)) if (c, h) == (NCH - 1, 1) else None
    if experts:
        return ("m" + kind, c) if h else None
    return ("gu", c, 2 * h + 1) if kind == "u" else None


FFN_COUNTED = [k for k in FFN_ORDER if ends_a_fill(k, False) is None]
EXPERT_COUNTED = [k for k in EXPERT_ORDER if ends_a_fill(k, True) is None]


def plan_banks():
    banks = Banks()

    def norm(j):
        for i in range(4):
            banks.fill(("norm", j, i), i)

    banks.fill("vectors", 7)
    norm(0)
    banks.fill("fgate_rows", 5)
    banks.fill("fgate", 4)
    for n in range(FOX_AFTER + FOX_H + 2):
        h = n - FOX_AFTER
        if n < len(EVEN_JOBS):
            banks.fill(("even", n), 6 + n % 2)
        if n == EVEN_SUMS_AFTER:
            banks.fill("fcum", 2)
        if h in WOUT_STEPS and WOUT_STEPS[h] == 0:
            banks.fill(("wout", 0, 0), 6)
            banks.fill(("wout", 0, 1), 7)
        if 0 <= h < FOX_H:
            banks.fill(("fox_s", h), h % 2)
        if 1 <= h <= FOX_H:
            banks.fill(("fox_pt", h - 1), 2 + (h - 1) % 2)
        if h >= 2 and h % 2 == 1:
            banks.fill(("fox_o", (h - 2) // 2), 4 + (h - 2) // 2 % 2)
        for g2 in range(2):
            if h == POOL_STEP + g2:
                banks.fill(("pool", g2), 6 + g2)
            if h == POOL_STEP + g2 + 1:
                banks.fill(("poolmix", g2), 6 + g2)
    banks.fill(("wout", 0, 2), 0)
    banks.fill(("wout", 0, 3), 1)
    norm(1)
    for c in range(NCH):
        for j in range(4):
            banks.fill(("gu", c, j), j)
    for n in range(4):
        banks.fill(("fdown", n), 4 + n)
    norm(2)
    banks.fill("mgate_rows", 5)
    banks.fill("mgate", 4)
    for n in range(len(ODD_JOBS)):
        banks.fill(("odd", n), 6 + n % 2)
        if n == ODD_SUMS_AFTER:
            banks.fill("mcum", 2)
        if n in ODD_ROWS_AFTER:
            for h in ODD_ROWS_AFTER[n]:
                banks.fill(("mrow", h), 4 + h % 2)
        h = n - SB_AFTER
        if 0 <= h < SB_H:
            banks.fill(("sb_z", h), h % 2)
        if 1 <= h <= SB_H:
            banks.fill(("sb_lat", h - 1), 2 + (h - 1) % 2)
        if h >= 2 and h % 2 == 1 and h < SB_H + 2:
            banks.fill(("sb_o", (h - 2) // 2), 4 + (h - 2) // 2 % 2)
        if h == ROWS_TURNED_AT:
            banks.fill("mr", 3)
    for n in range(4):
        banks.fill(("wout", 1, n), 4 + n)
    for h in range(ML_H + 1):
        if h < ML_H:
            banks.fill(("ml_s", h), h % 2)
        if h:
            banks.fill(("ml_n", h - 1), 2 + (h - 1) % 2)
    for h in range(ML_H):
        banks.fill(("ml_t", h), h % 2)
    norm(3)
    banks.fill("router_rows", 5)
    banks.fill("router", 4)
    banks.fill("rank", 5)
    for half in range(2):
        banks.fill(("gather0", half), 1 + 2 * half)
    before = list(banks.count)
    banks.fill("sgt", 7)
    for c in range(NCH + 1):
        if c < NCH:
            banks.fill(("mg", c), c % 2)
            banks.fill(("mu", c), 2 + c % 2)
        if c:
            banks.fill(("mt", c - 1), 6)
        if c == NCH - 1:
            for half in range(2):
                banks.fill(("gather", half), 1 + 2 * half)
    for n in range(2):
        banks.fill(("my", n), 4 + n)
    for n in range(4):
        banks.fill(("mc", n), 6 + n % 2)
    per_item = [a - b for a, b in zip(banks.count, before)]
    return banks.uses, per_item


def build_trunk(nc, x_d, w, cst_d, out_d):
    uses, bank_fills_per_item = plan_banks()

    with ExitStack() as ctx:
        def sb(name, shape, dt=F32):
            return ctx.enter_context(nc.sbuf_tensor(name, shape, dt))

        def sem(name):
            return ctx.enter_context(nc.semaphore(name))

        bank = [ctx.enter_context(nc.psum_tensor(f"bank{b}", [P, 512], F32)) for b in range(8)]
        s_filled = [sem(f"filled{b}") for b in range(8)]
        s_drained = [sem(f"drained{b}") for b in range(8)]
        raw_full = [sem(f"raw_full{r}") for r in range(RAW)]
        high_ready = sem("high_ready")
        split_ready = sem("split_ready")
        wo_piece_used = sem("wo_piece_used")
        ffn_piece_used = sem("ffn_piece_used")
        expert_piece_used = sem("expert_piece_used")

        def ps(use):
            return bank[uses[use][0]][:, :]

        def filled(use, item=0):
            b, n = uses[use]
            return s_filled[b], n + item * bank_fills_per_item[b]

        def drained(use, item=0):
            b, n = uses[use]
            return s_drained[b], n + item * bank_fills_per_item[b]

        def fill_sem(use):
            return s_filled[uses[use][0]]

        def drain_sem(use):
            return s_drained[uses[use][0]]

        def open_bank(pe, use, item=0):
            b, n = uses[use]
            if n > 1:
                pe.wait_ge(s_drained[b], n - 1 + item * bank_fills_per_item[b])

        raw = sb("raw", [P, RAW, PIECE])
        high = sb("high", [P, SPLITS, PIECE], F32R)
        low = sb("low", [P, SPLITS, PIECE], F32R)
        x = sb("x", [P, T, DM])
        hn = sb("hn", [P, T, DM])
        ht_h = sb("ht_h", [P, DK, SEQ], F32R)
        ht_l = sb("ht_l", [P, DK, SEQ], F32R)
        mix_h = sb("mix_h", [P, DK, SEQ], F32R)
        mix_h_at = nc.sbuf_base - DK * SEQ * 4
        mix_l = sb("mix_l", [P, DK, SEQ], F32R)
        cst = sb("cst", [P, C_BAND])
        g_row = sb("g_row", [P, DM])
        vec_rows = sb("vec_rows", [V_ALL, P])
        vec = sb("vec", [P, V_ALL])
        few_rows = sb("few_rows", [16, SEQ])
        w_small = sb("w_small", [P, DK, S_ALL])
        ws_h = sb("ws_h", [P, DK, S_ALL], F32R)
        ws_l = sb("ws_l", [P, DK, S_ALL], F32R)
        b_fgate = sb("b_fgate", [P, FOX_H])
        b_mgate = sb("b_mgate", [P, 2 * ML_H])
        ssq = sb("ssq", [P, 5, T])
        inv_ms = sb("inv_ms", [P, 5, T])
        rstd = sb("rstd", [P, 5, T])
        route_i = sb("route_i", [1, 16], I32)
        s_cols = sb("s_cols", [P, 720])
        arena = sb("arena", [P, ARENA])
        arena_at = nc.sbuf_base - ARENA * 4

        f_act_h = nc.alloc_sbuf_tensor_at("f_act_h", [P, 8, SEQ], F32R, offset=arena_at)
        f_act_l = nc.alloc_sbuf_tensor_at("f_act_l", [P, 8, SEQ], F32R, offset=arena_at + 8 * SEQ * 4)
        xg_h = nc.alloc_sbuf_tensor_at("xg_h", [P, DK, P], F32R, offset=arena_at)
        xg_l = nc.alloc_sbuf_tensor_at("xg_l", [P, DK, P], F32R, offset=arena_at + DK * P * 4)
        m_act_h = nc.alloc_sbuf_tensor_at("m_act_h", [P, 8, P], F32R, offset=arena_at + 2 * DK * P * 4)
        m_act_l = nc.alloc_sbuf_tensor_at("m_act_l", [P, 8, P], F32R, offset=arena_at + 3 * DK * P * 4)
        mq_in = nc.alloc_sbuf_tensor_at("mq_in", [P, 4, SEQ], F32, offset=mix_h_at + 4 * SEQ * 4)

        taken = [0, 0]

        def view(region, at, *shape):
            size = int(np.prod(shape))
            v = region[:, at:at + size]
            if len(shape) == 2:
                return v.rearrange("p (a b) -> p a b", a=shape[0])
            if len(shape) == 3:
                return v.rearrange("p (a b c) -> p a b c", a=shape[0], b=shape[1])
            return v

        def layout(region, *parts):
            at, out = 0, []
            for shape in parts:
                out.append(view(region, at, *shape))
                at += int(np.prod(shape))
            taken[0] = max(taken[0], at)
            return out

        bands, pool_a, fq, fk, fv, fp, fpt, pooled, pool_w = layout(
            arena, (len(POOL_WINDOWS) * 3, P), (T, POOL_W), (6, SEQ), (6, SEQ), (T, FOX_H * HD), (3, 384), (4, 384),
            (2, SEQ), (2, P))
        _, f_silu, f_v = layout(arena, (16, SEQ), (2, SEQ), (2, SEQ))
        sq, sk, sv, mk_in, mqk, mv, sb_l, sb_sp, sb_w, ml_r, ml_f = layout(
            arena, (4, SEQ), (4, SEQ), (T, 512), (4, SEQ), (8, SEQ), (T * ML_H, 129), (2, 384), (3, 384), (4, 384),
            (ML_H, SEQ), (2, SEQ))
        assert taken[0] <= ARENA
        ml_e = sb_sp
        ml_w = sb_w
        ml_h = hn[:, :, 0:512]
        ml_o = hn[:, :, 512:1024]
        _, sel, sel_g, sgt, m_silu, m_act, y_e = layout(
            arena, (4 * DK, P), (T, P), (T, P), (T, P), (2, FC), (2, FC), (2, 512))
        taken[0] = 0

        taken[0] = 0
        (fu, fe, flf, fnlf, fcum, fmax, fsum, finv, mu, me, ml_lf, m_rn_f, m_an, m_em, m_den, m_rden, m_ssq, m_inv,
         m_rstd) = layout(
            s_cols, (T, FOX_H), (T, FOX_H), (T, FOX_H), (T, FOX_H), (T, FOX_H), (FOX_H, T), (FOX_H, T), (FOX_H, T),
            (T, 2 * ML_H), (T, ML_H), (T, ML_H), (T, ML_H), (T, ML_H), (T, ML_H), (ML_H, T), (ML_H, T), (ML_H, T),
            (ML_H, T), (ML_H, T))
        (r_log, r_cmp, r_eq, r_rank, r_sel, r_max, r_e, r_sum, r_gate, r_pos, r_cnt, r_over, r_oc, r_pick, r_prod, pos_i,
         gate_i, r_eidf) = layout(
            s_cols, (T, NE), (T * NE, NE), (T * NE, NE), (T, NE), (T, NE), (T, 1), (T, NE), (T, 1), (T, NE),
            (T, NE), (T, NE), (NE,), (NE,), (NEXTRA, NE), (NEXTRA * T, NE), (NITEM + 1, T), (NITEM + 1, T),
            (1 + NEXTRA,))
        assert taken[0] <= 720

        ident = cst[:, C_ID:C_ID + P]
        u_inc = cst[:, C_UINC:C_UINC + P]
        u_inc_ones = cst[:, C_UINC:C_UINC + 2 * P]
        ones = cst[:, C_ONES:C_ONES + P]
        u_str = cst[:, C_USTR:C_USTR + P]
        l_str = cst[:, C_LSTR:C_LSTR + P]

        x_loaded = sem("x_loaded")
        cst_loaded = sem("cst_loaded")
        vec_loaded = sem("vec_loaded")
        gate_w_loaded = sem("gate_w_loaded")
        bias_loaded = sem("bias_loaded")
        pool_w_zero = sem("pool_w_zero")
        pool_w_loaded = sem("pool_w_loaded")
        g_loaded = sem("g_loaded")
        ws_high = sem("ws_high")
        ws_ready = sem("ws_ready")
        ht_high = sem("ht_high")
        mix_high = sem("mix_high")
        fact_high = sem("fact_high")
        fact_ready = sem("fact_ready")
        xg_high = sem("xg_high")
        mact_high = sem("mact_high")
        ssq_ready = sem("ssq_ready")
        inv_ready = sem("inv_ready")
        rstd_ready = sem("rstd_ready")
        hn_ready = sem("hn_ready")
        dve_step = sem("dve_step")
        act_step = sem("act_step")
        fu_ready = sem("fu_ready")
        fln_ready = sem("fln_ready")
        flf_ready = sem("flf_ready")
        fmax_ready = sem("fmax_ready")
        fexp_ready = sem("fexp_ready")
        fprob_ready = sem("fprob_ready")
        fsilu_ready = sem("fsilu_ready")
        mu_ready = sem("mu_ready")
        mln_ready = sem("mln_ready")
        mlf_ready = sem("mlf_ready")
        mv_ones = sem("mv_ones")
        conv_ready = sem("conv_ready")
        conv_silu = sem("conv_silu")
        mr_ready = sem("mr_ready")
        mem_ready = sem("mem_ready")
        sbl_ready = sem("sbl_ready")
        sbsp_ready = sem("sbsp_ready")
        sbsp_masked = sem("sbsp_masked")
        sbw_exp = sem("sbw_exp")
        sbw_masked = sem("sbw_masked")
        me_in = sem("me_in")
        me_ready = sem("me_ready")
        mw_masked = sem("mw_masked")
        mh_sq = sem("mh_sq")
        mh_inv = sem("mh_inv")
        mh_rstd = sem("mh_rstd")
        md_ready = sem("md_ready")
        r_in = sem("r_in")
        r_exp = sem("r_exp")
        rsel_ready = sem("rsel_ready")
        route_ready = sem("route_ready")
        sel_ready = sem("sel_ready")
        experts_done = sem("experts_done")
        out_ready = sem("out_ready")
        out_done = sem("out_done")

        def piece(buf, n, rows):
            return buf[:, n % (RAW if buf is raw else SPLITS), :].rearrange("p (k f) -> p k f", k=rows)

        def used(n, item=0):
            if n < N_WO0:
                return filled(("even", n))
            if N_ODD <= n < N_WO1:
                return filled(("odd", n - N_ODD))
            for layer, base in enumerate((N_WO0, N_WO1)):
                if base <= n < base + WO_PIECES - 1:
                    return wo_piece_used, layer * (WO_PIECES - 1) + n - base + 1
                if n == base + WO_PIECES - 1:
                    return filled(("wout", layer, 3))
            experts = n >= N_MOE
            key = (EXPERT_ORDER if experts else FFN_ORDER)[n - (N_MOE if experts else N_FFN)]
            fill = ends_a_fill(key, experts)
            if fill is not None:
                return filled(fill, item)
            if experts:
                return expert_piece_used, len(EXPERT_COUNTED) * item + EXPERT_COUNTED.index(key) + 1
            return ffn_piece_used, FFN_COUNTED.index(key) + 1

        def split_done(n, item=0):
            return split_ready, n + 1 + FFN_PIECES * item

        def make_high(act, n, item=0):
            act.wait_ge(raw_full[n % RAW], 16 * (n // RAW + 1) + item * (16 * FFN_PIECES // RAW))
            if n - SPLITS >= N_MOE or SPLITS <= n < N_MOE:
                act.wait_ge(*used(n - SPLITS, item))
            elif n == N_MOE + SPLITS - 1:
                b, count = uses[("my", 1)]
                act.wait_ge(s_filled[b], count - 1 + item * bank_fills_per_item[b])
            nc.scalar.activation(high[:, n % SPLITS, :], raw[:, n % RAW, :], ACT.Copy).then_inc(high_ready, 1)

        def make_low(dve, n, item=0):
            dve.wait_ge(high_ready, n + 1 + FFN_PIECES * item)
            nc.vector.tensor_tensor(low[:, n % SPLITS, :], raw[:, n % RAW, :], high[:, n % SPLITS, :].bitcast(F32),
                                    ALU.subtract).then_inc(split_ready, 1)

        class Steps:

            def __init__(self, eng, s):
                self.eng, self.s, self.n, self.item, self.per_item = eng, s, 0, 0, 0

            def mark(self, ins):
                self.n += 1
                ins.then_inc(self.s, 1)
                return self.n

            def wait(self, n):
                self.eng.wait_ge(self.s, n + self.item * self.per_item)

            def done(self, ins):
                self.wait(self.mark(ins))

        def job_target(job):
            _, what, idx = job

            def pairs(b):
                return b[:, :].rearrange("p (c n) -> p c n", c=2)

            cols = slice(idx * SEQ, (idx + 1) * SEQ)
            if what == "a":
                return pool_a, 1.0, pairs
            if what == "v":
                return fv[:, :, cols], 1.0, pairs
            if what == "sv":
                return sv[:, :, cols], 1.0, pairs
            if what == "mo":
                return ml_o[:, :, cols], 1.0, pairs
            if what == "mv":
                return (mv.rearrange("p (t h) d -> p t h d", t=T)[:, :, 2 * idx:2 * idx + 2, 0:P], 1.0,
                        lambda b: b[:, :].rearrange("p (t h d) -> p t h d", t=T, h=2))
            dst = {"q": fq, "k": fk, "sq": sq, "sk": sk, "mq": mq_in, "mk": mk_in}[what]
            return dst[:, idx:idx + 2, :], (HD ** -0.5 if what in ("q", "sq") else 1.0), pairs

        ACT_ODD_JOBS = [n for n, job in enumerate(ODD_JOBS) if n % 2 or job[1] == "mo"]

        block = ctx.enter_context(nc.Block())

        @block.sync
        def _(sp):
            def load(n, src, item=0):
                if n >= RAW:
                    sp.wait_ge(*split_done(n - RAW, item))
                sp.dma_start(piece(raw, n, src.shape[1]), src).then_inc(raw_full[n % RAW], 16)

            def columns(wt, c0, k0=0, k1=DK, width=SEQ):
                return wt.rearrange("(k p) c -> p k c", p=P)[:, k0:k1, c0:c0 + width]

            def ffn_pieces(wg, wu, wd):
                for j, (kind, c, h) in enumerate(FFN_ORDER):
                    if kind == "d":
                        src = columns(wd, 0, 4 * c + 2 * h, 4 * c + 2 * h + 2, DM)
                    else:
                        src = columns(wg if kind == "g" else wu, c * FC + h * SEQ)
                    load(N_FFN + j, src)

            def expert_weights(kind, expert, after=0):
                wt = w[{"g": "moe_w_gate", "u": "moe_w_up", "d": "moe_w_down"}[kind]][0][after:]
                return wt[bass.ds(expert, 1)].rearrange("o r c -> (o r) c")

            def expert_piece(wt, j):
                kind, c, h = EXPERT_ORDER[j]
                if kind == "d":
                    return columns(wt, 0, 4 * c + 2 * h, 4 * c + 2 * h + 2, DM)
                return columns(wt, c * FC, 4 * h, 4 * h + 4, FC)

            def expert_pieces(item, expert, following, after=0):
                wt = {kind: expert_weights(kind, expert) for kind in "gud"}
                for j in range(1, FFN_PIECES):
                    load(N_MOE + j, expert_piece(wt[EXPERT_ORDER[j][0]], j), item)
                load(N_MOE + FFN_PIECES, expert_piece(expert_weights("g", following, after), 0), item)

            for t in range(T):
                sp.dma_start(x[:, t, :], x_d[0, t * P:(t + 1) * P, :]).then_inc(x_loaded, 16)
            sp.dma_start(cst[:, :], cst_d[:, 0:C_BAND]).then_inc(cst_loaded, 16)
            for name, col, width, src_col in (("ev_w_in", S_F, FOX_H, EVEN_PIECES * SEQ),
                                              ("od_w_in", S_M, 2 * ML_H, ODD_PIECES * SEQ),
                                              ("moe_w_router", S_R, NE, 0)):
                sp.dma_start(w_small[:, :, col:col + width], columns(w[name][0], src_col, width=width)).then_inc(
                    gate_w_loaded, 16)
            for j, job in enumerate(EVEN_JOBS):
                load(j, columns(w["ev_w_in"][0], EVEN_COLUMNS.index(job) * SEQ))
            for j in range(WO_PIECES):
                load(N_WO0 + j, columns(w["ev_w_out"][0], 0, 2 * j, 2 * j + 2, DM))
            ffn_pieces(w["ffn_w_gate"][0], w["ffn_w_up"][0], w["ffn_w_down"][0])
            for j, job in enumerate(ODD_JOBS):
                load(N_ODD + j, columns(w["od_w_in"][0], ODD_COLUMNS.index(job) * SEQ))
            for j in range(WO_PIECES):
                load(N_WO1 + j, columns(w["od_w_out"][0], 0, 2 * j, 2 * j + 2, DM))

            load(N_MOE, expert_piece(expert_weights("g", 0), 0))
            with sp.Fori(0, NE - 1) as item:
                expert_pieces(item, item, item, 1)
            sp.wait_ge(route_ready, 1)
            n_items = sp.value_load(route_i[0:1, 0:1], min_val=NE, max_val=NITEM)
            extra = [sp.value_load(route_i[0:1, 1 + j:2 + j], min_val=0, max_val=NE - 1) for j in range(NEXTRA)]
            expert_pieces(NE - 1, NE - 1, extra[0])
            for over in range(NOVER):
                with sp.If(n_items > NE + over):
                    expert_pieces(NE + over, extra[over], extra[over + 1])
            for t in range(T):
                sp.wait_ge(out_ready, t + 1)
                sp.dma_start(out_d[0, t * P:(t + 1) * P, :], hn[:, t, :]).then_inc(out_done, 16)
            sp.wait_ge(out_done, 16 * T)

        @block.tensor
        def _(pe):
            mm = nc.tensor.matmul

            def transposes_of_norm(j):
                for i in range(4):
                    open_bank(pe, ("norm", j, i))
                    for c in range(2):
                        for t in range(T):
                            if i == 0 and c == 0:
                                pe.wait_ge(hn_ready, T * j + t + 1)
                            last = nc.tensor.transpose(
                                ps(("norm", j, i))[:, (c * T + t) * P:(c * T + t + 1) * P],
                                hn[:, t, (2 * i + c) * P:(2 * i + c + 1) * P], ident)
                    last.then_inc(fill_sem(("norm", j, i)), 1)

            def mm3(out, l_high, l_low, r_high, r_low, start, stop):
                mm(out, l_high, r_high, start=start, stop=False)
                mm(out, l_high, r_low, start=False, stop=False)
                return mm(out, l_low, r_high, start=False, stop=stop)

            def project(stage, n, jobs, base):
                use = (stage, n)
                pe.wait_ge(*split_done(base + n))
                open_bank(pe, use)
                wh, wl = piece(high, base + n, DK), piece(low, base + n, DK)
                for c in range(2):
                    for k in range(DK):
                        out = ps(use)[:, c * SEQ:(c + 1) * SEQ]
                        half = slice(c * P, (c + 1) * P)
                        first, final = k == 0, k == DK - 1
                        if jobs[n][0] == "T":
                            last = mm3(out, wh[:, k, half], wl[:, k, half], ht_h[:, k, :], ht_l[:, k, :], first, final)
                        else:
                            last = mm3(out, ht_h[:, k, half], ht_l[:, k, half], wh[:, k, :], wl[:, k, :], first, final)
                last.then_inc(fill_sem(use), 1)

            def small_projection(use, col, width, j):
                rows = use + "_rows"
                open_bank(pe, rows)
                pe.wait_ge(ws_ready, 1)
                for k in range(DK):
                    if k % 2 == 0:
                        pe.wait_ge(*drained(("norm", j, k // 2)))
                    last = mm3(ps(rows)[0:width, 0:SEQ], ws_h[:, k, col:col + width], ws_l[:, k, col:col + width],
                               ht_h[:, k, :], ht_l[:, k, :], k == 0, k == DK - 1)
                last.then_inc(fill_sem(rows), 1)

            def small_columns(use, width):
                open_bank(pe, use)
                pe.wait_ge(*drained(use + "_rows"))
                for t in range(T):
                    last = nc.tensor.transpose(ps(use)[:, t * width:(t + 1) * width],
                                               few_rows[0:width, t * P:(t + 1) * P], ident[0:width, 0:width])
                last.then_inc(fill_sem(use), 1)

            def prefix_sums(use, src, width):
                open_bank(pe, use)
                mm(ps(use)[:, 0:width], u_inc, src[:, 0, :], start=True, stop=True)
                mm(ps(use)[:, width:2 * width], ones, src[:, 0, :], start=True, stop=False)
                mm(ps(use)[:, width:2 * width], u_inc, src[:, 1, :], start=False,
                   stop=True).then_inc(fill_sem(use), 1)

            def output_piece(layer, base, j, tiles=(0, 1)):
                pe.wait_ge(*split_done(base + j))
                wh, wl = piece(high, base + j, 2), piece(low, base + j, 2)
                for n in range(2 * tiles[0], 2 * tiles[-1] + 2):
                    t, cols = n // 2, slice(n % 2 * 512, n % 2 * 512 + 512)
                    use = ("wout", layer, n)
                    if j == 0:
                        open_bank(pe, use)
                    for k in range(2):
                        last = mm3(ps(use), mix_h[:, 2 * j + k, t * P:(t + 1) * P],
                                   mix_l[:, 2 * j + k, t * P:(t + 1) * P], wh[:, k, cols], wl[:, k, cols],
                                   j == 0 and k == 0, j == WO_PIECES - 1 and k == 1)
                    if j == WO_PIECES - 1:
                        last.then_inc(fill_sem(use), 1)
                    elif n == 3:
                        last.then_inc(wo_piece_used, 1)

            pe.wait_ge(cst_loaded, 16)
            transposes_of_norm(0)
            small_projection("fgate", S_F, FOX_H, 0)
            pe.wait_ge(vec_loaded, 16 * 3)
            nc.tensor.transpose(ps("vectors")[:, 0:V_ALL], vec_rows[:, :], ident[0:V_ALL, 0:V_ALL]).then_inc(
                fill_sem("vectors"), 1)

            def pool_windows(g2):
                use = ("pool", g2)
                open_bank(pe, use)
                for g in range(2):
                    grp = 2 * g2 + g
                    o = ps(use)[g * HD:(g + 1) * HD, :]
                    cols = slice(grp * HD, (grp + 1) * HD)
                    mm(o[:, 0:P], pool_a[:, 0, cols], bands[:, 3 * grp, :], start=True, stop=True)
                    mm(o[:, P:2 * P], pool_a[:, 0, cols], bands[:, 3 * grp + 1, :], start=True, stop=False)
                    last = mm(o[:, P:2 * P], pool_a[:, 1, cols], bands[:, 3 * grp + 2, :], start=False, stop=True)
                last.then_inc(fill_sem(use), 1)

            def pool_mix(g2):
                use = ("poolmix", g2)
                open_bank(pe, use)
                mm(ps(use)[:, 0:SEQ], pool_w[:, g2, :], pooled[:, g2, :], start=True, stop=True).then_inc(
                    fill_sem(use), 1)

            def values(use, h, v, p0, q01, q1):
                o = ps(use)[(h % 2) * HD:(h % 2 + 1) * HD, 0:SEQ]
                mm(o, v[:, 0, h * HD:(h + 1) * HD], q01, start=True, stop=False)
                return mm(o[:, P:SEQ], v[:, 1, h * HD:(h + 1) * HD], q1, start=False, stop=True)

            def fox(h):
                if h < FOX_H:
                    use = ("fox_s", h)
                    rows_h = slice((h % 2) * HD, (h % 2 + 1) * HD)
                    if h % 4 == 0:
                        for n in range(3 * h // 4, 3 * h // 4 + 3):
                            pe.wait_ge(*drained(("even", n)))
                    open_bank(pe, use)
                    lf0 = fnlf[:, 0, h:h + 1].to_broadcast([P, P])
                    lf1 = fnlf[:, 1, h:h + 1].to_broadcast([P, P])
                    mm(ps(use)[:, 0:P], fq[rows_h, h // 2, 0:P], fk[rows_h, h // 2, 0:P], start=True, stop=False)
                    mm(ps(use)[:, 0:P], lf0, u_inc, start=False, stop=True)
                    mm(ps(use)[:, P:384], fq[rows_h, h // 2, P:SEQ], fk[rows_h, h // 2, :], start=True, stop=False)
                    mm(ps(use)[:, P:384], lf0, u_inc_ones, start=False, stop=False)
                    mm(ps(use)[:, 2 * P:384], lf1, u_inc, start=False, stop=True).then_inc(fill_sem(use), 1)
                if 1 <= h <= FOX_H:
                    use = ("fox_pt", h - 1)
                    open_bank(pe, use)
                    pe.wait_ge(fprob_ready, h)
                    for b in range(3):
                        last = nc.tensor.transpose(ps(use)[:, b * P:(b + 1) * P],
                                                   fp[:, (h - 1) % 3, b * P:(b + 1) * P], ident)
                    last.then_inc(fill_sem(use), 1)
                if h >= 2:
                    g = h - 2
                    use = ("fox_o", g // 2)
                    if g % 2 == 0:
                        open_bank(pe, use)
                    pe.wait_ge(*drained(("fox_pt", g)))
                    last = values(use, g, fv, 0, fpt[:, g % 4, 0:SEQ], fpt[:, g % 4, SEQ:384])
                    if g % 2 == 1:
                        last.then_inc(fill_sem(use), 1)

            for n in range(FOX_AFTER + FOX_H + 2):
                h = n - FOX_AFTER
                if n < len(EVEN_JOBS):
                    project("even", n, EVEN_JOBS, 0)
                if n == 0:
                    small_columns("fgate", FOX_H)
                if n == EVEN_SUMS_AFTER:
                    pe.wait_ge(flf_ready, 1)
                    prefix_sums("fcum", flf, FOX_H)
                if h >= 0:
                    fox(h)
                if h in WOUT_STEPS:
                    j = WOUT_STEPS[h]
                    for part in (0, 1):
                        pe.wait_ge(*drained(("fox_o", 2 * j - 2 + part) if j else ("poolmix", part)))
                    output_piece(0, N_WO0, j, (0,))
                if h == POOL_STEP:
                    pe.wait_ge(pool_w_loaded, 16 * 5)
                for g2 in range(2):
                    if h == POOL_STEP + g2:
                        pe.wait_ge(*drained(("even", len(EVEN_JOBS) - 1)))
                        pool_windows(g2)
                for g2 in range(2):
                    if h == POOL_STEP + g2 + 1:
                        pe.wait_ge(*drained(("pool", g2)))
                        pool_mix(g2)
            for j in range(WO_PIECES - 1):
                output_piece(0, N_WO0, j, (1,))
            for g in range(FOX_H // 2 - 2, FOX_H // 2):
                pe.wait_ge(*drained(("fox_o", g)))
            output_piece(0, N_WO0, WO_PIECES - 1)

            transposes_of_norm(1)

            def ffn_gate_up(n, kind, c, h):
                g = 0 if kind == "g" else 1
                wh, wl = piece(high, n, DK), piece(low, n, DK)
                for j in (2 * h, 2 * h + 1):
                    use = ("gu", c, j)
                    if g == 0:
                        open_bank(pe, use)
                    cols = slice((j % 2) * P, (j % 2 + 1) * P)
                    for k in range(DK):
                        if (g, c, j) == (0, 0, 0) and k % 2 == 0:
                            pe.wait_ge(*drained(("norm", 1, k // 2)))
                        last = mm3(ps(use)[:, g * SEQ:(g + 1) * SEQ], wh[:, k, cols], wl[:, k, cols], ht_h[:, k, :],
                                   ht_l[:, k, :], k == 0, k == DK - 1)
                    if g:
                        last.then_inc(fill_sem(use), 1)
                return last

            def ffn_down(n, c, h):
                wh, wl = piece(high, n, 2), piece(low, n, 2)
                pe.wait_ge(fact_ready, 4 * c + 2 * h + 2)
                for q in range(4):
                    t, cols = q // 2, slice(q % 2 * 512, q % 2 * 512 + 512)
                    if c == 0 and h == 0:
                        open_bank(pe, ("fdown", q))
                    for k in range(2):
                        a = (c % 2) * 4 + 2 * h + k
                        last = mm3(ps(("fdown", q)), f_act_h[:, a, t * P:(t + 1) * P], f_act_l[:, a, t * P:(t + 1) * P],
                                   wh[:, k, cols], wl[:, k, cols], c == 0 and h == 0 and k == 0,
                                   c == NCH - 1 and h == 1 and k == 1)
                    if c == NCH - 1 and h == 1:
                        last.then_inc(fill_sem(("fdown", q)), 1)
                return last

            for j, key in enumerate(FFN_ORDER):
                kind, c, h = key
                pe.wait_ge(*split_done(N_FFN + j))
                last = ffn_down(N_FFN + j, c, h) if kind == "d" else ffn_gate_up(N_FFN + j, kind, c, h)
                if key in FFN_COUNTED:
                    last.then_inc(ffn_piece_used, 1)

            transposes_of_norm(2)
            small_projection("mgate", S_M, 2 * ML_H, 2)

            def gate_rows(h):
                use = ("mrow", h)
                open_bank(pe, use)
                lf = [ml_lf[:, t, h:h + 1].to_broadcast([P, P]) for t in range(T)]
                li = [mu[:, t, h:h + 1].to_broadcast([P, P]) for t in range(T)]
                mm(ps(use)[:, 0:SEQ], lf[0], u_inc_ones, start=True, stop=False)
                mm(ps(use)[:, P:SEQ], lf[1], u_inc, start=False, stop=True)
                for t in range(T):
                    last = mm(ps(use)[:, SEQ + t * P:SEQ + (t + 1) * P], li[t], ident, start=True, stop=True)
                last.then_inc(fill_sem(use), 1)

            def rows_to_columns():
                open_bank(pe, "mr")
                pe.wait_ge(mr_ready, ML_H)
                for t in range(T):
                    for h in range(ML_H):
                        last = mm(ps("mr")[:, t * ML_H + h:t * ML_H + h + 1], ml_r[0:1, h, t * P:(t + 1) * P],
                                  ones[0:1, 0:1], start=True, stop=True)
                last.then_inc(fill_sem("mr"), 1)

            def stick_breaking(h):
                if h < SB_H:
                    use = ("sb_z", h)
                    rows_h = slice((h % 2) * HD, (h % 2 + 1) * HD)
                    if h % 4 == 0:
                        for n in range(3 * h // 4, 3 * h // 4 + 3):
                            pe.wait_ge(*drained(("odd", n)))
                    open_bank(pe, use)
                    mm(ps(use)[:, 0:SEQ], sk[rows_h, h // 2, 0:P], sq[rows_h, h // 2, :], start=True, stop=True)
                    mm(ps(use)[:, SEQ:384], sk[rows_h, h // 2, P:SEQ], sq[rows_h, h // 2, P:SEQ], start=True,
                       stop=True).then_inc(fill_sem(use), 1)
                if 1 <= h <= SB_H:
                    use = ("sb_lat", h - 1)
                    sp_h = sb_sp[:, (h - 1) % 3, :]
                    open_bank(pe, use)
                    pe.wait_ge(sbsp_masked, h)
                    mm(ps(use)[:, 0:SEQ], l_str, sp_h[:, 0:SEQ], start=True, stop=False)
                    mm(ps(use)[:, P:SEQ], ones, sp_h[:, SEQ:384], start=False, stop=True)
                    mm(ps(use)[:, SEQ:384], l_str, sp_h[:, SEQ:384], start=True, stop=True).then_inc(
                        fill_sem(use), 1)
                if h >= 2:
                    g = h - 2
                    use = ("sb_o", g // 2)
                    if g % 2 == 0:
                        open_bank(pe, use)
                    pe.wait_ge(sbw_masked, g + 1)
                    last = values(use, g, sv, 0, sb_w[:, g % 4, 0:SEQ], sb_w[:, g % 4, SEQ:384])
                    if g % 2 == 1:
                        last.then_inc(fill_sem(use), 1)
                if h == ROWS_TURNED_AT:
                    rows_to_columns()

            for n in range(len(ODD_JOBS)):
                project("odd", n, ODD_JOBS, N_ODD)
                if n == 0:
                    small_columns("mgate", 2 * ML_H)
                if n == ODD_SUMS_AFTER:
                    pe.wait_ge(mlf_ready, 1)
                    prefix_sums("mcum", ml_lf, ML_H)
                for h in ODD_ROWS_AFTER.get(n, ()):
                    gate_rows(h)
                if 0 <= n - SB_AFTER < SB_H + 2:
                    stick_breaking(n - SB_AFTER)

            for g in range(SB_H // 2 - 2):
                pe.wait_ge(*drained(("sb_o", g)))
            output_piece(1, N_WO1, 0)
            pe.wait_ge(conv_silu, 2)
            for n in range(10, 12):
                pe.wait_ge(*drained(("odd", n)))
            pe.wait_ge(mv_ones, 1)
            for h in range(ML_H + 1):
                if h < ML_H:
                    use = ("ml_s", h)
                    open_bank(pe, use)
                    mm(ps(use)[:, 0:SEQ], mqk[:, 4 + h, 0:P], mqk[:, h, :], start=True, stop=True)
                    mm(ps(use)[:, SEQ:384], mqk[:, 4 + h, P:SEQ], mqk[:, h, P:SEQ], start=True, stop=True).then_inc(
                        fill_sem(use), 1)
                if h:
                    g = h - 1
                    use = ("ml_n", g)
                    open_bank(pe, use)
                    pe.wait_ge(mw_masked, g + 1)
                    o = ps(use)[:, 0:2 * 129].rearrange("p (t d) -> p t d", t=T)
                    wt = ml_w[:, g % 4, :]
                    mm(o[:, 0, :], wt[:, 0:P], mv[:, g, :], start=True, stop=True)
                    mm(o[:, 1, :], wt[:, P:SEQ], mv[:, g, :], start=True, stop=False)
                    mm(o[:, 1, :], wt[:, SEQ:384], mv[:, ML_H + g, :], start=False, stop=True).then_inc(
                        fill_sem(use), 1)
            for g in range(SB_H // 2 - 2, SB_H // 2):
                pe.wait_ge(*drained(("sb_o", g)))
            output_piece(1, N_WO1, 1)
            for h in range(ML_H):
                use = ("ml_t", h)
                open_bank(pe, use)
                for t in range(T):
                    pe.wait_ge(md_ready, t + 1)
                    last = nc.tensor.transpose(ps(use)[:, t * P:(t + 1) * P], ml_h[:, t, h * P:(h + 1) * P], ident)
                last.then_inc(fill_sem(use), 1)
            for j in range(2, WO_PIECES):
                for h in (2 * j - 4, 2 * j - 3):
                    pe.wait_ge(*drained(("ml_t", h)))
                output_piece(1, N_WO1, j)

            transposes_of_norm(3)
            small_projection("router", S_R, NE, 3)
            small_columns("router", NE)
            pe.wait_ge(rsel_ready, 1)
            open_bank(pe, "rank")
            rk = ps("rank")
            mm(rk[:, 0:NE], u_inc, r_sel[:, 0, :], start=True, stop=True)
            mm(rk[:, NE:2 * NE], ones, r_sel[:, 0, :], start=True, stop=False)
            mm(rk[:, NE:2 * NE], u_inc, r_sel[:, 1, :], start=False, stop=True)
            mm(rk[:, 2 * NE:3 * NE], ones, r_sel[:, 0, :], start=True, stop=False)
            mm(rk[:, 2 * NE:3 * NE], ones, r_sel[:, 1, :], start=False, stop=True).then_inc(fill_sem("rank"), 1)

            def act_transposes(c, item):
                use = ("mt", c)
                open_bank(pe, use, item)
                pe.wait_ge(*drained(("mu", c), item))
                for j in range(4):
                    last = nc.tensor.transpose(ps(use)[:, j * P:(j + 1) * P], m_act[:, c % 2, j * P:(j + 1) * P],
                                               ident)
                last.then_inc(fill_sem(use), 1)

            def expert_gate_up(n, kind, c, h, item):
                use = ("m" + kind, c)
                if h == 0:
                    open_bank(pe, use, item)
                wh, wl = piece(high, n, 4), piece(low, n, 4)
                for k in range(4):
                    last = mm3(ps(use), xg_h[:, 4 * h + k, :], xg_l[:, 4 * h + k, :], wh[:, k, :], wl[:, k, :],
                               h == 0 and k == 0, h == 1 and k == 3)
                if h:
                    last.then_inc(fill_sem(use), 1)
                return last

            def expert_down(n, c, h, item):
                pe.wait_ge(*drained(("mt", c), item))
                wh, wl = piece(high, n, 2), piece(low, n, 2)
                for nh in range(2):
                    use, cols = ("my", nh), slice(nh * 512, (nh + 1) * 512)
                    if c == 0 and h == 0:
                        open_bank(pe, use, item)
                    for k in range(2):
                        a = (c % 2) * 4 + 2 * h + k
                        last = mm3(ps(use), m_act_h[:, a, :], m_act_l[:, a, :], wh[:, k, cols], wl[:, k, cols],
                                   c == 0 and h == 0 and k == 0, c == NCH - 1 and h == 1 and k == 1)
                    if c == NCH - 1 and h == 1:
                        last.then_inc(fill_sem(use), 1)
                return last

            def gather(name, item):
                for half in range(2):
                    use = (name, half)
                    open_bank(pe, use, item)
                    for k in range(4):
                        for t in range(T):
                            last = mm(ps(use)[:, k * P:(k + 1) * P],
                                      hn[:, t, (half * 4 + k) * P:(half * 4 + k + 1) * P], sel[:, t, :],
                                      start=t == 0, stop=t == T - 1)
                    last.then_inc(fill_sem(use), 1)

            def expert_item(item):
                for half in range(2):
                    b, n = uses[("gather", half)]
                    pe.wait_ge(s_drained[b], n - bank_fills_per_item[b] + item * bank_fills_per_item[b])
                for j, key in enumerate(EXPERT_ORDER):
                    kind, c, h = key
                    if key == ("u", 0, 1):
                        open_bank(pe, "sgt", item)
                        for t in range(T):
                            last = nc.tensor.transpose(ps("sgt")[:, t * P:(t + 1) * P], sel_g[:, t, :], ident)
                        last.then_inc(fill_sem("sgt"), 1)
                    if key == ("u", c, 0) and c:
                        act_transposes(c - 1, item)
                    if key == ("d", NCH - 1, 0):
                        act_transposes(NCH - 1, item)
                        pe.wait_ge(sel_ready, item + 2)
                        gather("gather", item)
                    pe.wait_ge(*split_done(N_MOE + j, item))
                    if kind == "d":
                        last = expert_down(N_MOE + j, c, h, item)
                    else:
                        last = expert_gate_up(N_MOE + j, kind, c, h, item)
                    if key in EXPERT_COUNTED:
                        last.then_inc(expert_piece_used, 1)
                pe.wait_ge(*drained("sgt", item))
                for n in range(4):
                    t, nh = n // 2, n % 2
                    use = ("mc", n)
                    open_bank(pe, use, item)
                    pe.wait_ge(*drained(("my", nh), item))
                    mm(ps(use), sgt[:, t, :], y_e[:, nh, :], start=True, stop=True).then_inc(fill_sem(use), 1)

            pe.wait_ge(sel_ready, 1)
            gather("gather0", 0)
            with pe.Fori(0, NE) as item:
                expert_item(item)
            pe.wait_ge(route_ready, 1)
            n_items = pe.value_load(route_i[0:1, 0:1], min_val=NE, max_val=NITEM)
            with pe.Fori(NE, NITEM) as item:
                with pe.If(n_items > item):
                    expert_item(item)

        @block.scalar
        def _(act):
            fn = nc.scalar.activation
            steps = Steps(act, act_step)

            def high_parts(first, count=1):
                for n in range(first, first + count):
                    make_high(act, n)

            def mix_high_part(chunk, use, scale=1.0):
                act.wait_ge(*filled(use))
                fn(mix_h[:, chunk, :], ps(use)[:, 0:SEQ], ACT.Copy, scale=scale).then_inc(mix_high, 1)

            def squares(j, added=None):
                for t in range(T):
                    for n in (2 * t, 2 * t + 1) if added else ():
                        act.wait_ge(*drained(added + (n,)))
                    fn(hn[:, t, :], x[:, t, :], ACT.Square, accum_out=ssq[:, j, t:t + 1]).then_inc(ssq_ready, 1)
                act.wait_ge(inv_ready, j + 1)
                fn(rstd[:, j, :], inv_ms[:, j, :], ACT.Sqrt).then_inc(rstd_ready, 1)

            def norm_banks(j):
                for i in range(4):
                    act.wait_ge(*filled(("norm", j, i)))
                    fn(ht_h[:, 2 * i:2 * i + 2, :], ps(("norm", j, i)).rearrange("p (k c) -> p k c", k=2),
                       ACT.Copy).then_inc(ht_high, 1)

            def log_of_1_plus_exp(v, ready, n, out_sem):
                act.wait_ge(ready, n)
                steps.done(fn(v, v, ACT.Exp))
                fn(v, v, ACT.Ln, bias=1.0).then_inc(out_sem, 1)

            act.wait_ge(x_loaded, 32)
            squares(0)
            act.wait_ge(gate_w_loaded, 48)
            fn(ws_h[:, :, :], w_small[:, :, :], ACT.Copy).then_inc(ws_high, 1)
            high_parts(0)
            norm_banks(0)
            high_parts(1, 2)
            log_of_1_plus_exp(fe, fu_ready, 1, fln_ready)

            def fox(h):
                if h < FOX_H:
                    act.wait_ge(fmax_ready, 2 * h + 2)
                    fn(fp[:, h % 3, 0:P], fp[:, h % 3, 0:P], ACT.Exp, bias=fmax[:, h, 0:1],
                       accum_out=fsum[:, h, 0:1])
                    fn(fp[:, h % 3, P:384], fp[:, h % 3, P:384], ACT.Exp, bias=fmax[:, h, 1:2],
                       accum_out=fsum[:, h, 1:2]).then_inc(fexp_ready, 1)
                if 1 <= h <= FOX_H:
                    use = ("fox_pt", h - 1)
                    act.wait_ge(*filled(use))
                    fn(fpt[:, (h - 1) % 4, :], ps(use)[:, 0:384], ACT.Copy).then_inc(drain_sem(use), 1)
                if h >= 2 and h % 2 == 1:
                    mix_high_part(2 + (h - 2) // 2, ("fox_o", (h - 2) // 2))

            for n in range(FOX_AFTER + FOX_H + 2):
                if n < len(EVEN_JOBS):
                    if n % 2:
                        act.wait_ge(*filled(("even", n)))
                        dst, scale, shape = job_target(EVEN_JOBS[n])
                        fn(dst, shape(ps(("even", n))), ACT.Copy, scale=scale).then_inc(drain_sem(("even", n)), 1)
                    high_parts(n + SPLITS)
                if n >= FOX_AFTER:
                    fox(n - FOX_AFTER)
            high_parts(N_WO0 + SPLITS)

            high_parts(N_FFN)
            squares(1, ("wout", 0))
            high_parts(N_FFN + 1)
            norm_banks(1)
            high_parts(N_FFN + 2)

            def silu_pair(c, h):
                for j in (2 * h, 2 * h + 1):
                    act.wait_ge(*filled(("gu", c, j)))
                    if (c, h) != (0, 0):
                        b = (c, j - 2) if h else (c - 1, j + 2)
                        act.wait_ge(*drained(("gu",) + b))
                    fn(f_silu[:, j % 2, :], ps(("gu", c, j))[:, 0:SEQ], ACT.Silu).then_inc(fsilu_ready, 1)

            def act_high_pair(c, h):
                for j in (2 * h, 2 * h + 1):
                    act.wait_ge(*drained(("gu", c, j)))
                    fn(f_act_h[:, (c % 2) * 4 + j, :], f_v[:, j % 2, :], ACT.Copy).then_inc(fact_high, 1)

            for j, (kind, c, h) in enumerate(FFN_ORDER):
                if j >= SPLITS:
                    high_parts(N_FFN + j)
                    kind, c, h = FFN_ORDER[j - SPLITS]
                    if kind == "u":
                        silu_pair(c, h)
                    kind, c, h = FFN_ORDER[j - SPLITS - 1] if j > SPLITS else ("", 0, 0)
                    if kind == "u":
                        act_high_pair(c, h)

            high_parts(N_ODD)
            squares(2, ("fdown",))
            high_parts(N_ODD + 1)
            norm_banks(2)
            high_parts(N_ODD + 2)
            log_of_1_plus_exp(me, mu_ready, 1, mln_ready)

            def stick_breaking(h):
                if h < SB_H:
                    use = ("sb_z", h)
                    lb = sb_l[:, h % 2, :]
                    act.wait_ge(*filled(use))
                    if h >= 2:
                        act.wait_ge(*drained(("sb_z", h - 2)))
                    steps.done(fn(lb, ps(use)[:, 0:384], ACT.Abs))
                    steps.done(fn(lb, lb, ACT.Exp, scale=-1.0))
                    fn(lb, lb, ACT.Ln, bias=1.0).then_inc(sbl_ready, 1)
                if 1 <= h <= SB_H:
                    act.wait_ge(*drained(("sb_lat", h - 1)))
                    fn(sb_w[:, (h - 1) % 4, :], sb_w[:, (h - 1) % 4, :], ACT.Exp).then_inc(sbw_exp, 1)
                if h >= 2 and h % 2 == 1:
                    mix_high_part((h - 2) // 2, ("sb_o", (h - 2) // 2))

            for n in range(len(ODD_JOBS)):
                if n in ACT_ODD_JOBS:
                    act.wait_ge(*filled(("odd", n)))
                    dst, scale, shape = job_target(ODD_JOBS[n])
                    func = ACT.Sigmoid if ODD_JOBS[n][1] == "mo" else ACT.Copy
                    fn(dst, shape(ps(("odd", n))), func, scale=scale).then_inc(drain_sem(("odd", n)), 1)
                high_parts(N_ODD + n + SPLITS)
                if 0 <= n - SB_AFTER < SB_H + 2:
                    stick_breaking(n - SB_AFTER)
                if n == CONV_AFTER + 4:
                    act.wait_ge(conv_ready, 8)
                    for half in range(2):
                        v = mqk[:, 4 * half:4 * half + 4, :]
                        fn(v, v, ACT.Silu).then_inc(conv_silu, 1)
            act.wait_ge(*drained("mr"))
            fn(m_em, m_em, ACT.Exp).then_inc(mem_ready, 1)
            for h in range(ML_H + 1):
                if h < ML_H:
                    act.wait_ge(me_in, h + 1)
                    fn(ml_e[:, h % 3, :], ml_e[:, h % 3, :], ACT.Exp).then_inc(me_ready, 1)
                if h:
                    g = h - 1
                    act.wait_ge(*drained(("ml_n", g)))
                    for t in range(T):
                        fn(sb_l[:, t, 0:P], ml_h[:, t, g * P:(g + 1) * P], ACT.Square,
                           accum_out=m_ssq[:, g, t:t + 1]).then_inc(mh_sq, 1)
                        act.wait_ge(mh_sq, 2 * g + t + 1)
            act.wait_ge(mh_inv, 1)
            fn(m_rstd, m_inv, ACT.Sqrt).then_inc(mh_rstd, 1)
            high_parts(N_WO1 + SPLITS)
            for h in range(ML_H):
                mix_high_part(4 + h, ("ml_t", h), vec[:, V_HEAD + h:V_HEAD + h + 1])

            squares(3, ("wout", 1))
            norm_banks(3)
            act.wait_ge(r_in, 1)
            fn(r_e, r_e, ACT.Exp).then_inc(r_exp, 1)

            def rows_high(name, item):
                for half in range(2):
                    act.wait_ge(*filled((name, half), item))
                    fn(xg_h[:, 4 * half:4 * half + 4, :], ps((name, half)).rearrange("p (k c) -> p k c", k=4),
                       ACT.Copy).then_inc(xg_high, 1)

            def expert_item(item):
                for n in range(1, SPLITS):
                    make_high(act, N_MOE + n, item)

                def act_high(c):
                    act.wait_ge(*filled(("mt", c), item))
                    at = (c % 2) * 4
                    fn(m_act_h[:, at:at + 4, :], ps(("mt", c)).rearrange("p (j c) -> p j c", j=4),
                       ACT.Copy).then_inc(mact_high, 1)

                for j in range(SPLITS, FFN_PIECES):
                    make_high(act, N_MOE + j, item)
                    kind, c, h = EXPERT_ORDER[j - SPLITS]
                    if (kind, c, h) == ("u", 0, 1):
                        act.wait_ge(*filled("sgt", item))
                        fn(sgt, ps("sgt")[:, 0:SEQ].rearrange("p (t c) -> p t c", t=T), ACT.Copy).then_inc(
                            drain_sem("sgt"), 1)
                    if (kind, h) == ("g", 1):
                        if c:
                            act_high(c - 1)
                        b, n = uses[("mu", c)]
                        act.wait_ge(*filled(("mg", c), item))
                        act.wait_ge(s_drained[b], n - 1 + item * bank_fills_per_item[b])
                        fn(m_silu[:, c % 2, :], ps(("mg", c)), ACT.Silu).then_inc(drain_sem(("mg", c)), 1)
                act_high(NCH - 1)
                rows_high("gather", item)
                make_high(act, N_MOE + FFN_PIECES, item)
                act.wait_ge(*filled(("my", 0), item))
                fn(y_e[:, 0, :], ps(("my", 0)), ACT.Copy).then_inc(drain_sem(("my", 0)), 1)

            make_high(act, N_MOE)
            rows_high("gather0", 0)
            with act.Fori(0, NE) as item:
                expert_item(item)
            act.wait_ge(route_ready, 1)
            n_items = act.value_load(route_i[0:1, 0:1], min_val=NE, max_val=NITEM)
            with act.Fori(NE, NITEM) as item:
                with act.If(n_items > item):
                    expert_item(item)
            act.wait_ge(experts_done, 1)
            squares(4)

        @block.gpsimd
        def _(pool):
            def load_gain(j, src):
                if j:
                    pool.wait_ge(hn_ready, T * j)
                pool.dma_start(g_row[:, :], src.partition_broadcast(P)).then_inc(g_loaded, 16)

            load_gain(0, w["norm_mix_g"][0])
            nc.gpsimd.memset(pool_w, 0.0).then_inc(pool_w_zero, 1)
            def as_rows(v):
                return v.rearrange("(k p) -> k p", p=P)

            for row, src in ((V_CONV, w["od_conv_w"][0].rearrange("t (k p) -> (t k) p", p=P)),
                             (V_POOL, as_rows(w["ev_pool_scale"][0])), (V_HEAD, w["od_head_norm_g"][0])):
                pool.dma_start(vec_rows[row:row + src.shape[0], :], src).then_inc(vec_loaded, 16)
            pool.dma_start(b_fgate[:, :], w["ev_b_forget"][0].partition_broadcast(P)).then_inc(bias_loaded, 16)
            pool.dma_start(b_mgate[:, 0:ML_H], w["od_b_igate"][0].partition_broadcast(P)).then_inc(bias_loaded, 16)
            pool.dma_start(b_mgate[:, ML_H:], w["od_b_fgate"][0].partition_broadcast(P)).then_inc(bias_loaded, 16)
            pool.dma_start(bands, cst_d[:, C_BAND:C_ALL].rearrange("p (b c) -> p b c", c=P)
                          ).then_inc(pool_w_loaded, 16)
            pool.wait_ge(pool_w_zero, 1)
            for g in range(4):
                half = slice((g % 2) * HD, (g % 2 + 1) * HD)
                pool.dma_start(pool_w[half, g // 2, half], w["ev_pool_w"][0, g]).then_inc(pool_w_loaded, 16)
            load_gain(1, w["norm_ffn_g"][0])
            load_gain(2, w["norm_mix_g"][1])

            def mask_diagonals(v, mask, s):
                blocks = v.rearrange("p (b c) -> p b c", b=3)[:, 0:3:2, :]
                nc.gpsimd.tensor_tensor(blocks, blocks, mask[:, None, :].to_broadcast([P, 2, P]),
                                        ALU.mult).then_inc(s, 1)

            pool.wait_ge(*filled(("odd", 0)))
            nc.gpsimd.memset(mv[:, :, 128:129], 1.0).then_inc(mv_ones, 1)
            for h in range(SB_H + 1):
                if h < SB_H:
                    pool.wait_ge(sbsp_ready, h + 1)
                    mask_diagonals(sb_sp[:, h % 3, :], u_str, sbsp_masked)
                if h:
                    pool.wait_ge(sbw_exp, h)
                    mask_diagonals(sb_w[:, (h - 1) % 4, :], u_str, sbw_masked)
                if h == 0:
                    load_gain(3, w["norm_ffn_g"][1])
            for h in range(ML_H):
                pool.wait_ge(*drained(("ml_s", h)))
                mask_diagonals(ml_w[:, h % 4, :], u_inc, mw_masked)
            load_gain(4, w["norm_final_g"])

        @block.vector
        def _(dve):
            V = nc.vector
            steps = Steps(dve, dve_step)

            def norm_scale(j):
                dve.wait_ge(ssq_ready, T * (j + 1))
                steps.done(V.tensor_scalar(inv_ms[:, j, :], ssq[:, j, :], 1.0 / DM, EPS, ALU.mult, ALU.add))
                V.reciprocal(inv_ms[:, j, :], inv_ms[:, j, :]).then_inc(inv_ready, 1)
                dve.wait_ge(rstd_ready, j + 1)
                dve.wait_ge(g_loaded, 16 * (j + 1))
                if j == 4:
                    return
                for t in range(T):
                    V.scalar_tensor_tensor(hn[:, t, :], x[:, t, :], rstd[:, j, t:t + 1], g_row[:, :], ALU.mult,
                                           ALU.mult).then_inc(hn_ready, 1)

            def norm_banks(j):
                for i in range(4):
                    dve.wait_ge(ht_high, 4 * j + i + 1)
                    V.tensor_tensor(ht_l[:, 2 * i:2 * i + 2, :], ps(("norm", j, i)).rearrange("p (k c) -> p k c", k=2),
                                    ht_h[:, 2 * i:2 * i + 2, :].bitcast(F32), ALU.subtract).then_inc(
                                        drain_sem(("norm", j, i)), 1)

            def copy_rows(use, width):
                rows = use + "_rows"
                dve.wait_ge(*filled(rows))
                V.tensor_copy(few_rows[0:width, :], ps(rows)[0:width, 0:SEQ]).then_inc(drain_sem(rows), 1)

            def low_parts(first, count=1):
                for n in range(first, first + count):
                    make_low(dve, n)

            def mix_low_part(chunk, use, number, scale=1.0):
                if number:
                    dve.wait_ge(mix_high, number)
                V.scalar_tensor_tensor(mix_l[:, chunk, :], ps(use)[:, 0:SEQ], scale, mix_h[:, chunk, :].bitcast(F32),
                                       ALU.mult, ALU.subtract).then_inc(drain_sem(use), 1)

            def drain_job(stage, jobs, n):
                dve.wait_ge(*filled((stage, n)))
                dst, scale, shape = job_target(jobs[n])
                V.tensor_scalar(dst, shape(ps((stage, n))), scale, None, ALU.mult).then_inc(
                    drain_sem((stage, n)), 1)

            def add_to_x(names):
                for n, use in enumerate(names):
                    t, nh = n // 2, n % 2
                    quarter = x[:, t, nh * 512:(nh + 1) * 512]
                    dve.wait_ge(*filled(use))
                    V.tensor_tensor(quarter, quarter, ps(use), ALU.add).then_inc(drain_sem(use), 1)

            def row_bias(b, n):
                return b[:, None, :].to_broadcast([P, T, n])

            dve.wait_ge(x_loaded, 32)
            norm_scale(0)
            dve.wait_ge(ws_high, 1)
            V.tensor_tensor(ws_l[:, :, :], w_small[:, :, :], ws_h[:, :, :].bitcast(F32), ALU.subtract).then_inc(
                ws_ready, 1)
            norm_banks(0)
            low_parts(0)
            copy_rows("fgate", FOX_H)
            low_parts(1, SPLITS - 1)
            dve.wait_ge(bias_loaded, 48)
            dve.wait_ge(*filled("fgate"))
            V.tensor_tensor(fu, ps("fgate")[:, 0:T * FOX_H].rearrange("p (t h) -> p t h", t=T),
                            row_bias(b_fgate, FOX_H), ALU.add).then_inc(drain_sem("fgate"), 1)
            dve.wait_ge(*drained("fgate"))
            V.scalar_tensor_tensor(fe, fu, -1.0, fu, ALU.mult, ALU.min).then_inc(fu_ready, 1)
            dve.wait_ge(fln_ready, 1)
            steps.done(V.scalar_tensor_tensor(flf, fu, 0.0, fe, ALU.min, ALU.subtract))
            V.tensor_scalar(fnlf, flf, -1.0, None, ALU.mult).then_inc(flf_ready, 1)
            dve.wait_ge(*filled("vectors"))
            V.tensor_copy(vec[:, :], ps("vectors")[:, 0:V_ALL]).then_inc(drain_sem("vectors"), 1)
            dve.wait_ge(*drained("vectors"))

            def fox(h):
                if h < FOX_H:
                    use = ("fox_s", h)
                    buf = fp[:, h % 3, :]
                    dve.wait_ge(*filled(use))
                    V.scalar_tensor_tensor(buf[:, 0:P], ps(use)[:, 0:P], fcum[:, 0, h:h + 1],
                                           cst[:, C_CM + P:C_CM + 2 * P], ALU.add, ALU.add)
                    V.scalar_tensor_tensor(buf[:, P:384], ps(use)[:, P:384], fcum[:, 1, h:h + 1],
                                           cst[:, C_CM:C_CM + 2 * P], ALU.add, ALU.add).then_inc(drain_sem(use), 1)
                    dve.wait_ge(*drained(use))
                    V.tensor_reduce(fmax[:, h, 0:1], buf[:, 0:P], AX, ALU.max, negate=True).then_inc(fmax_ready, 1)
                    V.tensor_reduce(fmax[:, h, 1:2], buf[:, P:384], AX, ALU.max, negate=True).then_inc(
                        fmax_ready, 1)
                    dve.wait_ge(fexp_ready, h + 1)
                    steps.done(V.reciprocal(finv[:, h, :], fsum[:, h, :]))
                    V.tensor_scalar(buf[:, 0:P], buf[:, 0:P], finv[:, h, 0:1], None, ALU.mult)
                    V.tensor_scalar(buf[:, P:384], buf[:, P:384], finv[:, h, 1:2], None, ALU.mult).then_inc(
                        fprob_ready, 1)
                if h >= 3 and h % 2 == 1:
                    mix_low_part(2 + (h - 3) // 2, ("fox_o", (h - 3) // 2), (h - 3) // 2 + 1)

            for n in range(FOX_AFTER + FOX_H + 2):
                h = n - FOX_AFTER
                if n < len(EVEN_JOBS):
                    if n % 2 == 0:
                        drain_job("even", EVEN_JOBS, n)
                    low_parts(n + SPLITS)
                if n == EVEN_SUMS_AFTER:
                    dve.wait_ge(*filled("fcum"))
                    V.tensor_copy(fcum, ps("fcum")[:, 0:T * FOX_H].rearrange("p (t h) -> p t h", t=T)).then_inc(
                        drain_sem("fcum"), 1)
                    dve.wait_ge(*drained("fcum"))
                if h >= 0:
                    fox(h)
                for g2 in range(2):
                    if h == POOL_STEP + g2:
                        dve.wait_ge(*filled(("pool", g2)))
                        V.tensor_copy(pooled[:, g2, :], ps(("pool", g2))[:, 0:SEQ]).then_inc(
                            drain_sem(("pool", g2)), 1)
                for g2 in range(2):
                    if h == POOL_STEP + g2 + 1:
                        dve.wait_ge(*filled(("poolmix", g2)))
                        scale = vec[:, V_POOL + g2:V_POOL + g2 + 1]
                        steps.done(V.tensor_scalar(mix_h[:, g2, :], ps(("poolmix", g2))[:, 0:SEQ], scale, None,
                                                   ALU.mult))
                        mix_low_part(g2, ("poolmix", g2), 0, scale)
            low_parts(N_WO0 + SPLITS)
            add_to_x([("wout", 0, n) for n in range(4)])

            low_parts(N_FFN)
            norm_scale(1)
            norm_banks(1)
            low_parts(N_FFN + 1, 2)

            def gated_pair(c, h):
                for j in (2 * h, 2 * h + 1):
                    use = ("gu", c, j)
                    dve.wait_ge(fsilu_ready, 4 * c + j + 1)
                    if (c, h) != (0, 0):
                        dve.wait_ge(fact_ready, 4 * c + j - 1)
                    V.tensor_tensor(f_v[:, j % 2, :], f_silu[:, j % 2, :], ps(use)[:, SEQ:2 * SEQ],
                                    ALU.mult).then_inc(drain_sem(use), 1)

            def act_low_pair(c, h):
                for j in (2 * h, 2 * h + 1):
                    a = (c % 2) * 4 + j
                    dve.wait_ge(fact_high, 4 * c + j + 1)
                    V.tensor_tensor(f_act_l[:, a, :], f_v[:, j % 2, :], f_act_h[:, a, :].bitcast(F32),
                                    ALU.subtract).then_inc(fact_ready, 1)

            for j in range(SPLITS, FFN_PIECES):
                low_parts(N_FFN + j)
                kind, c, h = FFN_ORDER[j - SPLITS]
                if kind == "u":
                    gated_pair(c, h)
                kind, c, h = FFN_ORDER[j - SPLITS - 1] if j > SPLITS else ("", 0, 0)
                if kind == "u":
                    act_low_pair(c, h)
            add_to_x([("fdown", n) for n in range(4)])
            low_parts(N_ODD)

            norm_scale(2)
            norm_banks(2)
            copy_rows("mgate", 2 * ML_H)
            low_parts(N_ODD + 1, 2)
            dve.wait_ge(*filled("mgate"))
            V.tensor_tensor(mu, ps("mgate")[:, 0:T * 2 * ML_H].rearrange("p (t h) -> p t h", t=T),
                            row_bias(b_mgate, 2 * ML_H), ALU.add).then_inc(drain_sem("mgate"), 1)
            dve.wait_ge(*drained("mgate"))
            V.scalar_tensor_tensor(me, mu[:, :, ML_H:], -1.0, mu[:, :, ML_H:], ALU.mult, ALU.min).then_inc(mu_ready, 1)
            dve.wait_ge(mln_ready, 1)
            V.scalar_tensor_tensor(ml_lf, mu[:, :, ML_H:], 0.0, me, ALU.min, ALU.subtract).then_inc(mlf_ready, 1)

            def gate_columns():
                dve.wait_ge(*filled("mcum"))
                V.tensor_copy(m_rn_f, ps("mcum")[:, 0:T * ML_H].rearrange("p (t h) -> p t h", t=T)).then_inc(
                    drain_sem("mcum"), 1)
                dve.wait_ge(*drained("mcum"))
                steps.done(V.tensor_tensor(m_an, mu[:, :, 0:ML_H], m_rn_f, ALU.subtract))

            def gate_rows(h):
                use = ("mrow", h)
                dve.wait_ge(*filled(use))
                steps.done(V.tensor_copy(ml_f[:, 0, :], ps(use)[:, 0:SEQ]))
                V.tensor_tensor(ml_f[:, 1, :], ps(use)[:, SEQ:2 * SEQ], ml_f[:, 0, :], ALU.subtract).then_inc(
                    drain_sem(use), 1)
                dve.wait_ge(*drained(use))
                steps.done(V.tensor_tensor_scan(ml_r[:, h, :], ml_f[:, 1, :], ml_f[:, 1, :], -3e38, ALU.max,
                                                ALU.max))
                V.scalar_tensor_tensor(ml_r[:, h, :], ml_r[:, h, :], -1.0, ml_f[:, 0, :], ALU.mult,
                                       ALU.min).then_inc(mr_ready, 1)
                dve.wait_ge(mr_ready, h + 1)

            def conv_chunk(k):
                src = mq_in[:, k, :] if k < 4 else mk_in[:, k - 4, :]
                dst = mqk[:, k, :]

                def tap(j):
                    return vec[:, V_CONV + 8 * j + k:V_CONV + 8 * j + k + 1]

                n = steps.mark(V.tensor_scalar(dst, src, tap(TAPS - 1), None, ALU.mult))
                for d in range(1, TAPS):
                    steps.wait(n)
                    ins = V.scalar_tensor_tensor(dst[:, d:], src[:, 0:SEQ - d], tap(TAPS - 1 - d), dst[:, d:],
                                                 ALU.mult, ALU.add)
                    if d < TAPS - 1:
                        n = steps.mark(ins)
                    else:
                        ins.then_inc(conv_ready, 1)

            def stick_breaking(h):
                if h < SB_H:
                    use = ("sb_z", h)
                    z = ps(use)[:, 0:384]
                    dve.wait_ge(sbl_ready, h + 1)
                    V.scalar_tensor_tensor(sb_sp[:, h % 3, :], z, 0.0, sb_l[:, h % 2, :], ALU.max,
                                           ALU.add).then_inc(sbsp_ready, 1)
                    V.scalar_tensor_tensor(sb_w[:, h % 4, :], z, 0.0, sb_l[:, h % 2, :], ALU.min,
                                           ALU.subtract).then_inc(drain_sem(use), 1)
                if 1 <= h <= SB_H:
                    use = ("sb_lat", h - 1)
                    buf = sb_w[:, (h - 1) % 4, :]
                    dve.wait_ge(*drained(("sb_z", h - 1)))
                    dve.wait_ge(*filled(use))
                    V.tensor_tensor(buf, buf, ps(use)[:, 0:384], ALU.subtract).then_inc(drain_sem(use), 1)
                if h == ROWS_TURNED_AT:
                    dve.wait_ge(*filled("mr"))
                    V.tensor_tensor(m_em, ps("mr")[:, 0:T * ML_H].rearrange("p (t h) -> p t h", t=T), m_rn_f,
                                    ALU.subtract).then_inc(drain_sem("mr"), 1)
                if h >= 3 and h % 2 == 1:
                    mix_low_part((h - 3) // 2, ("sb_o", (h - 3) // 2), FOX_H // 2 + (h - 3) // 2 + 1)

            for n in range(len(ODD_JOBS)):
                if n not in ACT_ODD_JOBS:
                    drain_job("odd", ODD_JOBS, n)
                low_parts(N_ODD + n + SPLITS)
                if n == ODD_SUMS_AFTER:
                    gate_columns()
                for h in ODD_ROWS_AFTER.get(n, ()):
                    gate_rows(h)
                if 0 <= n - SB_AFTER < SB_H + 2:
                    stick_breaking(n - SB_AFTER)
                if 0 <= n - CONV_AFTER < 4:
                    dve.wait_ge(*drained(("odd", n - 2)))
                    conv_chunk(2 * (n - CONV_AFTER))
                    conv_chunk(2 * (n - CONV_AFTER) + 1)

            dve.wait_ge(mem_ready, 1)

            def ml_exponent(h):
                V.tensor_scalar(ml_e[:, h % 3, 0:SEQ], ml_r[:, h, :], m_an[:, 0, h:h + 1], 0.0, ALU.add, ALU.min)
                V.tensor_scalar(ml_e[:, h % 3, SEQ:384], ml_r[:, h, P:SEQ], m_an[:, 1, h:h + 1], 0.0, ALU.add,
                                ALU.min).then_inc(me_in, 1)

            ml_exponent(0)
            for h in range(ML_H + 1):
                if h < ML_H:
                    if h + 1 < ML_H:
                        ml_exponent(h + 1)
                    use = ("ml_s", h)
                    dve.wait_ge(me_ready, h + 1)
                    dve.wait_ge(*filled(use))
                    V.scalar_tensor_tensor(ml_w[:, h % 4, :], ml_e[:, h % 3, :], P ** -0.5, ps(use)[:, 0:384],
                                           ALU.mult, ALU.mult).then_inc(drain_sem(use), 1)
                if h:
                    g = h - 1
                    use = ("ml_n", g)
                    o = ps(use)[:, 0:2 * 129].rearrange("p (t d) -> p t d", t=T)
                    dve.wait_ge(*filled(use))
                    steps.done(V.tensor_copy(m_den[:, g, :], o[:, :, 128]))
                    steps.done(V.scalar_tensor_tensor(m_den[:, g, :], m_den[:, g, :], -1.0, m_den[:, g, :],
                                                      ALU.mult, ALU.max))
                    steps.done(V.tensor_tensor(m_den[:, g, :], m_den[:, g, :], m_em[:, :, g], ALU.max))
                    steps.done(V.reciprocal(m_rden[:, g, :], m_den[:, g, :]))
                    for t in range(T):
                        last = V.tensor_scalar(ml_h[:, t, g * P:(g + 1) * P], o[:, t, 0:P], m_rden[:, g, t:t + 1],
                                               None, ALU.mult)
                    last.then_inc(drain_sem(use), 1)
            dve.wait_ge(mh_sq, T * ML_H)
            steps.done(V.tensor_scalar(m_inv, m_ssq, 1.0 / P, EPS, ALU.mult, ALU.add))
            V.reciprocal(m_inv, m_inv).then_inc(mh_inv, 1)
            dve.wait_ge(mh_rstd, 1)
            for n in (12, 13):
                dve.wait_ge(*drained(("odd", n)))
            for t in range(T):
                heads = ml_h[:, t, :].rearrange("p (h d) -> p h d", h=ML_H)
                steps.done(V.tensor_tensor(heads, heads, m_rstd[:, :, t:t + 1].to_broadcast([P, ML_H, P]),
                                           ALU.mult))
                V.tensor_tensor(ml_h[:, t, :], ml_h[:, t, :], ml_o[:, t, :], ALU.mult).then_inc(md_ready, 1)
            low_parts(N_WO1 + SPLITS)
            for h in range(ML_H):
                mix_low_part(4 + h, ("ml_t", h), FOX_H // 2 + SB_H // 2 + h + 1, vec[:, V_HEAD + h:V_HEAD + h + 1])
            add_to_x([("wout", 1, n) for n in range(4)])

            def one_hot(item):
                for t in range(T):
                    pos = pos_i[:, bass.ds(item, 1), t]
                    V.tensor_scalar(sel[:, t, :], cst[:, C_IOTA:C_IOTA + P], pos, None, ALU.is_equal)
                    last = V.tensor_scalar(sel_g[:, t, :], cst[:, C_IOTA:C_IOTA + P], pos,
                                           gate_i[:, bass.ds(item, 1), t], ALU.is_equal, ALU.mult)
                last.then_inc(sel_ready, 1)

            norm_scale(3)
            norm_banks(3)
            copy_rows("router", NE)
            dve.wait_ge(*filled("router"))
            V.tensor_copy(r_log, ps("router")[:, 0:T * NE].rearrange("p (t e) -> p t e", t=T)).then_inc(
                drain_sem("router"), 1)
            dve.wait_ge(*drained("router"))
            steps.done(V.tensor_reduce(r_max, r_log, AX, ALU.max))
            V.tensor_tensor(r_e, r_log, r_max.to_broadcast([P, T, NE]), ALU.subtract).then_inc(r_in, 1)
            for t in range(T):
                other = r_log[:, t, None, :].to_broadcast([P, NE, NE])
                own = r_log[:, t, :, None].to_broadcast([P, NE, NE])
                cmp_t, eq_t = r_cmp[:, t * NE:(t + 1) * NE, :], r_eq[:, t * NE:(t + 1) * NE, :]
                V.tensor_tensor(cmp_t, other, own, ALU.is_gt)
                steps.done(V.tensor_tensor(eq_t, other, own, ALU.is_equal))
                steps.done(V.tensor_tensor(eq_t, eq_t, cst[:, C_TIE:C_TIE + NE * NE].rearrange(
                    "p (a b) -> p a b", a=NE), ALU.mult))
                steps.done(V.tensor_tensor(cmp_t, cmp_t, eq_t, ALU.add))
                steps.done(V.tensor_reduce(r_rank[:, t, :], cmp_t, AX, ALU.add))
            V.tensor_scalar(r_sel, r_rank, 1.5, None, ALU.is_lt).then_inc(rsel_ready, 1)
            dve.wait_ge(rsel_ready, 1)
            dve.wait_ge(r_exp, 1)
            steps.done(V.tensor_tensor(r_e, r_e, r_sel, ALU.mult))
            steps.done(V.tensor_reduce(r_sum, r_e, AX, ALU.add))
            steps.done(V.reciprocal(r_sum, r_sum))
            steps.done(V.tensor_tensor(r_gate, r_e, r_sum.to_broadcast([P, T, NE]), ALU.mult))
            dve.wait_ge(*filled("rank"))
            V.tensor_copy(r_cnt[:, 0, :], ps("rank")[:, 2 * NE:3 * NE])
            V.tensor_tensor(r_pos, ps("rank")[:, 0:T * NE].rearrange("p (t e) -> p t e", t=T), r_sel,
                            ALU.mult).then_inc(drain_sem("rank"), 1)
            dve.wait_ge(*drained("rank"))
            steps.done(V.tensor_scalar(r_pos, r_pos, -1.0, None, ALU.add))
            for t in range(T):
                V.tensor_copy(pos_i[:, 0:NE, t], r_pos[:, t, :])
                steps.done(V.tensor_copy(gate_i[:, 0:NE, t], r_gate[:, t, :]))
            one_hot(0)
            make_low(dve, N_MOE)
            steps.done(V.tensor_scalar(r_over, r_cnt[:, 0, :], float(P) + 0.5, None, ALU.is_gt))
            steps.done(V.tensor_tensor_scan(r_oc, ones[:, 0:NE], r_over, 0.0, ALU.mult, ALU.add))
            steps.done(V.tensor_scalar(r_eidf[:, 0:1], r_oc[:, NE - 1:NE], float(NE), None, ALU.add))
            steps.done(V.tensor_tensor(r_oc, r_oc, r_over, ALU.subtract))
            steps.done(V.tensor_scalar(r_pos, r_pos, -float(P), None, ALU.add))
            steps.done(V.tensor_tensor(r_pick, r_oc[:, None, :].to_broadcast([P, NEXTRA, NE]),
                                       cst[:, C_SLOTNO:C_SLOTNO + NEXTRA, None].to_broadcast([P, NEXTRA, NE]),
                                       ALU.is_equal))
            steps.done(V.tensor_tensor(r_pick, r_pick, r_over[:, None, :].to_broadcast([P, NEXTRA, NE]), ALU.mult))
            prod = r_prod.rearrange("p (j t) e -> p j t e", t=T)
            for table, values_of in ((pos_i, r_pos), (gate_i, r_gate)):
                for t in range(T):
                    last = V.tensor_tensor(prod[:, :, t, :], r_pick,
                                           values_of[:, t, None, :].to_broadcast([P, NEXTRA, NE]), ALU.mult)
                steps.done(last)
                steps.done(V.tensor_reduce(table[:, NE:NE + NEXTRA, :], prod, AX, ALU.add))
            steps.done(V.tensor_tensor(r_pick, r_pick, cst[:, None, C_EID:C_EID + NE].to_broadcast([P, NEXTRA, NE]),
                                       ALU.mult))
            steps.done(V.tensor_reduce(r_eidf[:, 1:1 + NEXTRA], r_pick, AX, ALU.add))
            V.tensor_copy(route_i[0:1, 0:1 + NEXTRA], r_eidf[0:1, 0:1 + NEXTRA]).then_inc(route_ready, 1)

            def rows_low(name, item, number):
                for half in range(2):
                    use = (name, half)
                    dve.wait_ge(xg_high, number + half + 1)
                    V.tensor_tensor(xg_l[:, 4 * half:4 * half + 4, :], ps(use).rearrange("p (k c) -> p k c", k=4),
                                    xg_h[:, 4 * half:4 * half + 4, :].bitcast(F32), ALU.subtract).then_inc(
                                        drain_sem(use), 1)

            def expert_item(item):
                for n in range(1, SPLITS):
                    make_low(dve, N_MOE + n, item)

                def act_low(c):
                    at = (c % 2) * 4
                    dve.wait_ge(mact_high, NCH * item + c + 1)
                    V.tensor_tensor(m_act_l[:, at:at + 4, :], ps(("mt", c)).rearrange("p (j c) -> p j c", j=4),
                                    m_act_h[:, at:at + 4, :].bitcast(F32), ALU.subtract).then_inc(
                                        drain_sem(("mt", c)), 1)

                for j in range(SPLITS, FFN_PIECES):
                    make_low(dve, N_MOE + j, item)
                    kind, c, h = EXPERT_ORDER[j - SPLITS]
                    if (kind, h) == ("g", 1) and c:
                        act_low(c - 1)
                    if (kind, c, h) == ("u", 2, 1):
                        dve.wait_ge(*filled("sgt", item))
                        one_hot(item + 1)
                    if (kind, h) == ("u", 1):
                        dve.wait_ge(*drained(("mg", c), item))
                        dve.wait_ge(*filled(("mu", c), item))
                        V.tensor_tensor(m_act[:, c % 2, :], m_silu[:, c % 2, :], ps(("mu", c)), ALU.mult).then_inc(
                            drain_sem(("mu", c)), 1)
                act_low(NCH - 1)
                rows_low("gather", item, 2 * item + 2)
                make_low(dve, N_MOE + FFN_PIECES, item)
                dve.wait_ge(*filled(("my", 1), item))
                V.tensor_copy(y_e[:, 1, :], ps(("my", 1))).then_inc(drain_sem(("my", 1)), 1)
                for n in range(4):
                    t, nh = n // 2, n % 2
                    use = ("mc", n)
                    quarter = x[:, t, nh * 512:(nh + 1) * 512]
                    dve.wait_ge(*filled(use, item))
                    V.tensor_tensor(quarter, quarter, ps(use), ALU.add).then_inc(drain_sem(use), 1)

            rows_low("gather0", 0, 0)
            with dve.Fori(0, NE) as item:
                expert_item(item)
            n_items = dve.value_load(route_i[0:1, 0:1], min_val=NE, max_val=NITEM)
            with dve.Fori(NE, NITEM) as item:
                with dve.If(n_items > item):
                    expert_item(item)
            V.memset(r_max, 0.0).then_inc(experts_done, 1)

            norm_scale(4)
            for t in range(T):
                V.scalar_tensor_tensor(hn[:, t, :], x[:, t, :], rstd[:, 4, t:t + 1], g_row[:, :], ALU.mult,
                                       ALU.mult).then_inc(out_ready, 1)


_WEIGHTS = ["norm_mix_g", "norm_ffn_g", "norm_final_g", "ev_w_in", "ev_b_forget", "ev_pool_w", "ev_pool_scale",
            "ev_w_out", "ffn_w_gate", "ffn_w_up", "ffn_w_down", "od_w_in", "od_b_igate", "od_b_fgate", "od_conv_w",
            "od_head_norm_g", "od_w_out", "moe_w_router", "moe_w_gate", "moe_w_up", "moe_w_down"]


def kernel(**inputs):
    import concourse.bacc as _bacc
    from concourse.bass_utils import run_bass_kernel_spmd as _run

    nc = _bacc.Bacc("TRN2", target_bir_lowering=False, num_devices=1)
    arrays, aps = {}, {}
    for name in ["x"] + _WEIGHTS:
        a = np.ascontiguousarray(inputs[name])
        arrays[f"in_{name}"] = a
        aps[name] = nc.dram_tensor(f"in_{name}", a.shape, mybir.dt.from_np(a.dtype), kind="ExternalInput").ap()
    arrays["in_constants"] = constants()
    cst_d = nc.dram_tensor("in_constants", (P, C_ALL), F32, kind="ExternalInput").ap()
    out_d = nc.dram_tensor("out_trunk", (1, SEQ, DM), F32, kind="ExternalOutput").ap()
    build_trunk(nc, aps["x"], aps, cst_d, out_d)
    r = _run(nc, [arrays], core_ids=[0])
    return r.results[0]["out_trunk"]
```
